# Optimizing a Trainium2 kernel written in Bass

```python
import math
import jax, jax.numpy as jnp
from jax import lax
import numpy as np

D_MODEL = 1024
BATCH = 1
SEQ = 256
DEPTH = 1

N_META = 16
NORM_EPS = 1e-6

DA_HEADS = 8
DA_HEAD_DIM = 64
DA_V_DIM = 2 * DA_HEAD_DIM
DA_QK = DA_HEADS * 2 * DA_HEAD_DIM
DA_V = DA_HEADS * DA_V_DIM
Q_BLOCK = 128
ALIBI_SLOPES = tuple(2.0 ** (-8.0 * (h + 1) / DA_HEADS) for h in range(DA_HEADS))

DN_HEADS = 8
DN_HEAD_DIM = 128
DN_QK = DN_HEADS * DN_HEAD_DIM
DN_V = DN_HEADS * DN_HEAD_DIM
DN_CONV = 4
DN_CHUNK = 64

N_GROUPS = 4
EXPERTS_PER_GROUP = 8
N_EXPERTS = N_GROUPS * EXPERTS_PER_GROUP
D_EXPERT = 256
TOP_K = 2

IN_SIZES = (DA_QK, DA_QK, DA_V, DN_QK, DN_QK, DN_V, DN_V, DN_HEADS, DN_HEADS, D_MODEL, D_MODEL)
IN_OFFSETS = tuple(int(s) for s in np.cumsum(IN_SIZES)[:-1])
W_IN_COLS = int(sum(IN_SIZES))

kernel_name = "hybrid_diffattn_gdn_hmoe_block"

F32 = jnp.float32

def rms_norm(x, w):
    xf = x.astype(F32)
    y = xf * lax.rsqrt(jnp.mean(xf * xf, axis=-1, keepdims=True) + NORM_EPS)
    return (y * w.astype(F32)).astype(x.dtype)

def l2_normalize(x):
    return x * lax.rsqrt(jnp.sum(x * x, axis=-1, keepdims=True) + 1e-6)

def differential_attention(q, k, v, lq1, lk1, lq2, lk2, subln_w, lambda_init):
    B, L, _ = q.shape
    n_blk = -(-L // Q_BLOCK)
    Lp = n_blk * Q_BLOCK
    pad = ((0, 0), (0, Lp - L), (0, 0))
    qb = jnp.pad(q, pad).reshape(B, n_blk, Q_BLOCK, DA_HEADS, 2, DA_HEAD_DIM)
    qb = jnp.moveaxis(qb, 1, 0)
    kk = jnp.pad(k, pad).reshape(B, Lp, DA_HEADS, 2, DA_HEAD_DIM)
    vv = jnp.pad(v, pad).reshape(B, Lp, DA_HEADS, DA_V_DIM)
    lam = (jnp.exp(jnp.sum(lq1.astype(F32) * lk1.astype(F32)))
           - jnp.exp(jnp.sum(lq2.astype(F32) * lk2.astype(F32))) + lambda_init)
    slopes = jnp.asarray(ALIBI_SLOPES, dtype=F32)[:, None, None]
    k_pos = jnp.arange(Lp, dtype=jnp.int32)
    scale = DA_HEAD_DIM ** -0.5

    def attend_block(args):
        q_blk, start = args
        q_pos = start + jnp.arange(Q_BLOCK, dtype=jnp.int32)
        dist = (q_pos[:, None] - k_pos[None, :]).astype(F32)
        bias = jnp.where(dist >= 0, -slopes * dist, -jnp.inf)
        s = jnp.einsum('bqhmd,bkhmd->bhmqk', q_blk, kk, preferred_element_type=F32) * scale
        p = jax.nn.softmax(s + bias[None, :, None], axis=-1)
        w = p[:, :, 0] - lam * p[:, :, 1]
        return jnp.einsum('bhqk,bkhe->bqhe', w.astype(vv.dtype), vv, preferred_element_type=F32)

    starts = jnp.arange(n_blk, dtype=jnp.int32) * Q_BLOCK
    o = lax.map(attend_block, (qb, starts))
    o = jnp.moveaxis(o, 0, 1).reshape(B, Lp, DA_HEADS, DA_V_DIM)[:, :L]
    o = rms_norm(o, subln_w) * (1.0 - lambda_init)
    return o.reshape(B, L, DA_V).astype(v.dtype)

def chunk_gated_delta_rule(q, k, v, beta, g):
    B, Lc, H, _ = q.shape
    dv = v.shape[-1]
    C = DN_CHUNK
    N = Lc // C

    def to_chunks(t):
        return jnp.moveaxis(t.reshape((B, N, C, H) + t.shape[3:]), 3, 1)

    q, k, v, beta, g = (to_chunks(t) for t in (q, k, v, beta, g))
    gc = jnp.cumsum(g, axis=-1)
    incl = jnp.tril(jnp.ones((C, C), dtype=bool))
    strict = jnp.tril(jnp.ones((C, C), dtype=bool), -1)
    diff = gc[..., :, None] - gc[..., None, :]
    decay = jnp.where(incl, jnp.exp(jnp.where(incl, diff, 0.0)), 0.0)
    kb = k * beta[..., None]
    A = jnp.where(strict, jnp.einsum('bhnid,bhnjd->bhnij', kb, k) * decay, 0.0)
    eye = jnp.eye(C, dtype=F32)
    T = lax.linalg.triangular_solve(A + eye, jnp.broadcast_to(eye, A.shape),
                                    left_side=True, lower=True, unit_diagonal=True)
    u = jnp.einsum('bhnij,bhnje->bhnie', T, v * beta[..., None])
    w = jnp.einsum('bhnij,bhnjd->bhnid', T, kb * jnp.exp(gc)[..., None])
    qk = jnp.einsum('bhnid,bhnjd->bhnij', q, k) * decay
    q_dec = q * jnp.exp(gc)[..., None]
    k_dec = k * jnp.exp(gc[..., -1:] - gc)[..., None]
    g_tot = jnp.exp(gc[..., -1])
    xs = tuple(jnp.moveaxis(t, 2, 0) for t in (u, w, q_dec, k_dec, qk, g_tot))

    def step(S, inp):
        u_n, w_n, qd_n, kd_n, qk_n, gt_n = inp
        v_new = u_n - jnp.einsum('bhcd,bhde->bhce', w_n, S)
        o_n = jnp.einsum('bhcd,bhde->bhce', qd_n, S) + jnp.einsum('bhij,bhje->bhie', qk_n, v_new)
        S = S * gt_n[..., None, None] + jnp.einsum('bhcd,bhce->bhde', kd_n, v_new)
        return S, o_n

    S0 = jnp.zeros((B, H, q.shape[-1], dv), dtype=F32)
    _, o = lax.scan(step, S0, xs)
    o = jnp.moveaxis(o, 0, 2)
    return jnp.moveaxis(o, 1, 3).reshape(B, Lc, H, dv)

def gated_deltanet(q, k, v, gate, beta_logit, a_logit, conv_w, A_log, dt_bias, norm_w):
    B, L, _ = q.shape
    qkv = jnp.concatenate([q, k, v], axis=-1)
    ch = qkv.shape[-1]
    qkv = lax.conv_general_dilated(qkv, conv_w[:, None, :].astype(qkv.dtype), (1,), [(DN_CONV - 1, 0)],
                                   dimension_numbers=('NWC', 'WIO', 'NWC'), feature_group_count=ch)
    qkv = jax.nn.silu(qkv.astype(F32))
    qc, kc, vc = jnp.split(qkv, [DN_QK, 2 * DN_QK], axis=-1)
    qc = l2_normalize(qc.reshape(B, L, DN_HEADS, DN_HEAD_DIM)) * (DN_HEAD_DIM ** -0.5)
    kc = l2_normalize(kc.reshape(B, L, DN_HEADS, DN_HEAD_DIM))
    vc = vc.reshape(B, L, DN_HEADS, DN_HEAD_DIM)
    beta = jax.nn.sigmoid(beta_logit.astype(F32))
    g = -jnp.exp(A_log.astype(F32)) * jax.nn.softplus(a_logit.astype(F32) + dt_bias.astype(F32))
    front = (-N_META) % DN_CHUNK
    total = front + L
    back = (-total) % DN_CHUNK

    def pad(t):
        return jnp.pad(t, ((0, 0), (front, back)) + ((0, 0),) * (t.ndim - 2))

    o = chunk_gated_delta_rule(pad(qc), pad(kc), pad(vc), pad(beta), pad(g))[:, front:front + L]
    o = rms_norm(o, norm_w) * jax.nn.silu(gate.astype(F32).reshape(B, L, DN_HEADS, DN_HEAD_DIM))
    return o.reshape(B, L, DN_V).astype(gate.dtype)

def hierarchical_moe(x, wg_r, bg_r, we_r, be_r, w_gate, w_up, w_down):
    B, L, D = x.shape
    xt = x.reshape(B * L, D)
    g_prob = jax.nn.softmax((xt @ wg_r).astype(F32) + bg_r.astype(F32), axis=-1)
    g_w, g_i = lax.top_k(g_prob, 1)
    e_logit = ((xt @ we_r).astype(F32) + be_r.astype(F32)).reshape(-1, N_GROUPS, EXPERTS_PER_GROUP)
    e_logit = jnp.einsum('tg,tge->te', jax.nn.one_hot(g_i[:, 0], N_GROUPS, dtype=F32), e_logit)
    e_prob = jax.nn.softmax(e_logit, axis=-1)
    e_w, e_i = lax.top_k(e_prob, TOP_K)
    e_w = e_w / jnp.sum(e_w, axis=-1, keepdims=True)
    weights = g_w * e_w
    expert_ids = g_i * EXPERTS_PER_GROUP + e_i
    combine = jnp.sum(jax.nn.one_hot(expert_ids, N_EXPERTS, dtype=F32) * weights[..., None], axis=1)
    y = jnp.zeros((B * L, D), dtype=F32)
    for e in range(N_EXPERTS):
        h = jax.nn.silu(xt @ w_gate[e]) * (xt @ w_up[e])
        y = y + combine[:, e:e + 1] * (h @ w_down[e]).astype(F32)
    return y.reshape(B, L, D).astype(x.dtype)

def setup_inputs(seed: int = 0) -> dict:
    key = jax.random.key(seed)
    ks = jax.random.split(key, 26)
    nrm = jax.random.normal
    Ld = DEPTH
    dt = jnp.exp(jax.random.uniform(ks[11], (Ld, DN_HEADS)) * (math.log(0.1) - math.log(0.001)) + math.log(0.001))
    return {
        "x": nrm(ks[0], (BATCH, SEQ, D_MODEL), F32),
        "meta_tokens": nrm(ks[1], (N_META, D_MODEL), F32),
        "norm1_w": 1.0 + 0.02 * nrm(ks[2], (Ld, D_MODEL), F32),
        "w_in": nrm(ks[3], (Ld, D_MODEL, W_IN_COLS), F32) * D_MODEL ** -0.5,
        "lambda_q1": 0.1 * nrm(ks[4], (Ld, DA_HEAD_DIM), F32),
        "lambda_k1": 0.1 * nrm(ks[5], (Ld, DA_HEAD_DIM), F32),
        "lambda_q2": 0.1 * nrm(ks[6], (Ld, DA_HEAD_DIM), F32),
        "lambda_k2": 0.1 * nrm(ks[7], (Ld, DA_HEAD_DIM), F32),
        "da_subln_w": 1.0 + 0.02 * nrm(ks[8], (Ld, DA_V_DIM), F32),
        "dn_conv_w": nrm(ks[9], (Ld, DN_CONV, 2 * DN_QK + DN_V), F32) * DN_CONV ** -0.5,
        "dn_A_log": jnp.log(jax.random.uniform(ks[10], (Ld, DN_HEADS), F32, 1.0, 16.0)),
        "dn_dt_bias": dt + jnp.log(-jnp.expm1(-dt)),
        "dn_norm_w": 1.0 + 0.02 * nrm(ks[12], (Ld, DN_HEAD_DIM), F32),
        "w_branch_attn": nrm(ks[13], (Ld, DA_V, D_MODEL), F32) * DA_V ** -0.5,
        "w_branch_dn": nrm(ks[14], (Ld, DN_V, D_MODEL), F32) * DN_V ** -0.5,
        "w_out": nrm(ks[15], (Ld, D_MODEL, D_MODEL), F32) * D_MODEL ** -0.5,
        "norm2_w": 1.0 + 0.02 * nrm(ks[16], (Ld, D_MODEL), F32),
        "router_group_w": nrm(ks[17], (Ld, D_MODEL, N_GROUPS), F32) * D_MODEL ** -0.5,
        "router_group_b": 0.01 * nrm(ks[18], (Ld, N_GROUPS), F32),
        "router_expert_w": nrm(ks[19], (Ld, D_MODEL, N_EXPERTS), F32) * D_MODEL ** -0.5,
        "router_expert_b": 0.01 * nrm(ks[20], (Ld, N_EXPERTS), F32),
        "expert_w_gate": nrm(ks[21], (Ld, N_EXPERTS, D_MODEL, D_EXPERT), F32) * D_MODEL ** -0.5,
        "expert_w_up": nrm(ks[22], (Ld, N_EXPERTS, D_MODEL, D_EXPERT), F32) * D_MODEL ** -0.5,
        "expert_w_down": nrm(ks[23], (Ld, N_EXPERTS, D_EXPERT, D_MODEL), F32) * D_EXPERT ** -0.5,
        "final_norm_w": 1.0 + 0.02 * nrm(ks[24], (D_MODEL,), F32),
    }

def reference(x, meta_tokens, norm1_w, w_in, lambda_q1, lambda_k1, lambda_q2, lambda_k2, da_subln_w,
              dn_conv_w, dn_A_log, dn_dt_bias, dn_norm_w, w_branch_attn, w_branch_dn, w_out, norm2_w,
              router_group_w, router_group_b, router_expert_w, router_expert_b,
              expert_w_gate, expert_w_up, expert_w_down, final_norm_w):
    B = x.shape[0]
    meta = jnp.broadcast_to(meta_tokens[None].astype(x.dtype), (B, N_META, D_MODEL))
    h = jnp.concatenate([meta, x], axis=1)
    for layer in range(DEPTH):
        lambda_init = 0.8 - 0.6 * math.exp(-0.3 * layer)
        u = rms_norm(h, norm1_w[layer])
        proj = jnp.einsum('bld,dn->bln', u, w_in[layer])
        (a_q, a_k, a_v, d_q, d_k, d_v, d_gate, d_beta, d_a, gate_a, gate_d) = jnp.split(proj, IN_OFFSETS, axis=-1)
        y_a = differential_attention(a_q, a_k, a_v, lambda_q1[layer], lambda_k1[layer], lambda_q2[layer],
                                     lambda_k2[layer], da_subln_w[layer], lambda_init)
        y_d = gated_deltanet(d_q, d_k, d_v, d_gate, d_beta, d_a, dn_conv_w[layer], dn_A_log[layer],
                             dn_dt_bias[layer], dn_norm_w[layer])
        y_a = jnp.einsum('ble,ed->bld', y_a, w_branch_attn[layer])
        y_d = jnp.einsum('ble,ed->bld', y_d, w_branch_dn[layer])
        mixed = jax.nn.sigmoid(gate_a) * y_a + jax.nn.sigmoid(gate_d) * y_d
        h = h + jnp.einsum('bld,de->ble', mixed, w_out[layer])
        h = h + hierarchical_moe(rms_norm(h, norm2_w[layer]), router_group_w[layer], router_group_b[layer],
                                 router_expert_w[layer], router_expert_b[layer], expert_w_gate[layer],
                                 expert_w_up[layer], expert_w_down[layer])
    h = rms_norm(h, final_norm_w)
    return h[:, N_META:]


_drawn_inputs = setup_inputs


def setup_inputs(seed=0):
    import zlib

    import numpy as np

    out = dict(_drawn_inputs(seed))
    spreads = {}
    factors = {'router_group_b': 2.936,
     'router_expert_b': 4.521,
     'final_norm_w': 8.165,
     'da_subln_w': 3.626,
     'dn_norm_w': 5.31,
     'norm2_w': 3.045}
    for name, (base, spread) in spreads.items():
        noise = np.random.default_rng([zlib.crc32(name.encode()), seed]).standard_normal(out[name].shape)
        drawn = base * np.exp(spread * noise) if base else spread * noise
        out[name] = __import__('jax').numpy.asarray(drawn.astype(out[name].dtype))
    for name, factor in factors.items():
        out[name] = (out[name] * factor).astype(out[name].dtype)
    return out
```

```python
from contextlib import ExitStack
import math

import concourse.bass as bass
from concourse import mybir

P = 128
D = 1024
NC = D // P
META = 16
SEQ = 256
L = META + SEQ
TT = SEQ // P
H = 8
SCALE = 64 ** -0.5
LAMBDA_INIT = 0.8 - 0.6 * math.exp(-0.3 * 0)
EPS = 1e-6
NEG = -1e30
CONV = 4
N_GROUPS, PER_GROUP, N_EXPERTS, D_EXPERT = 4, 8, 32, 256
EPB = 4
N_BATCH = N_EXPERTS // EPB
CAP = P // EPB
UNIT = 2048
SLOTS = 12

F32 = mybir.dt.float32
I32 = mybir.dt.int32
ALU = mybir.AluOpType
ACT = mybir.ActivationFunctionType
AX = mybir.AxisListType.X

W_COL = dict(aq=0, ak=1024, av=2048, dq=3072, dk=4096, dv=5120, gate=6144, ga=7184, gb=8208)
BA_COL = 7168
KINDS = ["ak", "av", "aq", "dq", "dk", "dv", "gate", "ga", "ya", "gb", "yd", "out"]
TILES = [(kind, j) for kind in KINDS for j in range(8)]
FIRST = {kind: 8 * i for i, kind in enumerate(KINDS)}
N_UNITS = len(TILES) // 2
V_NORM1, V_SUBLN, V_DNW, V_CONV = 0, 8, 9, 10
N_VEC = V_CONV + CONV * 3 * H


def hybrid_block(nc, x, meta_tokens, norm1_w, w_in, lambda_q1, lambda_k1, lambda_q2, lambda_k2, da_subln_w,
                 dn_conv_w, dn_A_log, dn_dt_bias, dn_norm_w, w_branch_attn, w_branch_dn, w_out, norm2_w,
                 router_group_w, router_group_b, router_expert_w, router_expert_b, expert_w_gate,
                 expert_w_up, expert_w_down, final_norm_w, out, dbg=None):
    with ExitStack() as ctx:
        def sem(name):
            return ctx.enter_context(nc.semaphore(name))

        FLOATS = 53100
        arena = ctx.enter_context(nc.sbuf_tensor("arena", [P, FLOATS], F32))
        bank = [ctx.enter_context(nc.psum_tensor(f"bank{i}", [P, 512], F32)) for i in range(8)]
        top = [0]

        def at(start, *shape):
            n = math.prod(shape)
            ap = arena[:, start:start + n]
            if len(shape) == 2:
                return ap.rearrange("p (a b) -> p a b", b=shape[1])
            if len(shape) == 3:
                return ap.rearrange("p (a b c) -> p a b c", b=shape[1], c=shape[2])
            return ap

        def new(*shape):
            start = top[0]
            top[0] += math.prod(shape)
            assert top[0] <= FLOATS, top[0]
            return at(start, *shape)

        ring = new(SLOTS, UNIT)
        ident, ones, tri, strict, causal_add = (new(P) for _ in range(5))
        block16, off32, off64, off128 = (new(P) for _ in range(4))
        tri16, causal_add16, spread16 = (new(P) for _ in range(3))
        own_head = new(H)
        slot_no = new(CAP)
        const = new(4)
        c_eps, c_ln08, c_lnq, c_one = (const[:, i:i + 1] for i in range(4))
        vec = new(P)
        lam_in, lam = new(4, 64), new(8)
        ssq, rstd = new(4), new(4)
        NCOL = 2 * H + 1
        blog, alog, dtb, eA, beta, g, sp, tmp17 = (new(NCOL) for _ in range(8))
        gc2 = new(2, NCOL)
        egc, begc, kdec, egt, ngc, nbeta = (new(NCOL) for _ in range(6))
        ba_meta = new(16)
        mx, rsum, rinv, nmax = (new(2, 2) for _ in range(4))
        uT_start = top[0]
        uT = new(NC, L)
        dqk_start = top[0]
        dqT, dkT = new(H, L), new(H, L)
        dv_start = top[0]
        dv_tok, dvT_meta, dkT_meta = new(TT, H, P), new(H, META), new(H, META)
        yaT_start = top[0]
        yaT = new(H, SEQ)
        zone = top[0]

        aqT, akT, v_tok, v_meta = new(H, SEQ), new(H, L), new(TT, H, P), new(H, P)
        qz = new(2, 2, P)
        dist, bias = new(TT, L), new(2, L)
        prob = new(2, 2, L)
        wT = new(2, 3, P)
        vtmp = new(2, L)
        osq, ors = new(SEQ), new(SEQ)
        cbuf = new(2, L + CONV - 1)
        NACC = 5
        acc = new(NACC, L)
        sg, csq, crs = new(2, L), new(2, L), new(L)
        xin = at(dqk_start, 3, D)
        vec_rows = at(dqk_start + 3 * D, P)
        w_ba = at(dv_start, NC, 16)

        top[0] = zone
        NB = 8
        work = [[new(4, P) for _ in range(NB)] for _ in range(2)]
        gateT, gaT, S = new(H, SEQ), new(H, SEQ), new(H, P)
        gx, gs = new(2, SEQ), new(2, SEQ)
        gbT = at(yaT_start, H, SEQ)
        mixT = gaT
        um = at(zone + 8 * 512, H, P)

        h_tok = at(uT_start, TT, D)
        u2, u2T = at(dqk_start, TT, D), at(dqk_start + TT * D, NC, SEQ)
        norm2_b, fnorm_b = at(dv_start, D), at(dv_start + D, D)
        top[0] = zone
        r_w = new(NC, 36)
        r_b = new(36)
        junk = new(D)
        lg, me, me2, eq, e1, e2 = new(TT, 36), new(TT, 32), new(TT, 32), new(TT, 32), new(TT, 32), new(TT, 32)
        cum, comb, asg, rank, ovf = new(TT, 32), new(TT, 32), new(TT, 32), new(TT, 32), new(TT, 32)
        gsel, gd, pen = new(TT, 4), new(TT, 4), new(TT, 4)
        sc = new(12, TT)
        pick, pickw = new(TT, EPB, CAP), new(TT, EPB, CAP)
        pickT = new(TT, P)
        xg = new(NC, P)
        sil, hid, hidT = new(D_EXPERT), new(D_EXPERT), new(2, P)
        dsb = new(D)
        ovcnt = new(2)
        ovi = new(1).bitcast(I32)
        ftmp = new(SEQ)
        fhT = new(2, SEQ)
        result = new(TT, D)
        assert top[0] <= zone + 8192 + 2048, top[0] - zone

        x_in, vec_in, wba_in, small_in = sem("x_in"), sem("vec_in"), sem("wba_in"), sem("small_in")
        h_in, norms_in, stored = sem("h_in"), sem("norms_in"), sem("stored")
        slot_in = [sem(f"slot_in{i}") for i in range(SLOTS)]
        const_ready = sem("const_ready")
        vec_T, vec_ready = sem("vec_T"), sem("vec_ready")
        ssq_ready, var_ready, rstd_ready, xn_ready = sem("ssq_ready"), sem("var_ready"), sem("rstd_ready"), sem("xn_ready")
        xT_ready, uT_ready = sem("xT_ready"), sem("uT_ready")
        ba_ready, ba_meta_ready, ba_spread, ba_logits = sem("ba_ready"), sem("ba_meta_ready"), sem("ba_spread"), sem("ba_logits")
        g_exp, g_ready, gc_ready, gc_copied, gate_cols = sem("g_exp"), sem("g_ready"), sem("gc_ready"), sem("gc_copied"), sem("gate_cols")
        cols_dve, lam_dot, lam_exp = sem("cols_dve"), sem("lam_dot"), sem("lam_exp")
        tile_ready, tile_copied, mixed = sem("tile_ready"), sem("tile_copied"), sem("mixed")
        tr_ready, tr_copied = sem("tr_ready"), sem("tr_copied")
        qz_ready, scores_ready, biased, nmax_ready, exp_ready, w_ready = (sem("qz_ready"), sem("scores_ready"), sem("biased"), sem("nmax_ready"), sem("exp_ready"), sem("w_ready"))
        o_ready, osq_ready, oss_ready, ors_ready, ya_ready = sem("o_ready"), sem("osq_ready"), sem("oss_ready"), sem("ors_ready"), sem("ya_ready")
        conv_ready, csig, silu_ready, csq_ready, css_ready, crs_ready, qk_ready = (sem("conv_ready"), sem("csig"), sem("silu_ready"), sem("csq_ready"), sem("css_ready"), sem("crs_ready"), sem("qk_ready"))
        gate_ready = sem("gate_ready")
        dn_pe = [sem("dn_pe_a"), sem("dn_pe_b")]
        dn_dve = [sem("dn_dve_a"), sem("dn_dve_b")]
        dn_act = [sem("dn_act_a"), sem("dn_act_b")]
        dn_pool = [sem("dn_pool_a"), sem("dn_pool_b")]
        dec_masked = [sem("dec_masked_a"), sem("dec_masked_b")]
        dve_step, act_step, pool_step = sem("dve_step"), sem("act_step"), sem("pool_step")
        ssq2_ready, var2_ready, rstd2_ready, u2_ready, u2T_ps, u2T_ready = (sem("ssq2_ready"), sem("var2_ready"), sem("rstd2_ready"), sem("u2_ready"), sem("u2T_ps"), sem("u2T_ready"))
        logits_ready, r_exp_in, r_exp, assigned, ranked, routed = (sem("logits_ready"), sem("r_exp_in"), sem("r_exp"), sem("assigned"), sem("ranked"), sem("routed"))
        ov_sum, ov_flag = sem("ov_sum"), sem("ov_flag")
        picked, gathered, xg_a, xg_d, g_sig, hid_ready, hidT_ps, hidT_ready, down_a, down_d, combined = (
            sem(n) for n in ("picked", "gathered", "xg_a", "xg_d", "g_sig", "hid_ready", "hidT_ps", "hidT_ready",
                             "down_a", "down_d", "combined"))
        slot_used, pick_made, hid_step, f_step = sem("slot_used"), sem("pick_made"), sem("hid_step"), sem("f_step")
        f_in, f_h, f_sig, f_hT, f_y, f_acc, f_sum = (sem(n) for n in ("f_in", "f_h", "f_sig", "f_hT", "f_y", "f_acc", "f_sum"))
        ssq3_ready, var3_ready, rstd3_ready, out_ready = sem("ssq3_ready"), sem("var3_ready"), sem("rstd3_ready"), sem("out_ready")

        w_in_v = w_in[0].rearrange("(c p) n -> p c n", p=P)
        branch_v = {k: w[0].rearrange("(c p) n -> p c n", p=P)
                    for k, w in (("ya", w_branch_attn), ("yd", w_branch_dn), ("out", w_out))}
        w_gate_v = expert_w_gate[0].rearrange("e (c p) f -> c p e f", p=P)
        w_up_v = expert_w_up[0].rearrange("e (c p) f -> c p e f", p=P)
        w_down_v = expert_w_down[0].rearrange("e (c p) n -> c p e n", p=P)

        w_gate_e = expert_w_gate[0].rearrange("e (c p) f -> p e c f", p=P)
        w_up_e = expert_w_up[0].rearrange("e (c p) f -> p e c f", p=P)
        w_down_e = expert_w_down[0].rearrange("e (c p) n -> p e c n", p=P)
        f_down = ring[:, 2, :].rearrange("p (c n) -> p c n", c=2)

        def unit(u):
            return ring[:, u % SLOTS, :].rearrange("p (c n) -> p c n", c=NC)

        def ring_gu(c):
            return ring[:, c, :].rearrange("p (e m f) -> p e m f", e=EPB, m=2)

        def ring_down(half, fc):
            return ring[:, NC + 2 * half + fc, :].rearrange("p (e n) -> p e n", e=EPB)

        BY_DVE = ("ya", "yd", "out")

        def wait_tile_out(eng, n):
            kind = TILES[n][0]
            same = [i for i in range(n + 1) if (TILES[i][0] in BY_DVE) == (kind in BY_DVE)]
            eng.wait_ge(mixed if kind in BY_DVE else tile_copied, len(same))

        ATT_UNITS = H * TT

        def merge_rows(a, width):
            return a.unsqueeze(2).broadcast_to([P, a.shape[1], width])

        TR = []
        for h in range(H):
            TR.append(("v", h))
        for m in range(24 + 4):
            if 2 <= m < ATT_UNITS + 2:
                TR.append(("w", m - 2))
            if m >= 16 + 2 and m - 2 < 24:
                TR.append(("dv", m - 2 - 16))
        TR_NO = {k: i for i, k in enumerate(TR)}

        STEPS = ["s0", "s1", "s2", "s3", "s4", "s5", "s6", "s7", "x1", "t1", "x2", "t2", "x3", "t3", "w", "v", "o", "q"]
        META_STEPS = ["s0", "s1", "s2", "s3", "s4", "s5", "s6", "s7", "w", "m"]
        DN = [("meta", 0, s) for s in META_STEPS]
        for t in range(TT):
            for s in STEPS:
                DN += [(t, 0, s), (t, 1, s)]
        WORKS = {
            "pe": set(STEPS + META_STEPS),
            "dve": {"s0", "s1", "s3", "s4", "s5", "s6", "s7", "t1", "t2", "t3", "q", "m"},
            "act": {"s0", "s2", "s3", "s4", "s5", "s7", "x1", "x2", "x3", "w", "v", "o", "q", "m"},
            "pool": {"s0", "s1", "s2", "s7", "t1", "t2", "q"},
        }

        def works(engine, key):
            t, _, s = key
            if t == "meta":
                if engine == "pool":
                    return s in ("s0", "s2")
                if engine in ("dve", "act") and s == "w":
                    return engine == "dve"
            if engine == "dve" and s == "o":
                return t == 0
            return s in WORKS[engine]

        def done(engine, key, before=False):
            chain = [k for k in DN if k[1] == key[1]]
            upto = chain.index(key) + (0 if before else 1)
            return sum(works(engine, k) for k in chain[:upto])

        def wait_step(eng, engine, key, before=False):
            sems = {"pe": dn_pe, "dve": dn_dve, "act": dn_act, "pool": dn_pool}[engine]
            n = done(engine, key, before)
            if n:
                eng.wait_ge(sems[key[1]], n)

        def tiles_between(lo, hi):
            return list(range(lo, hi))

        filler = tiles_between(FIRST["gate"], FIRST["yd"])
        MIX_ORDER = []
        every = max(1, len(DN) // len(filler))
        k = 0
        for i, step in enumerate(DN):
            if i % every == 0 and k < len(filler):
                MIX_ORDER.append(("tile", filler[k]))
                k += 1
            MIX_ORDER.append(("dn", step))
        MIX_ORDER += [("tile", n) for n in filler[k:]]

        block = ctx.enter_context(nc.Block())

        @block.sync
        def _(sp):
            for t in range(TT):
                sp.dma_start(xin[:, t, :], x[0, t * P:(t + 1) * P, :]).then_inc(x_in, 16)
            sp.dma_start(xin[0:META, 2, :], meta_tokens).then_inc(x_in, 16)
            for u in range(N_UNITS):
                kind, j = TILES[2 * u]
                if u >= SLOTS:
                    sp.wait_ge(tile_ready, 2 * (u - SLOTS) + 2)
                src = branch_v[kind] if kind in branch_v else w_in_v
                c0 = (0 if kind in branch_v else W_COL[kind]) + j * P
                sp.dma_start(unit(u), src[:, :, c0:c0 + 2 * P]).then_inc(slot_in[u % SLOTS], 16)
                if u == N_UNITS - 2:
                    sp.wait_ge(tile_ready, FIRST["gb"] + 8)
                    for t in range(TT):
                        sp.dma_start(h_tok[:, t, :], x[0, t * P:(t + 1) * P, :]).then_inc(h_in, 16)

            def load_batch(b, wait_slot):
                for c in range(NC):
                    wait_slot(c)
                    sp.dma_start(ring_gu(c)[:, :, 0, :], w_gate_v[c, :, bass.ds(b * EPB, EPB), :]).then_inc(slot_in[c], 16)
                    sp.dma_start(ring_gu(c)[:, :, 1, :], w_up_v[c, :, bass.ds(b * EPB, EPB), :]).then_inc(slot_in[c], 16)
                for half in range(2):
                    for fc in range(2):
                        s = NC + 2 * half + fc
                        wait_slot(s)
                        sp.dma_start(ring_down(half, fc), w_down_v[fc, :, bass.ds(b * EPB, EPB), half * 512:(half + 1) * 512]).then_inc(slot_in[s], 16)

            load_batch(0, lambda s: sp.wait_ge(tile_ready, len(TILES) - 2 * SLOTS + 2 * s + 2))
            with sp.Fori(0, N_BATCH - 1) as b:
                load_batch(b + 1, lambda s: sp.wait_ge(slot_used, b * SLOTS + s + 1))

            sp.wait_ge(ov_flag, 1)
            beyond = sp.value_load(ovi[0:1, 0:1], min_val=0, max_val=2 * SEQ)
            with sp.If(beyond > 0):
                with sp.Fori(0, N_EXPERTS) as e:
                    sp.wait_ge(combined, N_BATCH)
                    sp.wait_ge(f_y, e * 4 + 1)
                    sp.dma_start(unit(0), w_gate_e[:, bass.ds(e, 1), :, :].rearrange("p a c f -> p (a c) f")).then_inc(f_in, 16)
                    sp.dma_start(unit(1), w_up_e[:, bass.ds(e, 1), :, :].rearrange("p a c f -> p (a c) f")).then_inc(f_in, 16)
                    sp.dma_start(f_down, w_down_e[:, bass.ds(e, 1), :, :].rearrange("p a c f -> p (a c) f")).then_inc(f_in, 16)

            for t in range(TT):
                sp.wait_ge(out_ready, t + 1)
                sp.dma_start(out[0, t * P:(t + 1) * P, :], result[:, t, :]).then_inc(stored, 16)
            sp.wait_ge(stored, 16 * TT)

        @block.gpsimd
        def _(pool):
            n_step = [0]

            def link(ins):
                n_step[0] += 1
                ins.then_inc(pool_step, 1)
                pool.wait_ge(pool_step, n_step[0])

            def select(o, i, pattern, op, fill, base, mult):
                return pool.affine_select(out=o, in_=i, pattern=pattern, compare_op=op, fill=fill,
                                          base=base, channel_multiplier=mult)

            pool.memset(ones, 1.0)
            pool.memset(c_eps, EPS)
            pool.memset(c_ln08, math.log(1.0 - LAMBDA_INIT))
            pool.memset(c_lnq, -0.5 * math.log(P))
            pool.memset(c_one, 1.0)
            link(pool.memset(causal_add, 0.0))
            select(ident, ones, [[-1, P]], ALU.is_equal, 0.0, 0, 1)
            select(tri, ones, [[1, P]], ALU.is_ge, 0.0, 0, -1)
            select(strict, ones, [[1, P]], ALU.is_gt, 0.0, 0, -1)
            link(select(causal_add, causal_add, [[1, P]], ALU.is_ge, NEG, 0, -1))

            def blocks(dst, src, size, fill=0.0):
                v = dst.rearrange("p (b s) -> p b s", s=size)
                w = src.rearrange("p (b s) -> p b s", s=size)
                link(select(v, w, [[-size, P // size], [0, size]], ALU.is_ge, fill, 0, 1))
                link(select(v, v, [[size, P // size], [0, size]], ALU.is_ge, fill, size - 1, -1))

            blocks(block16, ones, META)
            blocks(tri16, tri, META)
            blocks(causal_add16, causal_add, META, NEG)
            blocks(off32, ones, 32)
            blocks(off64, ones, 64)
            link(pool.tensor_tensor(off128, ones, off64, ALU.subtract))
            link(pool.tensor_tensor(off64, off64, off32, ALU.subtract))
            link(pool.tensor_tensor(off32, off32, block16, ALU.subtract))
            link(pool.tensor_copy(own_head, block16.rearrange("p (b s) -> p b s", s=META)[:, :, 0]))
            pool.tensor_copy(spread16[0:META, :].rearrange("p (b s) -> p b s", s=META),
                             ident[0:META, 0:META].unsqueeze(1).broadcast_to([META, H, META]))
            pool.iota(slot_no.bitcast(I32), [[1, CAP]], base=0, channel_multiplier=0)
            for t in range(TT):
                pool.iota(dist[:, t, :].bitcast(I32), [[1, L]], base=-(META + t * P), channel_multiplier=-1)
            pool.memset(qz, 0.0)
            for i in range(2):
                pool.memset(cbuf[:, i, 0:CONV - 1], 0.0)
            link(pool.memset(rsum, 0.0))
            pool.tensor_copy(slot_no, slot_no.bitcast(I32))
            link(pool.tensor_copy(dist, dist.bitcast(I32)))
            for t in range(TT):
                last = select(dist[:, t, :], dist[:, t, :], [[-1, L]], ALU.is_ge, NEG, META + t * P, 1)
            last.then_inc(const_ready, 1)

            def att_prep(i):
                h, t = divmod(i, TT)
                b = i % 2
                if i == 0:
                    pool.wait_ge(const_ready, 1)
                wait_tile_out(pool, FIRST["aq"] + h)
                if i >= 2:
                    pool.wait_ge(scores_ready, i - 1)
                    pool.wait_ge(biased, i - 1)
                link(pool.tensor_copy(qz[0:64, b, 0, :], aqT[0:64, h, t * P:(t + 1) * P]))
                link(pool.tensor_copy(qz[64:P, b, 1, :], aqT[64:P, h, t * P:(t + 1) * P]))
                nk = META + (t + 1) * P
                pool.tensor_scalar(bias[:, b, 0:nk], dist[:, t, 0:nk], 2.0 ** (-(h + 1)) / SCALE, 0.0,
                                   ALU.mult, ALU.add).then_inc(qz_ready, 1)

            def conv_norm(c):
                pool.wait_ge(crs_ready, c + 1)
                dst = dqT if c < H else dkT
                if c >= H:
                    pool.tensor_tensor(dkT_meta[:, c % H, :], acc[:, c % NACC, 0:META], crs[:, 0:META], ALU.mult)
                pool.tensor_tensor(dst[:, c % H, :], acc[:, c % NACC, :], crs, ALU.mult).then_inc(qk_ready, 1)

            att_prep(0)
            for m in range(24 + 4):
                if m + 1 < ATT_UNITS:
                    att_prep(m + 1)
                if 3 <= m < 16 + 3:
                    conv_norm(m - 3)

            def dn(t, c, s):
                if not works("pool", (t, c, s)):
                    return
                w = work[c]
                n = 1 if t == "meta" else 4
                hs = slice(4 * c, 4 * c + 4)
                every = lambda m: m.unsqueeze(1).broadcast_to([P, n, P])
                for engine in ("pe", "act", "dve"):
                    wait_step(pool, engine, (t, c, s))
                if s == "s0":
                    last = pool.tensor_tensor(w[1][:, 0:n, :], w[1][:, 0:n, :], every(strict), ALU.mult)
                elif s == "s1":
                    q = dqT[:, hs, META + t * P:META + (t + 1) * P]
                    last = pool.tensor_tensor(q, q, w[7][:, 0:n, :], ALU.mult)
                elif s == "s2":
                    pool.tensor_tensor(w[5][:, 0:n, :], w[1][:, 0:n, :], every(block16), ALU.mult)
                    link(pool.tensor_tensor(w[4][:, 0:n, :], w[2][:, 0:n, :], every(block16), ALU.mult))
                    last = pool.tensor_tensor(w[6][:, 0:n, :], w[4][:, 0:n, :], every(ident), ALU.add)
                elif s in ("s7", "t1", "t2"):
                    off = {"s7": off32, "t1": off64, "t2": off128}[s]
                    last = pool.tensor_tensor(w[4][:, 0:n, :], w[1][:, 0:n, :], every(off), ALU.mult)
                elif s == "q":
                    y = gateT[:, hs, t * P:(t + 1) * P]
                    last = pool.tensor_tensor(y, y, w[7][:, 0:n, :], ALU.mult)
                last.then_inc(dn_pool[c], 1)

            for what, arg in MIX_ORDER:
                if what == "dn":
                    dn(*arg)

        @block.tensor
        def _(pe):
            pe.wait_ge(const_ready, 1)
            pe.wait_ge(vec_in, 16 * 4)
            pe.transpose(bank[0][:, 0:N_VEC], vec_rows[0:N_VEC, :], ident[0:N_VEC, 0:N_VEC]).then_inc(vec_T, 1)
            for t in range(3):
                rows = P if t < TT else META
                pe.wait_ge(xn_ready, t + 1)
                for c in range(NC):
                    last = pe.transpose(bank[2 + 2 * t + c // 4][:, (c % 4) * P:(c % 4) * P + rows],
                                        xin[0:rows, t, c * P:(c + 1) * P], ident[0:rows, 0:rows])
                last.then_inc(xT_ready, 1)

            pe.wait_ge(uT_ready, 3)
            pe.wait_ge(wba_in, 16)
            for t in range(3):
                rows, c0 = (P, META + t * P) if t < TT else (META, 0)
                for c in range(NC):
                    last = pe.matmul(bank[2][0:rows, 16 * t:16 * t + 16], uT[:, c, c0:c0 + rows], w_ba[:, c, :],
                                     start=(c == 0), stop=(c == NC - 1))
            last.then_inc(ba_ready, 1)

            def tile(n):
                kind, j = TILES[n]
                u, half = divmod(n, 2)
                pe.wait_ge(slot_in[u % SLOTS], 16 * (u // SLOTS + 1))
                if n >= 2:
                    wait_tile_out(pe, n - 2)
                ps = bank[n % 2]
                w = unit(u)
                if kind == "ya" and j == 0:
                    pe.wait_ge(ya_ready, H)
                if kind == "yd" and j == 0:
                    for c in (0, 1):
                        wait_step(pe, "pool", (TT - 1, c, "q"))
                if kind == "out":
                    if j == 0:
                        pe.wait_ge(mixed, 16)
                    for c in range(NC):
                        last = pe.matmul(ps[:, 0:2 * P], mixT[:, c, half * P:(half + 1) * P], w[:, c, :],
                                         start=(c == 0), stop=(c == NC - 1))
                else:
                    src = {"ya": yaT, "yd": gateT}.get(kind)
                    if src is None:
                        src = uT if kind in ("ak", "av", "dq", "dk", "dv") else uT[:, :, META:]
                    for c in range(NC):
                        last = pe.matmul(ps[:, 0:src.shape[2]], w[:, c, half * P:(half + 1) * P], src[:, c, :],
                                         start=(c == 0), stop=(c == NC - 1))
                last.then_inc(tile_ready, 1)

            def tr_free(key):
                k = TR_NO[key]
                if k:
                    pe.wait_ge(tr_copied, k)

            def tr_values(h, key, src, with_meta):
                tr_free(key)
                if with_meta:
                    pe.transpose(bank[4][0:META, 0:P], src[:, 0:META], ident)
                for t in range(TT):
                    last = pe.transpose(bank[4][:, (t + 1) * P:(t + 2) * P], src[:, META + t * P:META + (t + 1) * P], ident)
                last.then_inc(tr_ready, 1)

            for n in range(FIRST["aq"]):
                tile(n)
                if n == 0:
                    pe.wait_ge(ba_meta_ready, 1)
                    pe.matmul(bank[3][:, 0:16], spread16[0:META, :], ba_meta[0:META, :], start=True, stop=True).then_inc(ba_spread, 1)
                if n >= FIRST["av"] + 1:
                    h = n - 1 - FIRST["av"]
                    wait_tile_out(pe, n - 1)
                    tr_values(h, ("v", h), vtmp[:, h % 2, :], True)
            for n in range(FIRST["aq"], FIRST["dq"]):
                tile(n)
                if n == FIRST["aq"]:
                    wait_tile_out(pe, n - 1)
                    tr_values(H - 1, ("v", H - 1), vtmp[:, (H - 1) % 2, :], True)
                if n == FIRST["aq"] + 1:
                    pe.wait_ge(g_ready, 1)
                    real, own = slice(0, 2 * H), slice(2 * H, NCOL)
                    pe.matmul(bank[5][:, 0:16], tri, g[:, real], start=True, stop=True)
                    pe.matmul(bank[5][:, 16:17], tri16, g[:, own], start=True, stop=True)
                    pe.matmul(bank[5][:, 17:33], ones, g[:, real], start=True, stop=True)
                    pe.matmul(bank[5][:, 33:34], block16, g[:, own], start=True, stop=True).then_inc(gc_ready, 1)

            def att_scores(i):
                h, t = divmod(i, TT)
                nk = META + (t + 1) * P
                pe.wait_ge(qz_ready, i + 1)
                if i:
                    pe.wait_ge(biased, i)
                for m in range(2):
                    last = pe.matmul(bank[2 + m][:, 0:nk], qz[:, i % 2, m, :], akT[:, h, 0:nk], start=True, stop=True)
                last.then_inc(scores_ready, 1)

            def att_turn(i):
                h, t = divmod(i, TT)
                pe.wait_ge(w_ready, i + 1)
                tr_free(("w", i))
                w = prob[:, i % 2, 0, :]
                pe.transpose(bank[4][0:META, 0:P], w[:, 0:META], ident)
                for k in range(t + 1):
                    last = pe.transpose(bank[4][:, (k + 1) * P:(k + 2) * P], w[:, META + k * P:META + (k + 1) * P], ident)
                last.then_inc(tr_ready, 1)

            def att_out(i):
                h, t = divmod(i, TT)
                pe.wait_ge(tr_copied, TR_NO[("w", i)] + 1)
                if i == 0:
                    pe.wait_ge(gc_copied, 1)
                if t == 0 and h >= 2:
                    pe.wait_ge(ya_ready, h - 1)
                o = bank[5 + h % 2][:, t * P:(t + 1) * P]
                pe.matmul(o, v_meta[0:META, h, :], wT[0:META, i % 2, 0, :], start=True, stop=False)
                for k in range(t + 1):
                    last = pe.matmul(o, v_tok[:, k, h, :], wT[:, i % 2, 1 + k, :], start=False, stop=(k == t))
                last.then_inc(o_ready, 1)

            def att_ss(h):
                pe.wait_ge(osq_ready, h + 1)
                if h:
                    pe.wait_ge(ors_ready, h)
                pe.matmul(bank[5 + h % 2][:, SEQ:2 * SEQ], ones, osq, start=True, stop=True).then_inc(oss_ready, 1)

            def conv_ss(c):
                pe.wait_ge(csq_ready, c + 1)
                if c:
                    pe.wait_ge(crs_ready, c)
                pe.matmul(bank[7][:, 0:L], ones, csq[:, c % 2, :], start=True, stop=True).then_inc(css_ready, 1)

            for m in range(24 + 4):
                if m < 24:
                    tile(FIRST["dq"] + m)
                if m < ATT_UNITS:
                    att_scores(m)
                if 2 <= m < ATT_UNITS + 2:
                    att_turn(m - 2)
                if m >= 18 and m - 2 < 24:
                    h = m - 18
                    pe.wait_ge(silu_ready, m - 2 + 1)
                    tr_values(h, ("dv", h), acc[:, (m - 2) % NACC, :], False)
                if 3 <= m < ATT_UNITS + 3:
                    att_out(m - 3)
                if 5 <= m < ATT_UNITS + 5 and m % 2 == 1:
                    att_ss((m - 5) // 2)
                if 3 <= m < 16 + 3:
                    conv_ss(m - 3)

            def dn(t, c, s):
                w = work[c]
                X, Y, Z = (bank[2 + 3 * c + i][:, :].rearrange("p (h i) -> p h i", h=4) for i in range(3))
                n = 1 if t == "meta" else 4
                for engine in ("act", "dve", "pool"):
                    wait_step(pe, engine, (t, c, s), before=True)
                if (t, c, s) == DN[0]:
                    pe.wait_ge(ya_ready, H)
                    pe.wait_ge(tr_copied, len(TR))
                    pe.wait_ge(qk_ready, 16)
                    pe.wait_ge(gate_cols, 2)

                def each(o, lhsT, rhs, start=True, stop=True):
                    for h in range(n):
                        last = pe.matmul(o[:, h, :], lhsT(h), rhs(h), start=start, stop=stop)
                    return last

                if t == "meta":
                    kT = lambda h: dkT_meta.rearrange("p h i -> p (h i)")
                    vT = lambda h: dvT_meta.rearrange("p h i -> p (h i)")
                    col = lambda h: g[:, 2 * H:2 * H + 1]
                    lower = tri16
                else:
                    cols = slice(META + t * P, META + (t + 1) * P)
                    kT = lambda h: dkT[:, 4 * c + h, cols]
                    qT = lambda h: dqT[:, 4 * c + h, cols]
                    col = lambda h: g[:, t * H + 4 * c + h:t * H + 4 * c + h + 1]
                    lower = tri
                buf = lambda i: (lambda h: w[i][:, h, :])
                if s == "s0":
                    each(X, lambda h: col(h).broadcast_to([P, P]), lambda h: lower)
                    last = each(Y, kT, kT)
                elif s == "s1":
                    for h in range(n):
                        last = pe.transpose(X[:, h, :], w[1][:, h, :], ident)
                    if t != "meta":
                        last = each(Z, kT, qT)
                elif s == "s2":
                    for h in range(n):
                        last = pe.transpose(Y[:, h, :], w[2][:, h, :], ident)
                elif s == "s3":
                    each(X, buf(4), buf(5))
                    last = each(Z, buf(5), buf(4))
                elif s == "s4":
                    each(Y, buf(0), buf(6))
                    each(X, buf(2), buf(0))
                    last = each(Z, buf(0), buf(2))
                elif s == "s5":
                    each(Y, buf(4), buf(6))
                    last = each(X, buf(5), buf(4))
                elif s == "s6":
                    last = each(Z, buf(2), buf(6))
                elif s == "s7":
                    for h in range(n):
                        pe.transpose(X[:, h, :], w[6][:, h, :], ident)
                    for h in range(n):
                        last = pe.transpose(Y[:, h, :], kT(h), ident)
                    if t == "meta":
                        last = pe.transpose(Z[:, 0, :], vT(0), ident)
                elif s in ("x1", "x2", "x3"):
                    last = each(Z, buf(4), buf(6))
                elif s in ("t1", "t2", "t3"):
                    last = each(X, buf(5), buf(0))
                    if s != "t3":
                        last = each(Z, buf(0), buf(5))
                elif s == "w":
                    if t == "meta":
                        last = pe.matmul(Z[:, 0, :], w[0][:, 0, :], w[3][:, 0, :], start=True, stop=True)
                    else:
                        last = each(X, buf(2), buf(0))
                elif s == "m":
                    for half in range(2):
                        last = pe.matmul(bank[2 + half][:, :], w[7][:, 0, :], um[:, 4 * half:4 * half + 4, :],
                                         start=True, stop=True)
                elif s == "v":
                    for h in range(n):
                        pe.matmul(Z[:, h, :], w[0][:, h, :], w[4][:, h, :], start=True, stop=False)
                        last = pe.matmul(Z[:, h, :], w[6][:, h, :], S[:, 4 * c + h, :], start=False, stop=True)
                elif s == "o":
                    for h in range(n):
                        pe.matmul(Y[:, h, :], S[:, 4 * c + h, :], qT(h), start=True, stop=False)
                        last = pe.matmul(Y[:, h, :], w[5][:, h, :], w[3][:, h, :], start=False, stop=True)
                    if t < TT - 1:
                        last = each(X, buf(7), buf(5))
                elif s == "q":
                    last = pe.matmul(Z, ones, w[6], start=True, stop=True)
                last.then_inc(dn_pe[c], 1)

            for what, arg in MIX_ORDER:
                if what == "tile":
                    tile(arg)
                else:
                    if arg == (0, 1, "s0"):
                        wait_step(pe, "dve", ("meta", 0, "m"))
                        wait_step(pe, "act", ("meta", 0, "m"))
                    dn(*arg)
            for n in range(FIRST["yd"], len(TILES)):
                tile(n)

            for t in range(TT):
                pe.wait_ge(u2_ready, t + 1)
                for c in range(NC):
                    last = pe.transpose(bank[2 + 2 * t + c // 4][:, (c % 4) * P:(c % 4 + 1) * P], u2[:, t, c * P:(c + 1) * P], ident)
                last.then_inc(u2T_ps, 1)
            pe.wait_ge(norms_in, 16 * 6)
            for t in range(TT):
                pe.wait_ge(u2T_ready, t + 1)
                for c in range(NC):
                    last = pe.matmul(bank[6][:, 64 * t:64 * t + 36], u2T[:, c, t * P:(t + 1) * P], r_w[:, c, :],
                                     start=(c == 0), stop=(c == NC - 1))
            last.then_inc(logits_ready, 1)
            wait_tile_out(pe, len(TILES) - 1)
            for t in range(TT):
                for half in range(2):
                    last = pe.matmul(bank[2 * t + half][:, :], ident, h_tok[:, t, half * 512:(half + 1) * 512],
                                     start=True, stop=False, skip_group_check=True)
            last.then_inc(gathered, 1)
            pe.wait_ge(assigned, 1)
            pe.matmul(bank[7][:, 0:32], strict, asg[:, 0, :], start=True, stop=True)
            pe.matmul(bank[7][:, 32:64], ones, asg[:, 0, :], start=True, stop=False)
            pe.matmul(bank[7][:, 32:64], strict, asg[:, 1, :], start=False, stop=True).then_inc(ranked, 1)
            pe.wait_ge(routed, 1)
            pe.matmul(bank[7][:, 64:65], ones, ovcnt[:, 0:1], start=True, stop=True).then_inc(ov_sum, 1)
            pe.wait_ge(ov_flag, 1)

            with pe.Fori(0, N_BATCH) as b:
                pe.wait_ge(picked, b + 1)
                for c in range(NC):
                    for t in range(TT):
                        last = pe.matmul(bank[6 + c // 4][:, (c % 4) * P:(c % 4 + 1) * P], u2[:, t, c * P:(c + 1) * P],
                                         pick[:, t].rearrange("p e s -> p (e s)"), start=(t == 0), stop=(t == TT - 1))
                    if c % 4 == 3:
                        last.then_inc(gathered, 1)
                for t in range(TT):
                    last = pe.transpose(bank[5][:, t * P:(t + 1) * P], pickw[:, t].rearrange("p e s -> p (e s)"), ident)
                last.then_inc(gathered, 1)
                for c in range(NC):
                    pe.wait_ge(xg_a if c < 4 else xg_d, b + 1)
                    pe.wait_ge(slot_in[c], b * 32 + 16 * (N_UNITS // SLOTS) + 32)
                    for e in range(EPB):
                        last = pe.matmul(bank[4][CAP * e:CAP * (e + 1), :], xg[:, c, CAP * e:CAP * (e + 1)],
                                         ring_gu(c)[:, e].rearrange("p m f -> p (m f)"), start=(c == 0), stop=(c == NC - 1),
                                         tile_position=(0, CAP * e))
                    last.then_inc(slot_used, 1)
                pe.wait_ge(hid_ready, b + 1)
                for fc in range(2):
                    last = pe.transpose(bank[5][:, (2 + fc) * P:(3 + fc) * P], hid[:, fc * P:(fc + 1) * P], ident)
                last.then_inc(hidT_ps, 1)
                pe.wait_ge(hidT_ready, b + 1)
                for half in range(2):
                    for fc in range(2):
                        s = NC + 2 * half + fc
                        pe.wait_ge(slot_in[s], b * 16 + 16 * (N_UNITS // SLOTS) + 16)
                        for e in range(EPB):
                            last = pe.matmul(bank[6 + half][CAP * e:CAP * (e + 1), :], hidT[:, fc, CAP * e:CAP * (e + 1)],
                                             ring_down(half, fc)[:, e, :], start=(fc == 0), stop=(fc == 1),
                                             tile_position=(0, CAP * e))
                        last.then_inc(slot_used, 1)
                for half in range(2):
                    pe.wait_ge(down_a if half == 0 else down_d, b + 1)
                    for t in range(TT):
                        last = pe.matmul(bank[2 * t + half][:, :], pickT[:, t, :], dsb[:, half * 512:(half + 1) * 512],
                                         start=False, stop=False, skip_group_check=True)
                last.then_inc(combined, 1)

            beyond = pe.value_load(ovi[0:1, 0:1], min_val=0, max_val=2 * SEQ)
            with pe.If(beyond > 0):
                for s in (f_y, f_hT, f_sum):
                    pe.sem_inc(s, 1)
                with pe.Fori(0, N_EXPERTS) as e:
                    pe.wait_ge(f_in, e * 48 + 48)
                    for fc in range(2):
                        pe.wait_ge(f_hT, e * 2 + fc + 1)
                        for k in range(2):
                            for c in range(NC):
                                last = pe.matmul(bank[4][:, k * SEQ:(k + 1) * SEQ], unit(k)[:, c, fc * P:(fc + 1) * P], u2T[:, c, :],
                                                 start=(c == 0), stop=(c == NC - 1))
                        last.then_inc(f_h, 1)
                    pe.wait_ge(f_hT, e * 2 + 3)
                    for t in range(TT):
                        for half in range(2):
                            k = 2 * t + half
                            for fc in range(2):
                                last = pe.matmul(bank[5][:, :], fhT[:, fc, t * P:(t + 1) * P], f_down[:, fc, half * 512:(half + 1) * 512],
                                                 start=(fc == 0), stop=(fc == 1))
                            last.then_inc(f_y, 1)
                            pe.wait_ge(f_acc, e * 4 + k + 1)
                            last = pe.matmul(bank[k][:, :], ident, dsb[:, 0:512], start=False, stop=False, skip_group_check=True)
                            last.then_inc(f_sum, 1)

        @block.scalar
        def _(act):
            row = lambda v, n: v.rearrange("a n -> (a n)").unsqueeze(0).broadcast_to([P, n])
            act.dma_start(vec_rows[V_NORM1:V_NORM1 + 8, :], norm1_w[0].rearrange("(c p) -> c p", p=P)).then_inc(vec_in, 16)
            act.dma_start(vec_rows[V_SUBLN:V_SUBLN + 1, :], da_subln_w).then_inc(vec_in, 16)
            act.dma_start(vec_rows[V_DNW:V_DNW + 1, :], dn_norm_w).then_inc(vec_in, 16)
            act.dma_start(vec_rows[V_CONV:N_VEC, :], dn_conv_w[0].rearrange("k (c p) -> (k c) p", p=P)).then_inc(vec_in, 16)
            act.dma_start(w_ba, w_in_v[:, :, BA_COL:BA_COL + 16]).then_inc(wba_in, 16)
            for i, v in enumerate((lambda_q1, lambda_k1, lambda_q2, lambda_k2)):
                act.dma_start(lam_in[:, i, :], row(v, 64)).then_inc(small_in, 16)
            for t in range(TT):
                act.dma_start(dtb[:, t * H:(t + 1) * H], row(dn_dt_bias, H)).then_inc(small_in, 16)
                act.dma_start(eA[:, t * H:(t + 1) * H], row(dn_A_log, H)).then_inc(small_in, 16)
            act.preload_act_table_set("natural_log_exp_and_others")
            n_step = [0]

            def link(ins):
                n_step[0] += 1
                ins.then_inc(act_step, 1)
                act.wait_ge(act_step, n_step[0])

            act.wait_ge(x_in, 16 * 3)
            act.wait_ge(const_ready, 1)
            squares = at(zone, 3, D)
            for t in range(3):
                rows = P if t < TT else META
                act.activation(squares[0:rows, t, :], xin[0:rows, t, :], ACT.Square, accum_out=ssq[0:rows, t:t + 1]).then_inc(ssq_ready, 1)
            for t in range(3):
                rows = P if t < TT else META
                act.wait_ge(var_ready, t + 1)
                link(act.activation(rstd[0:rows, t:t + 1], ssq[0:rows, t:t + 1], ACT.Ln))
                act.activation(rstd[0:rows, t:t + 1], rstd[0:rows, t:t + 1], ACT.Exp, scale=-0.5).then_inc(rstd_ready, 1)

            act.wait_ge(lam_dot, 1)
            act.activation(lam[:, 2:4], lam[:, 0:2], ACT.Exp).then_inc(lam_exp, 1)

            def decay_logs():
                act.wait_ge(ba_logits, 1)
                act.activation(beta, blog, ACT.Exp, scale=-1.0)
                act.activation(eA, eA, ACT.Exp)
                link(act.activation(sp, tmp17, ACT.Exp, scale=-1.0))
                act.activation(sp, sp, ACT.Ln, bias=c_one).then_inc(g_exp, 1)

            def decay_exps():
                act.wait_ge(gc_copied, 2)
                act.activation(egc, gc2[:, 0, :], ACT.Exp)
                act.activation(egt, gc2[:, 1, :], ACT.Exp)
                act.activation(kdec, kdec, ACT.Exp).then_inc(gate_cols, 1)

            def tile_out(n):
                kind, j = TILES[n]
                if kind in BY_DVE:
                    return
                act.wait_ge(tile_ready, n + 1)
                ps = bank[n % 2]
                if kind == "ak":
                    if j == 0:
                        act.wait_ge(uT_ready, 3)
                    last = act.activation(akT[:, j, :], ps[:, 0:L], ACT.Copy)
                elif kind == "av":
                    if j >= 2:
                        act.wait_ge(tr_ready, j - 1)
                    last = act.activation(vtmp[:, j % 2, :], ps[:, 0:L], ACT.Copy)
                elif kind == "aq":
                    last = act.activation(aqT[:, j, :], ps[:, 0:SEQ], ACT.Copy)
                elif kind in ("dq", "dk", "dv"):
                    c = n - FIRST["dq"]
                    if c >= 2:
                        act.wait_ge(conv_ready, c - 1)
                    last = act.activation(cbuf[:, c % 2, CONV - 1:], ps[:, 0:L], ACT.Copy)
                else:
                    k = n - FIRST["gate"] if kind in ("gate", "ga") else n - FIRST["gb"] + 16
                    if k >= 2:
                        act.wait_ge(gate_ready, k - 1)
                    if kind == "gate":
                        act.activation(gx[:, k % 2, :], ps[:, 0:SEQ], ACT.Copy)
                    last = act.activation(gs[:, k % 2, :], ps[:, 0:SEQ], ACT.Exp, scale=-1.0)
                last.then_inc(tile_copied, 1)

            def tr_out(key):
                act.wait_ge(tr_ready, TR_NO[key] + 1)
                kind, i = key
                ps = bank[4][:, :].rearrange("p (k e) -> p k e", e=P)
                if kind == "v":
                    act.activation(v_meta[0:META, i, :], ps[0:META, 0, :], ACT.Copy)
                    last = act.activation(v_tok[:, :, i, :], ps[:, 1:3, :], ACT.Copy)
                elif kind == "dv":
                    last = act.activation(dv_tok[:, :, i, :], ps[:, 1:3, :], ACT.Copy)
                else:
                    h, t = divmod(i, TT)
                    if i >= 2:
                        act.wait_ge(o_ready, i - 1)
                    act.activation(wT[0:META, i % 2, 0, :], ps[0:META, 0, :], ACT.Copy)
                    last = act.activation(wT[:, i % 2, 1:2 + t, :], ps[:, 1:2 + t, :], ACT.Copy)
                last.then_inc(tr_copied, 1)

            for n in range(FIRST["dq"]):
                tile_out(n)
                if FIRST["av"] + 1 <= n <= FIRST["aq"]:
                    tr_out(("v", n - 1 - FIRST["av"]))
                if n == 6:
                    decay_logs()
                if n == FIRST["aq"] + 4:
                    decay_exps()

            def att_exp(i):
                h, t = divmod(i, TT)
                nk = META + (t + 1) * P
                act.wait_ge(nmax_ready, i + 1)
                for m in range(2):
                    last = act.activation(prob[:, i % 2, m, 0:nk], prob[:, i % 2, m, 0:nk], ACT.Exp, scale=SCALE,
                                          bias=nmax[:, i % 2, m:m + 1], accum_out=rsum[:, i % 2, m:m + 1])
                last.then_inc(exp_ready, 1)

            def att_sq(h):
                act.wait_ge(o_ready, 2 * h + 2)
                if h:
                    act.wait_ge(oss_ready, h)
                act.activation(osq, bank[5 + h % 2][:, 0:SEQ], ACT.Square).then_inc(osq_ready, 1)

            def att_rs(h):
                act.wait_ge(oss_ready, h + 1)
                if h:
                    act.wait_ge(ya_ready, h)
                link(act.activation(ors, bank[5 + h % 2][:, SEQ:2 * SEQ], ACT.Ln, scale=1.0 / P, bias=c_eps))
                act.activation(ors, ors, ACT.Exp, scale=-0.5, bias=c_ln08).then_inc(ors_ready, 1)

            def conv_sig(c):
                act.wait_ge(conv_ready, c + 1)
                if c >= 2:
                    act.wait_ge(silu_ready, c - 1)
                act.activation(sg[:, c % 2, :], acc[:, c % NACC, :], ACT.Exp, scale=-1.0).then_inc(csig, 1)

            def conv_sq(c):
                act.wait_ge(silu_ready, c + 1)
                if c >= 2:
                    act.wait_ge(css_ready, c - 1)
                act.activation(csq[:, c % 2, :], acc[:, c % NACC, :], ACT.Square).then_inc(csq_ready, 1)

            def conv_rs(c):
                act.wait_ge(css_ready, c + 1)
                if c:
                    act.wait_ge(qk_ready, c)
                link(act.activation(crs, bank[7][:, 0:L], ACT.Ln, bias=c_eps))
                if c < H:
                    act.activation(crs, crs, ACT.Exp, scale=-0.5, bias=c_lnq).then_inc(crs_ready, 1)
                else:
                    act.activation(crs, crs, ACT.Exp, scale=-0.5).then_inc(crs_ready, 1)

            for m in range(24 + 4):
                if m < 24:
                    tile_out(FIRST["dq"] + m)
                if 1 <= m <= 24:
                    conv_sig(m - 1)
                if 2 <= m < 16 + 2:
                    conv_sq(m - 2)
                if 18 <= m < 26:
                    act.wait_ge(silu_ready, m - 2 + 1)
                    act.activation(dvT_meta[:, m - 18, :], acc[:, (m - 2) % NACC, 0:META], ACT.Copy)
                if 2 <= m < ATT_UNITS + 2:
                    tr_out(("w", m - 2))
                if 18 <= m < 26:
                    tr_out(("dv", m - 18))
                if m < ATT_UNITS:
                    att_exp(m)
                if 4 <= m < ATT_UNITS + 4 and m % 2 == 0:
                    att_sq((m - 4) // 2)
                if 5 <= m < ATT_UNITS + 5 and m % 2 == 1:
                    att_rs((m - 5) // 2)
                if 3 <= m < 16 + 3:
                    conv_rs(m - 3)

            def dn(t, c, s):
                if not works("act", (t, c, s)):
                    return
                w = work[c]
                X, Y, Z = (bank[2 + 3 * c + i][:, :].rearrange("p (h i) -> p h i", h=4) for i in range(3))
                n = 1 if t == "meta" else 4
                wait_step(act, "pe", (t, c, s))
                if s == "s0":
                    act.wait_ge(dec_masked[c], {"meta": 1, 0: 2 - c, 1: 3 - c}[t])
                    if t != "meta":
                        act.activation(w[7][:, 0:n, :], X[:, 0:n, :], ACT.Exp)
                    for h in range(n):
                        k = 2 * H if t == "meta" else t * H + 4 * c + h
                        last = act.activation(w[0][:, h, :], w[0][:, h, :], ACT.Exp, bias=ngc[:, k:k + 1])
                elif s == "s2":
                    last = act.activation(w[1][:, 0:n, :], Y[:, 0:n, :], ACT.Copy)
                elif s == "s3":
                    last = act.activation(w[0][:, 0:n, :], X[:, 0:n, :], ACT.Copy)
                elif s == "s4":
                    last = act.activation(w[4][:, 0:n, :], X[:, 0:n, :], ACT.Copy)
                elif s == "s5":
                    last = act.activation(w[2][:, 0:n, :], X[:, 0:n, :], ACT.Copy)
                elif s == "s7":
                    last = act.activation(w[0][:, 0:n, :], X[:, 0:n, :], ACT.Copy)
                elif s in ("x1", "x2", "x3"):
                    last = act.activation(w[5][:, 0:n, :], Z[:, 0:n, :], ACT.Copy)
                elif s == "w" and t != "meta":
                    last = act.activation(w[6][:, 0:n, :], X[:, 0:n, :], ACT.Copy, scale=-1.0)
                elif s == "v":
                    last = act.activation(w[5][:, 0:n, :], Z[:, 0:n, :], ACT.Copy)
                elif s == "m":
                    last = act.activation(S[:, 0:4, :], X, ACT.Copy)
                elif s == "o":
                    last = act.activation(w[6][:, 0:n, :], Y[:, 0:n, :], ACT.Square)
                elif s == "q":
                    link(act.activation(w[7][:, 0:n, :], Z[:, 0:n, :], ACT.Ln, scale=1.0 / P, bias=c_eps))
                    last = act.activation(w[7][:, 0:n, :], w[7][:, 0:n, :], ACT.Exp, scale=-0.5)
                last.then_inc(dn_act[c], 1)

            act.wait_ge(ya_ready, H)
            act.wait_ge(qk_ready, 16)
            for what, arg in MIX_ORDER:
                if what == "tile":
                    tile_out(arg)
                else:
                    dn(*arg)

            for c in (0, 1):
                wait_step(act, "pool", (TT - 1, c, "q"))
            act.dma_start(norm2_b, row(norm2_w, D)).then_inc(norms_in, 16)
            act.dma_start(fnorm_b, final_norm_w.unsqueeze(0).broadcast_to([P, D])).then_inc(norms_in, 16)
            act.dma_start(r_w[:, :, 0:4], router_group_w[0].rearrange("(c p) n -> p c n", p=P)).then_inc(norms_in, 16)
            act.dma_start(r_w[:, :, 4:36], router_expert_w[0].rearrange("(c p) n -> p c n", p=P)).then_inc(norms_in, 16)
            act.dma_start(r_b[:, 0:4], row(router_group_b, 4)).then_inc(norms_in, 16)
            act.dma_start(r_b[:, 4:36], row(router_expert_b, 32)).then_inc(norms_in, 16)

            def root(into, ready, src, k):
                link(act.activation(into[:, k:k + 1], src[:, k:k + 1], ACT.Ln))
                act.activation(into[:, k:k + 1], into[:, k:k + 1], ACT.Exp, scale=-0.5).then_inc(ready, 1)

            act.wait_ge(norms_in, 16 * 6)
            for t in range(TT):
                act.wait_ge(mixed, 16 + 7 + t)
                if t:
                    act.wait_ge(ssq2_ready, t)
                act.activation(junk, h_tok[:, t, :], ACT.Square, accum_out=ssq[:, t:t + 1]).then_inc(ssq2_ready, 1)
            for t in range(TT):
                act.wait_ge(var2_ready, t + 1)
                root(rstd, rstd2_ready, ssq, t)
            for t in range(TT):
                act.wait_ge(u2T_ps, t + 1)
                for k in range(2):
                    last = act.activation(u2T[:, 4 * k:4 * k + 4, t * P:(t + 1) * P],
                                          bank[2 + 2 * t + k][:, :].rearrange("p (c i) -> p c i", i=P), ACT.Copy)
                last.then_inc(u2T_ready, 1)
            act.wait_ge(r_exp_in, 1)
            act.activation(gd, gd, ACT.Exp).then_inc(r_exp, 1)
            act.wait_ge(r_exp_in, 2)
            act.activation(sc[:, 4, :], sc[:, 4, :], ACT.Exp).then_inc(r_exp, 1)

            with act.Fori(0, N_BATCH) as b:
                act.wait_ge(gathered, b * 3 + 2)
                act.activation(xg[:, 0:4, :], bank[6][:, :].rearrange("p (c i) -> p c i", i=P), ACT.Copy).then_inc(xg_a, 1)
                act.wait_ge(slot_used, b * SLOTS + NC)
                act.activation(sil, bank[4][:, 0:D_EXPERT], ACT.Exp, scale=-1.0).then_inc(g_sig, 1)
                act.wait_ge(slot_used, b * SLOTS + NC + 2)
                act.activation(dsb[:, 0:512], bank[6][:, :], ACT.Copy).then_inc(down_a, 1)

            beyond = act.value_load(ovi[0:1, 0:1], min_val=0, max_val=2 * SEQ)
            with act.If(beyond > 0):
                with act.Fori(0, N_EXPERTS) as e:
                    for fc in range(2):
                        act.wait_ge(f_h, e * 2 + fc + 1)
                        act.activation(ftmp, bank[4][:, 0:SEQ], ACT.Exp, scale=-1.0).then_inc(f_sig, 1)
                act.wait_ge(f_sum, N_EXPERTS * 4 + 1)

            act.wait_ge(combined, N_BATCH)
            for t in range(TT):
                if t:
                    act.wait_ge(ssq3_ready, t)
                for half in range(2):
                    last = act.activation(junk[:, half * 512:(half + 1) * 512], bank[2 * t + half][:, :], ACT.Square,
                                          accum_out=sc[:, 8 + half, t:t + 1])
                last.then_inc(ssq3_ready, 1)
            for t in range(TT):
                act.wait_ge(var3_ready, t + 1)
                root(rstd, rstd3_ready, ssq, t)

        @block.vector
        def _(dve):
            n_step = [0]

            def link(ins):
                n_step[0] += 1
                ins.then_inc(dve_step, 1)
                dve.wait_ge(dve_step, n_step[0])

            tt, ts, stt = dve.tensor_tensor, dve.tensor_scalar, dve.scalar_tensor_tensor

            dve.wait_ge(vec_T, 1)
            dve.tensor_copy(vec[:, 0:N_VEC], bank[0][:, 0:N_VEC]).then_inc(vec_ready, 1)
            for t in range(3):
                rows = P if t < TT else META
                dve.wait_ge(ssq_ready, t + 1)
                ts(ssq[0:rows, t:t + 1], ssq[0:rows, t:t + 1], 1.0 / D, EPS, ALU.mult, ALU.add).then_inc(var_ready, 1)
            for t in range(3):
                rows = P if t < TT else META
                dve.wait_ge(rstd_ready, t + 1)
                ts(xin[0:rows, t, :], xin[0:rows, t, :], rstd[0:rows, t:t + 1], None, ALU.mult).then_inc(xn_ready, 1)
            dve.wait_ge(vec_ready, 1)
            for t in range(3):
                rows, c0 = (P, META + t * P) if t < TT else (META, 0)
                dve.wait_ge(xT_ready, t + 1)
                for k in range(2):
                    ps = bank[2 + 2 * t + k][:, :].rearrange("p (c i) -> p c i", i=P)[:, :, 0:rows]
                    last = tt(uT[:, 4 * k:4 * k + 4, c0:c0 + rows], ps,
                              vec[:, V_NORM1 + 4 * k:V_NORM1 + 4 * k + 4].unsqueeze(2).broadcast_to([P, 4, rows]), ALU.mult)
                last.then_inc(uT_ready, 1)

            dve.wait_ge(small_in, 16 * 8)
            dve.wait_ge(const_ready, 1)
            own = slice(2 * H, NCOL)
            for v in (dtb, eA):
                link(dve.tensor_tensor_reduce(tmp17[:, 0:H], v[:, 0:H], own_head, 1.0, 0.0, ALU.mult, ALU.add, v[:, own]))
            dve.wait_ge(ba_ready, 1)
            dve.tensor_copy(ba_meta[0:META, :], bank[2][0:META, 32:48]).then_inc(ba_meta_ready, 1)
            ba = bank[2][:, 0:32].rearrange("p (t k) -> p t k", t=TT)
            dve.tensor_copy(blog[:, 0:16].rearrange("p (t h) -> p t h", t=TT), ba[:, :, 0:H])
            dve.tensor_copy(alog[:, 0:16].rearrange("p (t h) -> p t h", t=TT), ba[:, :, H:16])
            dve.wait_ge(ba_spread, 1)
            link(dve.tensor_tensor_reduce(tmp17[:, 0:H], bank[3][:, 0:H], own_head, 1.0, 0.0, ALU.mult, ALU.add, blog[:, own]))
            link(dve.tensor_tensor_reduce(tmp17[:, 0:H], bank[3][:, H:16], own_head, 1.0, 0.0, ALU.mult, ALU.add, alog[:, own]))
            link(tt(alog, alog, dtb, ALU.add))
            stt(tmp17, alog, -1.0, alog, ALU.mult, ALU.max).then_inc(ba_logits, 1)

            dve.tensor_tensor_reduce(lam_in[:, 0, :], lam_in[:, 0, :], lam_in[:, 1, :], 1.0, 0.0, ALU.mult, ALU.add, lam[:, 0:1])
            dve.tensor_tensor_reduce(lam_in[:, 2, :], lam_in[:, 2, :], lam_in[:, 3, :], 1.0, 0.0, ALU.mult, ALU.add, lam[:, 1:2]).then_inc(lam_dot, 1)
            dve.wait_ge(lam_exp, 1)
            link(stt(lam[:, 4:5], lam[:, 2:3], -1.0, lam[:, 3:4], ALU.mult, ALU.add))
            link(ts(lam[:, 5:6], lam[:, 4:5], -LAMBDA_INIT, None, ALU.add))
            minus_lambda = lam[:, 5:6]

            dve.wait_ge(g_exp, 1)
            link(ts(beta, beta, 1.0, None, ALU.add))
            link(dve.reciprocal(beta, beta))
            ts(nbeta, beta, -1.0, None, ALU.mult)
            link(stt(sp, alog, 0.0, sp, ALU.max, ALU.add))
            stt(g, sp, -1.0, eA, ALU.mult, ALU.mult).then_inc(g_ready, 1)
            dve.wait_ge(gc_ready, 1)
            dve.tensor_copy(gc2.rearrange("p a b -> p (a b)"), bank[5][:, 0:2 * NCOL]).then_inc(gc_copied, 1)
            dve.wait_ge(gc_copied, 1)
            ts(ngc, gc2[:, 0, :], -1.0, None, ALU.mult)
            tt(kdec, gc2[:, 1, :], gc2[:, 0, :], ALU.subtract).then_inc(gc_copied, 1)
            dve.wait_ge(gate_cols, 1)
            tt(begc, beta, egc, ALU.mult).then_inc(gate_cols, 1)

            def conv(c):
                wait_tile_out(dve, FIRST["dq"] + c)
                if c >= NACC:
                    p = c - NACC
                    if p < 16:
                        dve.wait_ge(qk_ready, p + 1)
                    else:
                        dve.wait_ge(tr_copied, TR_NO[("dv", p - 16)] + 1)
                a, x_ = acc[:, c % NACC, :], cbuf[:, c % 2, :]
                tap = lambda k: vec[:, V_CONV + k * 3 * H + c:V_CONV + k * 3 * H + c + 1]
                link(ts(a, x_[:, 0:L], tap(0), None, ALU.mult))
                for k in range(1, CONV):
                    last = stt(a, x_[:, k:k + L], tap(k), a, ALU.mult, ALU.add)
                    if k < CONV - 1:
                        link(last)
                last.then_inc(conv_ready, 1)

            def silu(c):
                dve.wait_ge(csig, c + 1)
                s_ = sg[:, c % 2, :]
                link(ts(s_, s_, 1.0, None, ALU.add))
                link(dve.reciprocal(s_, s_))
                a = acc[:, c % NACC, :]
                tt(a, a, s_, ALU.mult).then_inc(silu_ready, 1)

            def att_bias(i):
                h, t = divmod(i, TT)
                nk = META + (t + 1) * P
                dve.wait_ge(scores_ready, i + 1)
                dve.wait_ge(qz_ready, i + 1)
                if i >= 2:
                    dve.wait_ge(tr_ready, TR_NO[("w", i - 2)] + 1)
                for m in range(2):
                    last = dve.tensor_tensor_reduce(prob[:, i % 2, m, 0:nk], bank[2 + m][:, 0:nk], bias[:, i % 2, 0:nk], 1.0, -3e38,
                                                    ALU.add, ALU.max, mx[:, i % 2, m:m + 1])
                last.then_inc(biased, 1)
                dve.wait_ge(biased, i + 1)
                ts(nmax[:, i % 2, :], mx[:, i % 2, :], -SCALE, None, ALU.mult).then_inc(nmax_ready, 1)

            def att_w(i):
                h, t = divmod(i, TT)
                nk = META + (t + 1) * P
                dve.wait_ge(exp_ready, i + 1)
                r = rinv[:, i % 2, :]
                link(dve.reciprocal(r, rsum[:, i % 2, :]))
                link(ts(r[:, 1:2], r[:, 1:2], minus_lambda, None, ALU.mult))
                a, b = prob[:, i % 2, 0, 0:nk], prob[:, i % 2, 1, 0:nk]
                link(ts(b, b, r[:, 1:2], None, ALU.mult))
                stt(a, a, r[:, 0:1], b, ALU.mult, ALU.add).then_inc(w_ready, 1)

            def att_norm(h):
                dve.wait_ge(ors_ready, h + 1)
                stt(yaT[:, h, :], bank[5 + h % 2][:, 0:SEQ], vec[:, V_SUBLN:V_SUBLN + 1], ors,
                    ALU.mult, ALU.mult).then_inc(ya_ready, 1)

            for m in range(24 + 4):
                if m < 24:
                    conv(m)
                if 1 <= m < ATT_UNITS + 1:
                    att_w(m - 1)
                if m < ATT_UNITS:
                    att_bias(m)
                if 1 <= m <= 24:
                    silu(m - 1)
                if 5 <= m < ATT_UNITS + 5 and m % 2 == 1:
                    att_norm((m - 5) // 2)

            def tile_out(n):
                kind, j = TILES[n]
                ps = bank[n % 2][:, 0:SEQ]
                if kind in ("gate", "ga", "gb"):
                    k = n - FIRST["gate"] if kind in ("gate", "ga") else n - FIRST["gb"] + 16
                    wait_tile_out(dve, n)
                    s_ = gs[:, k % 2, :]
                    link(ts(s_, s_, 1.0, None, ALU.add))
                    if kind == "gate":
                        link(dve.reciprocal(s_, s_))
                        last = tt(gateT[:, j, :], gx[:, k % 2, :], s_, ALU.mult)
                    else:
                        last = dve.reciprocal({"ga": gaT, "gb": gbT}[kind][:, j, :], s_)
                    last.then_inc(gate_ready, 1)
                    return
                dve.wait_ge(tile_ready, n + 1)
                if kind == "ya":
                    last = tt(gaT[:, j, :], ps, gaT[:, j, :], ALU.mult)
                elif kind == "yd":
                    link(tt(gbT[:, j, :], ps, gbT[:, j, :], ALU.mult))
                    last = tt(mixT[:, j, :], gaT[:, j, :], gbT[:, j, :], ALU.add)
                else:
                    if j == 0:
                        dve.wait_ge(h_in, 16 * TT)
                    piece = h_tok[:, j % 2, (j // 2) * 256:(j // 2 + 1) * 256]
                    last = tt(piece, ps, piece, ALU.add)
                last.then_inc(mixed, 1)

            def dn(t, c, s):
                if not works("dve", (t, c, s)):
                    return
                w = work[c]
                X, Y, Z = (bank[2 + 3 * c + i][:, :].rearrange("p (h i) -> p h i", h=4)[:, 0:1 if t == "meta" else 4, :] for i in range(3))
                n = 1 if t == "meta" else 4
                k0 = 2 * H if t == "meta" else t * H + 4 * c
                hs = slice(4 * c, 4 * c + 4)
                per_head = lambda v: v[:, k0:k0 + n].unsqueeze(2).broadcast_to([P, n, P])
                wait_step(dve, "pe", (t, c, s))
                b = lambda i: w[i][:, 0:n, :]
                if s == "s0":
                    mask = causal_add16 if t == "meta" else causal_add
                    tt(b(0), X, mask.unsqueeze(1).broadcast_to([P, n, P]), ALU.add).then_inc(dec_masked[c], 1)
                    wait_step(dve, "act", (t, c, s))
                    last = tt(b(1), Y, b(0), ALU.mult)
                elif s == "s1":
                    last = tt(b(2), X, per_head(nbeta), ALU.mult)
                    if t != "meta":
                        last = tt(b(3), Z, b(0), ALU.mult)
                elif s == "s3":
                    last = dve.tensor_copy(b(2), Z)
                elif s == "s4":
                    dve.tensor_copy(b(5), Z)
                    last = tt(b(6), Y, b(6), ALU.add)
                elif s == "s5":
                    last = tt(b(6), Y, b(6), ALU.add)
                elif s == "s6":
                    last = tt(b(6), Z, b(6), ALU.add)
                elif s == "s7":
                    last = tt(b(7), Y, per_head(kdec), ALU.mult)
                    if t == "meta":
                        last = tt(b(3), Z, per_head(beta), ALU.mult)
                    else:
                        last = tt(b(2), Y, per_head(begc), ALU.mult)
                elif s in ("t1", "t2", "t3"):
                    last = tt(b(0), X, b(0), ALU.add)
                    if s != "t3":
                        last = tt(b(6), Z, b(6), ALU.add)
                    else:
                        last = tt(b(4), dv_tok[:, t, hs, :], per_head(beta), ALU.mult)
                elif s == "w":
                    last = tt(um, Z[:, 0, :].unsqueeze(1).broadcast_to([P, H, P]),
                              own_head.unsqueeze(2).broadcast_to([P, H, P]), ALU.mult)
                elif s == "m":
                    last = dve.tensor_copy(S[:, 4:8, :], bank[3][:, :].rearrange("p (h i) -> p h i", h=4))
                elif s == "o":
                    for h in range(n):
                        last = stt(S[:, 4 * c + h, :], S[:, 4 * c + h, :], egt[:, k0 + h:k0 + h + 1], X[:, h, :], ALU.mult, ALU.add)
                elif s == "q":
                    wait_step(dve, "act", (t, c, s))
                    flat = lambda a: a.rearrange("p h i -> p (h i)")
                    last = stt(flat(b(7)), flat(Y), vec[:, V_DNW:V_DNW + 1], flat(b(7)), ALU.mult, ALU.mult)
                last.then_inc(dn_dve[c], 1)

            dve.wait_ge(tr_copied, len(TR))
            dve.wait_ge(qk_ready, 16)
            for what, arg in MIX_ORDER:
                if what == "tile":
                    tile_out(arg)
                else:
                    dn(*arg)
            for n in range(FIRST["yd"], len(TILES)):
                tile_out(n)

            for t in range(TT):
                dve.wait_ge(ssq2_ready, t + 1)
                ts(ssq[:, t:t + 1], ssq[:, t:t + 1], 1.0 / D, EPS, ALU.mult, ALU.add).then_inc(var2_ready, 1)
            dve.wait_ge(norms_in, 16 * 6)
            for t in range(TT):
                dve.wait_ge(rstd2_ready, t + 1)
                stt(u2[:, t, :], h_tok[:, t, :], rstd[:, t:t + 1], norm2_b, ALU.mult, ALU.mult).then_inc(u2_ready, 1)
            dve.wait_ge(logits_ready, 1)
            wide = lambda v, n: v.unsqueeze(2).broadcast_to([P, TT, n])
            sc_ = lambda i: sc[:, i, :]
            link(tt(lg, bank[6][:, 0:128].rearrange("p (t k) -> p t k", t=TT)[:, :, 0:36],
                    r_b.unsqueeze(1).broadcast_to([P, TT, 36]), ALU.add))
            link(dve.tensor_reduce(sc_(0), lg[:, :, 0:4], AX, ALU.max))
            link(tt(gd, lg[:, :, 0:4], wide(sc_(0), 4), ALU.subtract))

            def first(into, equal, n):
                for t in range(TT):
                    link(dve.tensor_tensor_scan(cum[:, t, 0:n], ones[:, 0:n], equal[:, t, :], 0.0, ALU.mult, ALU.add))
                link(stt(into, cum[:, :, 0:n], 1.0, equal, ALU.is_equal, ALU.mult))

            link(ts(pen, gd, 0.0, None, ALU.is_ge))
            first(gsel, pen, 4)
            link(ts(pen, gsel, -1.0, -NEG, ALU.add, ALU.mult))
            for t in range(TT):
                last = tt(me[:, t, :].rearrange("p (g e) -> p g e", g=4), lg[:, t, 4:36].rearrange("p (g e) -> p g e", g=4),
                          pen[:, t, :].unsqueeze(2).broadcast_to([P, 4, PER_GROUP]), ALU.add)
            last.then_inc(r_exp_in, 1)
            dve.wait_ge(r_exp_in, 1)
            link(dve.tensor_reduce(sc_(1), me, AX, ALU.max))
            link(tt(eq, me, wide(sc_(1), 32), ALU.is_equal))
            first(e1, eq, 32)
            link(stt(me2, e1, 2 * NEG, me, ALU.mult, ALU.add))
            link(dve.tensor_reduce(sc_(2), me2, AX, ALU.max))
            link(tt(eq, me2, wide(sc_(2), 32), ALU.is_equal))
            first(e2, eq, 32)
            tt(asg, e1, e2, ALU.add).then_inc(assigned, 1)
            tt(sc_(4), sc_(2), sc_(1), ALU.subtract).then_inc(r_exp_in, 1)
            dve.wait_ge(r_exp, 1)
            link(dve.tensor_reduce(sc_(5), gd, AX, ALU.add))
            link(dve.reciprocal(sc_(5), sc_(5)))
            dve.wait_ge(r_exp, 2)
            link(ts(sc_(6), sc_(4), 1.0, None, ALU.add))
            link(dve.reciprocal(sc_(6), sc_(6)))
            link(tt(sc_(6), sc_(6), sc_(5), ALU.mult))
            link(tt(sc_(7), sc_(6), sc_(4), ALU.mult))
            link(tt(e1, e1, wide(sc_(6), 32), ALU.mult))
            link(tt(e2, e2, wide(sc_(7), 32), ALU.mult))
            link(tt(comb, e1, e2, ALU.add))
            dve.wait_ge(ranked, 1)
            link(ts(rank, bank[7][:, 0:64].rearrange("p (t k) -> p t k", t=TT), 1.0, None, ALU.add))
            link(tt(rank, rank, asg, ALU.mult))
            link(ts(rank, rank, -1.0, None, ALU.add))
            link(ts(eq, rank, float(CAP), None, ALU.is_ge))
            tt(ovf, eq, comb, ALU.mult)
            link(dve.tensor_reduce(sc_(9), eq, AX, ALU.add))
            tt(ovcnt[:, 0:1], sc[:, 9, 0:1], sc[:, 9, 1:2], ALU.add).then_inc(routed, 1)
            dve.wait_ge(ov_sum, 1)
            dve.tensor_copy(ovi, bank[7][:, 64:65]).then_inc(ov_flag, 1)

            with dve.Fori(0, N_BATCH) as b:
                dve.wait_ge(gathered, b * 3 + 1)
                for t in range(TT):
                    last = tt(pick[:, t], slot_no.unsqueeze(1).broadcast_to([P, EPB, CAP]),
                              rank[:, t, bass.ds(b * EPB, EPB)].unsqueeze(2).broadcast_to([P, EPB, CAP]), ALU.is_equal)
                last.then_inc(pick_made, 1)
                dve.wait_ge(pick_made, b + 1)
                for t in range(TT):
                    last = tt(pickw[:, t], pick[:, t],
                              comb[:, t, bass.ds(b * EPB, EPB)].unsqueeze(2).broadcast_to([P, EPB, CAP]), ALU.mult)
                last.then_inc(picked, 1)
                dve.wait_ge(gathered, b * 3 + 3)
                dve.tensor_copy(xg[:, 4:8, :], bank[7][:, :].rearrange("p (c i) -> p c i", i=P)).then_inc(xg_d, 1)
                dve.wait_ge(gathered, b * 3 + 4)
                dve.tensor_copy(pickT, bank[5][:, 0:2 * P].rearrange("p (t i) -> p t i", t=TT))
                dve.wait_ge(g_sig, b + 1)
                ts(sil, sil, 1.0, None, ALU.add).then_inc(hid_step, 1)
                dve.wait_ge(hid_step, b * 3 + 1)
                dve.reciprocal(sil, sil).then_inc(hid_step, 1)
                dve.wait_ge(hid_step, b * 3 + 2)
                tt(sil, bank[4][:, 0:D_EXPERT], sil, ALU.mult).then_inc(hid_step, 1)
                dve.wait_ge(hid_step, b * 3 + 3)
                tt(hid, bank[4][:, D_EXPERT:2 * D_EXPERT], sil, ALU.mult).then_inc(hid_ready, 1)
                dve.wait_ge(hidT_ps, b + 1)
                dve.tensor_copy(hidT, bank[5][:, 2 * P:4 * P].rearrange("p (t i) -> p t i", t=2)).then_inc(hidT_ready, 1)
                dve.wait_ge(slot_used, b * SLOTS + SLOTS)
                dve.tensor_copy(dsb[:, 512:D], bank[7][:, :]).then_inc(down_d, 1)

            beyond = dve.value_load(ovi[0:1, 0:1], min_val=0, max_val=2 * SEQ)
            with dve.If(beyond > 0):
                with dve.Fori(0, N_EXPERTS) as e:
                    for fc in range(2):
                        dve.wait_ge(f_sig, e * 2 + fc + 1)
                        ts(ftmp, ftmp, 1.0, None, ALU.add).then_inc(f_step, 1)
                        dve.wait_ge(f_step, e * 6 + fc * 3 + 1)
                        dve.reciprocal(ftmp, ftmp).then_inc(f_step, 1)
                        dve.wait_ge(f_step, e * 6 + fc * 3 + 2)
                        tt(ftmp, bank[4][:, 0:SEQ], ftmp, ALU.mult).then_inc(f_step, 1)
                        dve.wait_ge(f_step, e * 6 + fc * 3 + 3)
                        tt(fhT[:, fc, :], bank[4][:, SEQ:2 * SEQ], ftmp, ALU.mult).then_inc(f_hT, 1)
                    for t in range(TT):
                        for half in range(2):
                            k = 2 * t + half
                            dve.wait_ge(f_y, e * 4 + k + 2)
                            dve.wait_ge(f_sum, e * 4 + k + 1)
                            dve.tensor_scalar(dsb[:, 0:512], bank[5][:, :], ovf[:, t, bass.ds(e, 1)], None, ALU.mult).then_inc(f_acc, 1)
                dve.wait_ge(f_sum, N_EXPERTS * 4 + 1)

            for t in range(TT):
                dve.wait_ge(ssq3_ready, t + 1)
                link(tt(ssq[:, t:t + 1], sc[:, 8, t:t + 1], sc[:, 9, t:t + 1], ALU.add))
                ts(ssq[:, t:t + 1], ssq[:, t:t + 1], 1.0 / D, EPS, ALU.mult, ALU.add).then_inc(var3_ready, 1)
            for t in range(TT):
                dve.wait_ge(rstd3_ready, t + 1)
                for half in range(2):
                    cols = slice(half * 512, (half + 1) * 512)
                    last = stt(result[:, t, cols], bank[2 * t + half][:, :], rstd[:, t:t + 1], fnorm_b[:, cols], ALU.mult, ALU.mult)
                last.then_inc(out_ready, 1)


_INS = ['x', 'meta_tokens', 'norm1_w', 'w_in', 'lambda_q1', 'lambda_k1', 'lambda_q2', 'lambda_k2', 'da_subln_w',
        'dn_conv_w', 'dn_A_log', 'dn_dt_bias', 'dn_norm_w', 'w_branch_attn', 'w_branch_dn', 'w_out', 'norm2_w',
        'router_group_w', 'router_group_b', 'router_expert_w', 'router_expert_b', 'expert_w_gate', 'expert_w_up',
        'expert_w_down', 'final_norm_w']
_OUTS = [((1, SEQ, D), 'float32')]


def kernel(**inputs):
    import numpy as _np
    import concourse.bacc as _bacc
    from concourse import mybir as _mybir
    from concourse.bass_utils import run_bass_kernel_spmd as _run

    nc = _bacc.Bacc("TRN2", target_bir_lowering=False, num_devices=1)
    arrays, args = {}, []
    for name in _INS:
        a = _np.ascontiguousarray(inputs[name])
        arrays[f"in_{name}_dram"] = a
        args.append(nc.dram_tensor(f"in_{name}_dram", a.shape, _mybir.dt.from_np(a.dtype), kind="ExternalInput").ap())
    for i, (shape, dtype) in enumerate(_OUTS):
        dt = _mybir.dt.from_np(_np.dtype(dtype))
        args.append(nc.dram_tensor(f"out_{i}_dram", shape, dt, kind="ExternalOutput").ap())
    hybrid_block(nc, *args)
    r = _run(nc, [arrays], core_ids=[0])
    got = tuple(r.results[0][f"out_{i}_dram"] for i in range(len(_OUTS)))
    return got[0]
```

```python
from contextlib import ExitStack
import math

import concourse.bass as bass
from concourse import mybir

P = 128
D = 1024
NC = D // P
META = 16
SEQ = 256
L = META + SEQ
TT = SEQ // P
H = 8
SCALE = 64 ** -0.5
LAMBDA_INIT = 0.8 - 0.6 * math.exp(-0.3 * 0)
EPS = 1e-6
NEG = -1e30
CONV = 4
N_GROUPS, PER_GROUP, N_EXPERTS, D_EXPERT = 4, 8, 32, 256
EPB = 4
N_BATCH = N_EXPERTS // EPB
CAP = P // EPB
UNIT = 2048
SLOTS = 12
NSS = 3 * H

F32 = mybir.dt.float32
F32R = mybir.dt.float32r
I32 = mybir.dt.int32
ALU = mybir.AluOpType
ACT = mybir.ActivationFunctionType
AX = mybir.AxisListType.X

W_COL = dict(aq=0, ak=1024, av=2048, dq=3072, dk=4096, dv=5120, gate=6144, ga=7184, gb=8208)
BA_COL = 7168
KINDS = ["ak", "av", "aq", "dq", "dk", "dv", "gate", "ga", "ya", "gb", "yd", "out"]
TILES = [(kind, j) for kind in KINDS for j in range(8)]
FIRST = {kind: 8 * i for i, kind in enumerate(KINDS)}
SPLIT = [n for n, (kind, _) in enumerate(TILES) if kind not in ("ya", "out")]
AHEAD = 3
NSPLIT = AHEAD + 2
TSLOTS = 6
N_UNITS = len(TILES) // 2
V_NORM1, V_SUBLN, V_DNW, V_CONV = 0, 8, 9, 10
N_VEC = V_CONV + CONV * 3 * H


def hybrid_block(nc, x, meta_tokens, norm1_w, w_in, lambda_q1, lambda_k1, lambda_q2, lambda_k2, da_subln_w,
                 dn_conv_w, dn_A_log, dn_dt_bias, dn_norm_w, w_branch_attn, w_branch_dn, w_out, norm2_w,
                 router_group_w, router_group_b, router_expert_w, router_expert_b, expert_w_gate,
                 expert_w_up, expert_w_down, final_norm_w, out, dbg=None):
    with ExitStack() as ctx:
        def sem(name):
            return ctx.enter_context(nc.semaphore(name))

        FLOATS = 53100
        base = -(-nc.sbuf_base // 64) * 64
        arena = nc.alloc_sbuf_tensor_at("arena", [P, FLOATS], F32, offset=base)
        bank = [ctx.enter_context(nc.psum_tensor(f"bank{i}", [P, 512], F32)) for i in range(8)]
        top = [0]

        def at(start, *shape):
            n = math.prod(shape)
            ap = arena[:, start:start + n]
            if len(shape) == 2:
                return ap.rearrange("p (a b) -> p a b", b=shape[1])
            if len(shape) == 3:
                return ap.rearrange("p (a b c) -> p a b c", b=shape[1], c=shape[2])
            return ap

        def rounded(name, start, a, b, kind=F32R):
            t = nc.alloc_sbuf_tensor_at(name, [P, a * b], kind, offset=base + 4 * start)
            return t[:, :].rearrange("p (a b) -> p a b", b=b)

        def new(*shape):
            start = top[0]
            top[0] += math.prod(shape)
            assert top[0] <= FLOATS, top[0]
            return at(start, *shape)

        ring = new(SLOTS, UNIT)
        w_hi = [rounded(f"w_hi{i}", (TSLOTS + i) * UNIT, NC, P) for i in range(NSPLIT)]
        w_lo = [rounded(f"w_lo{i}", (TSLOTS + i) * UNIT + D, NC, P) for i in range(NSPLIT)]
        spare = (TSLOTS + NSPLIT) * UNIT
        gx, gs = at(spare, 2, SEQ), at(spare + 2 * SEQ, 2, SEQ)
        S = at(spare + 4 * SEQ, H, P)
        ident, ones, tri, strict, causal_add = (new(P) for _ in range(5))
        block16, off32, off64, off128 = (new(P) for _ in range(4))
        tri16, causal_add16, spread16 = (new(P) for _ in range(3))
        own_head = new(H)
        one_of = new(2 * NSS - 1)
        c_rs, c_mean_eps = new(1), new(1)
        slot_no = new(CAP)
        const = new(4)
        c_eps, c_one = (const[:, i:i + 1] for i in range(2))
        vec = new(P)
        lam_in, lam = new(4, 64), new(8)
        ssq, rstd = new(4), new(4)
        NCOL = 2 * H + 1
        blog, alog, dtb, eA, beta, g, sp, tmp17 = (new(NCOL) for _ in range(8))
        gc2 = new(2, NCOL)
        egc, begc, kdec, egt, ngc, nbeta = (new(NCOL) for _ in range(6))
        ba_meta = new(16)
        mx, rsum, rinv, nmax = (new(2, 2) for _ in range(4))
        top[0] = -(-top[0] // 8) * 8
        uT_start = top[0]
        new(2 * NC, L)
        uT_hi, uT_lo = rounded("uT_hi", uT_start, NC, L), rounded("uT_lo", uT_start + NC * L, NC, L)
        dqk_start = top[0]
        dqT, dkT = new(H, L), new(H, L)
        dv_start = top[0]
        dv_tok, dvT_meta, dkT_meta = new(TT, H, P), new(H, META), new(H, META)
        yaT_start = top[0]
        yaT = new(H, SEQ)
        top[0] = -(-top[0] // 8) * 8
        zone = top[0]

        aqT, akT, v_tok = new(H, SEQ), new(H, L), new(TT, H, P)
        v_meta = at(spare, H, P)
        NPREP = 3
        qz = new(NPREP * 2, P).rearrange("p (a b) i -> p a b i", b=2)
        dist, bias = new(TT, L), new(NPREP, L)
        prob = at(dv_start, 2, 2, L)
        wT = new(2, 3, P)
        vtmp = new(2, L)
        osq = at(dv_start + H * P + 6 * P, SEQ)
        rs_rows = new(L)
        cbuf = new(2, L + CONV - 1)
        NACC = 3
        acc = new(NACC, L)
        sg = new(2, L)
        csq = vtmp
        first_use_end = top[0]
        xin = at(dqk_start, 3, D)
        vec_rows = at(dqk_start + 3 * D, P)
        w_ba = at(dqk_start + 3 * D + P, NC, 16)
        uT = rounded("uT", dv_start, NC, L, F32)

        top[0] = zone
        NB = 8
        work = [[new(4, P) for _ in range(NB)] for _ in range(2)]
        yd_hi, yd_lo = rounded("yd_hi", zone, H, SEQ), rounded("yd_lo", zone + 2048, H, SEQ)
        gateT = rounded("gateT", top[0], H, SEQ, F32)
        new(H * SEQ)
        gaT = new(H, SEQ)
        gbT = at(yaT_start, H, SEQ)
        mixT = gaT
        um = at(zone + 8 * 512, H, P)

        h_tok = at(uT_start, TT, D)
        u2, u2T = at(dqk_start, TT, D), at(dqk_start + TT * D, NC, SEQ)
        norm2_b, fnorm_b = at(dv_start, D), at(dv_start + D, D)
        top[0] = zone
        r_w, r_b = at(uT_start + TT * D, NC, 36), at(uT_start + TT * D + NC * 36, 36)
        junk = new(D)
        lg, me, me2, eq, e1, e2 = new(TT, 36), new(TT, 32), new(TT, 32), new(TT, 32), new(TT, 32), new(TT, 32)
        cum, comb, asg, rank, ovf = new(TT, 32), new(TT, 32), new(TT, 32), new(TT, 32), new(TT, 32)
        gsel, gd, pen = new(TT, 4), new(TT, 4), new(TT, 4)
        sc = new(12, TT)
        pick, pickw = new(TT, EPB, CAP), new(TT, EPB, CAP)
        pickT = new(TT, P)
        xg = new(NC, P)
        sil, hid, hidT = new(D_EXPERT), new(D_EXPERT), new(2, P)
        dsb = new(D)
        ovcnt = new(2)
        ovi = new(1).bitcast(I32)
        ftmp = new(SEQ)
        fhT = new(2, SEQ)
        result = new(TT, D)
        assert top[0] <= zone + 8192 + 2048, top[0] - zone

        x_in, vec_in, wba_in, small_in = sem("x_in"), sem("vec_in"), sem("wba_in"), sem("small_in")
        h_in, norms_in, stored = sem("h_in"), sem("norms_in"), sem("stored")
        slot_in = [sem(f"slot_in{i}") for i in range(SLOTS)]
        const_ready = sem("const_ready")
        vec_T, vec_ready = sem("vec_T"), sem("vec_ready")
        ssq_ready, var_ready, rstd_ready, xn_ready = sem("ssq_ready"), sem("var_ready"), sem("rstd_ready"), sem("xn_ready")
        xT_ready, uT_ready = sem("xT_ready"), sem("uT_ready")
        ba_ready, ba_meta_ready, ba_spread, ba_logits = sem("ba_ready"), sem("ba_meta_ready"), sem("ba_spread"), sem("ba_logits")
        g_exp, g_ready, gc_ready, gc_copied, gate_cols = sem("g_exp"), sem("g_ready"), sem("gc_ready"), sem("gc_copied"), sem("gate_cols")
        cols_dve, lam_dot, lam_exp = sem("cols_dve"), sem("lam_dot"), sem("lam_exp")
        tile_ready, tile_copied, mixed = sem("tile_ready"), sem("tile_copied"), sem("mixed")
        tr_ready, tr_copied = sem("tr_ready"), sem("tr_copied")
        qz_ready, scores_ready, biased, nmax_ready, exp_ready, w_ready = (sem("qz_ready"), sem("scores_ready"), sem("biased"), sem("nmax_ready"), sem("exp_ready"), sem("w_ready"))
        o_ready, osq_ready, oss_ready = sem("o_ready"), sem("osq_ready"), sem("oss_ready")
        conv_ready, csig, silu_ready, csq_ready, css_ready, rs_ready, qk_ready, spread_ready, o_copied = (sem("conv_ready"), sem("csig"), sem("silu_ready"), sem("csq_ready"), sem("css_ready"), sem("rs_ready"), sem("qk_ready"), sem("spread_ready"), sem("o_copied"))
        gate_ready = sem("gate_ready")
        w_hi_ready, w_lo_dve, w_lo_pool, u_hi, u_lo = sem("w_hi_ready"), sem("w_lo_dve"), sem("w_lo_pool"), sem("u_hi"), sem("u_lo")
        yd_hi_ready, yd_lo_ready = sem("yd_hi_ready"), sem("yd_lo_ready")
        dn_pe = [sem("dn_pe_a"), sem("dn_pe_b")]
        dn_dve = [sem("dn_dve_a"), sem("dn_dve_b")]
        dn_act = [sem("dn_act_a"), sem("dn_act_b")]
        dn_pool = [sem("dn_pool_a"), sem("dn_pool_b")]
        dec_masked = [sem("dec_masked_a"), sem("dec_masked_b")]
        dve_step, act_step, pool_step = sem("dve_step"), sem("act_step"), sem("pool_step")
        ssq2_ready, var2_ready, rstd2_ready, u2_ready, u2T_ps, u2T_ready = (sem("ssq2_ready"), sem("var2_ready"), sem("rstd2_ready"), sem("u2_ready"), sem("u2T_ps"), sem("u2T_ready"))
        logits_ready, r_exp_in, r_exp, assigned, ranked, routed = (sem("logits_ready"), sem("r_exp_in"), sem("r_exp"), sem("assigned"), sem("ranked"), sem("routed"))
        ov_sum, ov_flag = sem("ov_sum"), sem("ov_flag")
        picked, gathered, xg_a, xg_d, g_sig, hid_ready, hidT_ps, hidT_ready, down_a, down_d, combined = (
            sem(n) for n in ("picked", "gathered", "xg_a", "xg_d", "g_sig", "hid_ready", "hidT_ps", "hidT_ready",
                             "down_a", "down_d", "combined"))
        slot_used, pick_made, hid_step, f_step = sem("slot_used"), sem("pick_made"), sem("hid_step"), sem("f_step")
        f_in, f_h, f_sig, f_hT, f_y, f_acc, f_sum = (sem(n) for n in ("f_in", "f_h", "f_sig", "f_hT", "f_y", "f_acc", "f_sum"))
        ssq3_ready, var3_ready, rstd3_ready, out_ready = sem("ssq3_ready"), sem("var3_ready"), sem("rstd3_ready"), sem("out_ready")

        w_in_v = w_in[0].rearrange("(c p) n -> p c n", p=P)
        branch_v = {k: w[0].rearrange("(c p) n -> p c n", p=P)
                    for k, w in (("ya", w_branch_attn), ("yd", w_branch_dn), ("out", w_out))}
        w_gate_v = expert_w_gate[0].rearrange("e (c p) f -> c p e f", p=P)
        w_up_v = expert_w_up[0].rearrange("e (c p) f -> c p e f", p=P)
        w_down_v = expert_w_down[0].rearrange("e (c p) n -> c p e n", p=P)

        w_gate_e = expert_w_gate[0].rearrange("e (c p) f -> p e c f", p=P)
        w_up_e = expert_w_up[0].rearrange("e (c p) f -> p e c f", p=P)
        w_down_e = expert_w_down[0].rearrange("e (c p) n -> p e c n", p=P)
        f_down = ring[:, 2, :].rearrange("p (c n) -> p c n", c=2)

        def unit(u):
            return ring[:, u % TSLOTS, :].rearrange("p (c n) -> p c n", c=NC)

        def low_by_pool(q):
            return FIRST["dq"] <= q < FIRST["gate"] and q % 3 != 0

        def wait_split(eng, q):
            eng.wait_ge(w_hi_ready, q + 1)
            mine = [i for i in range(q + 1) if low_by_pool(i) == low_by_pool(q)]
            eng.wait_ge(w_lo_pool if low_by_pool(q) else w_lo_dve, len(mine))

        def split_source(eng, q):
            n = SPLIT[q]
            u, half = divmod(n, 2)
            eng.wait_ge(slot_in[u % TSLOTS], 16 * (u // TSLOTS + 1))
            if q >= NSPLIT:
                eng.wait_ge(tile_ready, SPLIT[q - NSPLIT] + 1)
            return unit(u)[:, :, half * P:(half + 1) * P]

        def split_high(q):
            nc.scalar.activation(w_hi[q % NSPLIT], split_source(nc.scalar, q), ACT.Copy).then_inc(w_hi_ready, 1)

        def split_low(eng, q):
            src = split_source(eng, q)
            eng.wait_ge(w_hi_ready, q + 1)
            eng.tensor_tensor(w_lo[q % NSPLIT], src, w_hi[q % NSPLIT].bitcast(F32), ALU.subtract).then_inc(
                w_lo_pool if low_by_pool(q) else w_lo_dve, 1)

        def splits_at(n):
            if n not in SPLIT:
                return []
            q = SPLIT.index(n)
            return [q + AHEAD] if q + AHEAD < len(SPLIT) else []

        def ring_gu(c):
            return ring[:, c, :].rearrange("p (e m f) -> p e m f", e=EPB, m=2)

        def ring_down(half, fc):
            return ring[:, NC + 2 * half + fc, :].rearrange("p (e n) -> p e n", e=EPB)

        BY_DVE = ("ya", "yd", "out")

        def wait_tile_out(eng, n):
            kind = TILES[n][0]
            same = [i for i in range(n + 1) if (TILES[i][0] in BY_DVE) == (kind in BY_DVE)]
            eng.wait_ge(mixed if kind in BY_DVE else tile_copied, len(same))

        ATT_UNITS = H * TT
        SLOTS_A = 24 + 4
        SPREAD = [H + h for h in range(H)] + list(range(H)) + [2 * H + h for h in range(H)]

        SPREAD_BANKS = (2, 3, 5, 6)

        def spread_at(m):
            return SPREAD[4 * (m - 22):4 * (m - 21)] if m >= 22 else []

        def merge_rows(a, width):
            return a.unsqueeze(2).broadcast_to([P, a.shape[1], width])

        TR = []
        for h in range(H):
            TR.append(("v", h))
        for m in range(SLOTS_A):
            if 2 <= m < ATT_UNITS + 2:
                TR.append(("w", m - 2))
            if m >= 16 + 2 and m - 2 < 24:
                TR.append(("dv", m - 2 - 16))
        TR_NO = {k: i for i, k in enumerate(TR)}

        STEPS = ["s0", "s1", "s2", "s3", "s4", "s5", "s6", "s7", "x1", "t1", "x2", "t2", "x3", "t3", "w", "v", "o", "q"]
        META_STEPS = ["s0", "s1", "s2", "s3", "s4", "s5", "s6", "s7", "w", "m"]
        DN = [("meta", 0, s) for s in META_STEPS]
        for t in range(TT):
            for s in STEPS:
                DN += [(t, 0, s), (t, 1, s)]
        WORKS = {
            "pe": set(STEPS + META_STEPS),
            "dve": {"s0", "s1", "s3", "s4", "s5", "s6", "s7", "t1", "t2", "t3", "q", "m"},
            "act": {"s0", "s2", "s3", "s4", "s5", "s7", "x1", "x2", "x3", "w", "v", "o", "q", "m"},
            "pool": {"s0", "s1", "s2", "s7", "t1", "t2", "q"},
        }

        def works(engine, key):
            t, _, s = key
            if t == "meta":
                if engine == "pool":
                    return s in ("s0", "s2")
                if engine in ("dve", "act") and s == "w":
                    return engine == "dve"
            if engine == "dve" and s == "o":
                return t == 0
            return s in WORKS[engine]

        def done(engine, key, before=False):
            chain = [k for k in DN if k[1] == key[1]]
            upto = chain.index(key) + (0 if before else 1)
            return sum(works(engine, k) for k in chain[:upto])

        def wait_step(eng, engine, key, before=False):
            sems = {"pe": dn_pe, "dve": dn_dve, "act": dn_act, "pool": dn_pool}[engine]
            n = done(engine, key, before)
            if n:
                eng.wait_ge(sems[key[1]], n)

        every, first_half, rest = slice(None), slice(0, H // 2), slice(H // 2, H)
        RESULTS = [[(every, every, slice(0, SEQ - P)), (every, first_half, slice(SEQ - P, SEQ))],
                   [(every, rest, slice(SEQ - P, SEQ))]]

        AFTER = 4
        filler = list(range(FIRST["dq"] + SLOTS_A, FIRST["yd"] - AFTER))
        after = list(range(FIRST["yd"] - AFTER, FIRST["yd"]))
        MIX_ORDER = []
        groups = [[k] for k in DN if k[0] == "meta"]
        pairs = [k for k in DN if k[0] != "meta"]
        groups += [pairs[i:i + 2] for i in range(0, len(pairs), 2)]
        given = 0
        for i, group in enumerate(groups):
            while given < len(filler) and given * (len(groups) - 4) < i * len(filler):
                MIX_ORDER.append(("tile", filler[given]))
                given += 1
            MIX_ORDER += [("dn", k) for k in group]
        MIX_ORDER += [("tile", n) for n in filler[given:]]

        BEHIND = []
        held = []
        for what in MIX_ORDER:
            if what[0] == "tile":
                BEHIND.append(("split", what[1]))
                held.append(what)
            else:
                BEHIND.append(what)
                BEHIND += held
                held = []
        BEHIND += held
        for i, n in enumerate(after):
            MIX_ORDER.append(("tile", n))
            BEHIND += [("split", n)] + ([("result", i)] if i < 2 else []) + [("tile", n)]

        block = ctx.enter_context(nc.Block())

        @block.sync
        def _(sp):
            for t in range(TT):
                sp.dma_start(xin[:, t, :], x[0, t * P:(t + 1) * P, :]).then_inc(x_in, 16)
            sp.dma_start(xin[0:META, 2, :], meta_tokens).then_inc(x_in, 16)
            for u in range(N_UNITS):
                kind, j = TILES[2 * u]
                if u >= TSLOTS:
                    n = 2 * (u - TSLOTS)
                    if n in SPLIT:
                        wait_split(sp, SPLIT.index(n))
                        wait_split(sp, SPLIT.index(n + 1))
                    else:
                        sp.wait_ge(tile_ready, n + 2)
                src = branch_v[kind] if kind in branch_v else w_in_v
                c0 = (0 if kind in branch_v else W_COL[kind]) + j * P
                sp.dma_start(unit(u), src[:, :, c0:c0 + 2 * P]).then_inc(slot_in[u % TSLOTS], 16)
                if u == N_UNITS - 2:
                    sp.wait_ge(tile_ready, FIRST["gb"] + 8)
                    for t in range(TT):
                        sp.dma_start(h_tok[:, t, :], x[0, t * P:(t + 1) * P, :]).then_inc(h_in, 16)

            def load_batch(b, wait_slot):
                for c in range(NC):
                    wait_slot(c)
                    sp.dma_start(ring_gu(c)[:, :, 0, :], w_gate_v[c, :, bass.ds(b * EPB, EPB), :]).then_inc(slot_in[c], 16)
                    sp.dma_start(ring_gu(c)[:, :, 1, :], w_up_v[c, :, bass.ds(b * EPB, EPB), :]).then_inc(slot_in[c], 16)
                for half in range(2):
                    for fc in range(2):
                        s = NC + 2 * half + fc
                        wait_slot(s)
                        sp.dma_start(ring_down(half, fc), w_down_v[fc, :, bass.ds(b * EPB, EPB), half * 512:(half + 1) * 512]).then_inc(slot_in[s], 16)

            def wait_tiles(s):
                n = 2 * (N_UNITS - TSLOTS + s)
                if s >= TSLOTS:
                    sp.wait_ge(tile_ready, len(TILES))
                elif n in SPLIT:
                    wait_split(sp, SPLIT.index(n))
                    wait_split(sp, SPLIT.index(n + 1))
                else:
                    sp.wait_ge(tile_ready, n + 2)

            load_batch(0, wait_tiles)
            with sp.Fori(0, N_BATCH - 1) as b:
                load_batch(b + 1, lambda s: sp.wait_ge(slot_used, b * SLOTS + s + 1))

            sp.wait_ge(ov_flag, 1)
            beyond = sp.value_load(ovi[0:1, 0:1], min_val=0, max_val=2 * SEQ)
            with sp.If(beyond > 0):
                with sp.Fori(0, N_EXPERTS) as e:
                    sp.wait_ge(combined, N_BATCH)
                    sp.wait_ge(f_y, e * 4 + 1)
                    sp.dma_start(unit(0), w_gate_e[:, bass.ds(e, 1), :, :].rearrange("p a c f -> p (a c) f")).then_inc(f_in, 16)
                    sp.dma_start(unit(1), w_up_e[:, bass.ds(e, 1), :, :].rearrange("p a c f -> p (a c) f")).then_inc(f_in, 16)
                    sp.dma_start(f_down, w_down_e[:, bass.ds(e, 1), :, :].rearrange("p a c f -> p (a c) f")).then_inc(f_in, 16)

            for t in range(TT):
                sp.wait_ge(out_ready, t + 1)
                sp.dma_start(out[0, t * P:(t + 1) * P, :], result[:, t, :]).then_inc(stored, 16)
            sp.wait_ge(stored, 16 * TT)

        @block.gpsimd
        def _(pool):
            n_step = [0]

            def link(ins):
                n_step[0] += 1
                ins.then_inc(pool_step, 1)
                pool.wait_ge(pool_step, n_step[0])

            def select(o, i, pattern, op, fill, base, mult):
                return pool.affine_select(out=o, in_=i, pattern=pattern, compare_op=op, fill=fill,
                                          base=base, channel_multiplier=mult)

            pool.memset(ones, 1.0)
            pool.memset(c_eps, EPS)
            pool.memset(one_of, 0.0)
            pool.memset(c_rs, 0.0)
            pool.memset(c_one, 1.0)
            link(pool.memset(causal_add, 0.0))
            select(ident, ones, [[-1, P]], ALU.is_equal, 0.0, 0, 1)
            select(tri, ones, [[1, P]], ALU.is_ge, 0.0, 0, -1)
            select(strict, ones, [[1, P]], ALU.is_gt, 0.0, 0, -1)
            link(select(causal_add, causal_add, [[1, P]], ALU.is_ge, NEG, 0, -1))

            def blocks(dst, src, size, fill=0.0):
                v = dst.rearrange("p (b s) -> p b s", s=size)
                w = src.rearrange("p (b s) -> p b s", s=size)
                link(select(v, w, [[-size, P // size], [0, size]], ALU.is_ge, fill, 0, 1))
                link(select(v, v, [[size, P // size], [0, size]], ALU.is_ge, fill, size - 1, -1))

            blocks(block16, ones, META)
            blocks(tri16, tri, META)
            blocks(causal_add16, causal_add, META, NEG)
            blocks(off32, ones, 32)
            blocks(off64, ones, 64)
            link(pool.tensor_tensor(off128, ones, off64, ALU.subtract))
            link(pool.tensor_tensor(off64, off64, off32, ALU.subtract))
            link(pool.tensor_tensor(off32, off32, block16, ALU.subtract))
            link(pool.tensor_copy(own_head, block16.rearrange("p (b s) -> p b s", s=META)[:, :, 0]))
            pool.tensor_copy(spread16[0:META, :].rearrange("p (b s) -> p b s", s=META),
                             ident[0:META, 0:META].unsqueeze(1).broadcast_to([META, H, META]))
            pool.iota(slot_no.bitcast(I32), [[1, CAP]], base=0, channel_multiplier=0)
            for t in range(TT):
                pool.iota(dist[:, t, :].bitcast(I32), [[1, L]], base=-(META + t * P), channel_multiplier=-1)
            pool.memset(qz, 0.0)
            pool.memset(v_meta, 0.0)
            pool.memset(rs_rows, 0.0)
            for i in range(2):
                pool.memset(wT[:, i, 0, :], 0.0)
            for i in range(2):
                pool.memset(cbuf[:, i, 0:CONV - 1], 0.0)
            pool.memset(one_of[:, NSS - 1:NSS], 1.0)
            link(select(c_rs, c_rs, [[0, 1]], ALU.is_ge, -0.5 * math.log(P), -H, 1))
            link(select(c_mean_eps, c_eps, [[0, 1]], ALU.is_ge, EPS * P, 2 * H - 1, -1))
            link(select(c_rs, c_rs, [[0, 1]], ALU.is_ge, 0.5 * math.log(P) + math.log(1.0 - LAMBDA_INIT), 2 * H - 1, -1))
            link(pool.memset(rsum, 0.0))
            pool.tensor_copy(slot_no, slot_no.bitcast(I32))
            link(pool.tensor_copy(dist, dist.bitcast(I32)))
            for t in range(TT):
                last = select(dist[:, t, :], dist[:, t, :], [[-1, L]], ALU.is_ge, NEG, META + t * P, 1)
            last.then_inc(const_ready, 1)

            def att_prep(i):
                h, t = divmod(i, TT)
                b = i % NPREP
                if i == 0:
                    pool.wait_ge(const_ready, 1)
                wait_tile_out(pool, FIRST["aq"] + h)
                if i >= NPREP:
                    pool.wait_ge(scores_ready, i - NPREP + 1)
                    pool.wait_ge(biased, i - NPREP + 1)
                link(pool.tensor_copy(qz[0:64, b, 0, :], aqT[0:64, h, t * P:(t + 1) * P]))
                link(pool.tensor_copy(qz[64:P, b, 1, :], aqT[64:P, h, t * P:(t + 1) * P]))
                nk = META + (t + 1) * P
                pool.tensor_scalar(bias[:, b, 0:nk], dist[:, t, 0:nk], 2.0 ** (-(h + 1)) / SCALE, 0.0,
                                   ALU.mult, ALU.add).then_inc(qz_ready, 1)

            for n in range(FIRST["dq"]):
                for q in splits_at(n):
                    if low_by_pool(q):
                        split_low(pool, q)
            for i in range(NPREP - 1):
                att_prep(i)
            for n in range(FIRST["dq"], FIRST["dq"] + SLOTS_A):
                i = n - FIRST["dq"] + NPREP - 1
                if i < ATT_UNITS:
                    att_prep(i)
                for q in splits_at(n):
                    if low_by_pool(q):
                        split_low(pool, q)

            def dn(t, c, s):
                if not works("pool", (t, c, s)):
                    return
                w = work[c]
                n = 1 if t == "meta" else 4
                hs = slice(4 * c, 4 * c + 4)
                every = lambda m: m.unsqueeze(1).broadcast_to([P, n, P])
                for engine in ("pe", "act", "dve"):
                    wait_step(pool, engine, (t, c, s))
                if s == "s0":
                    last = pool.tensor_tensor(w[1][:, 0:n, :], w[1][:, 0:n, :], every(strict), ALU.mult)
                elif s == "s1":
                    q = dqT[:, hs, META + t * P:META + (t + 1) * P]
                    last = pool.tensor_tensor(q, q, w[7][:, 0:n, :], ALU.mult)
                elif s == "s2":
                    pool.tensor_tensor(w[5][:, 0:n, :], w[1][:, 0:n, :], every(block16), ALU.mult)
                    link(pool.tensor_tensor(w[4][:, 0:n, :], w[2][:, 0:n, :], every(block16), ALU.mult))
                    last = pool.tensor_tensor(w[6][:, 0:n, :], w[4][:, 0:n, :], every(ident), ALU.add)
                elif s in ("s7", "t1", "t2"):
                    off = {"s7": off32, "t1": off64, "t2": off128}[s]
                    last = pool.tensor_tensor(w[4][:, 0:n, :], w[1][:, 0:n, :], every(off), ALU.mult)
                elif s == "q":
                    y = gateT[:, hs, t * P:(t + 1) * P]
                    last = pool.tensor_tensor(y, y, w[7][:, 0:n, :], ALU.mult)
                last.then_inc(dn_pool[c], 1)

            for what, arg in BEHIND:
                if what == "dn":
                    dn(*arg)

        @block.tensor
        def _(pe):
            pe.wait_ge(const_ready, 1)
            pe.wait_ge(vec_in, 16 * 4)
            pe.transpose(bank[0][:, 0:N_VEC], vec_rows[0:N_VEC, :], ident[0:N_VEC, 0:N_VEC]).then_inc(vec_T, 1)
            for t in range(3):
                rows = P if t < TT else META
                pe.wait_ge(xn_ready, t + 1)
                for c in range(NC):
                    last = pe.transpose(bank[2 + 2 * t + c // 4][:, (c % 4) * P:(c % 4) * P + rows],
                                        xin[0:rows, t, c * P:(c + 1) * P], ident[0:rows, 0:rows])
                last.then_inc(xT_ready, 1)

            def ba_logit_products():
                pe.wait_ge(wba_in, 16)
                for t in range(3):
                    rows, c0 = (P, META + t * P) if t < TT else (META, 0)
                    for c in range(NC):
                        last = pe.matmul(bank[2][0:rows, 16 * t:16 * t + 16], uT[:, c, c0:c0 + rows], w_ba[:, c, :],
                                         start=(c == 0), stop=(c == NC - 1))
                last.then_inc(ba_ready, 1)

            def tile(n):
                kind, j = TILES[n]
                u, half = divmod(n, 2)
                if n in SPLIT:
                    q = SPLIT.index(n)
                    wait_split(pe, q)
                    hi, lo = w_hi[q % NSPLIT], w_lo[q % NSPLIT]
                else:
                    pe.wait_ge(slot_in[u % TSLOTS], 16 * (u // TSLOTS + 1))
                if n >= 2:
                    wait_tile_out(pe, n - 2)
                ps = bank[n % 2]
                if kind == "ya":
                    if j == 0:
                        pe.wait_ge(qk_ready, NSS)
                    for c in range(NC):
                        last = pe.matmul(ps[:, 0:SEQ], unit(u)[:, c, half * P:(half + 1) * P], yaT[:, c, :],
                                         start=(c == 0), stop=(c == NC - 1))
                elif kind == "out":
                    t = j % 2
                    pe.wait_ge(mixed, 2 * NC)
                    for c in range(NC):
                        last = pe.matmul(ps[:, 0:SEQ], mixT[:, c, t * P:(t + 1) * P], unit(u)[:, c, :],
                                         start=(c == 0), stop=(c == NC - 1))
                else:
                    if kind == "yd":
                        pe.wait_ge(yd_hi_ready, 2)
                        pe.wait_ge(yd_lo_ready, 2)
                        s_hi, s_lo = yd_hi, yd_lo
                    else:
                        s_hi, s_lo = (uT_hi, uT_lo) if kind in ("ak", "av", "dq", "dk", "dv") else (uT_hi[:, :, META:], uT_lo[:, :, META:])
                    for c in range(NC):
                        for i, (a, b) in enumerate(((hi, s_hi), (hi, s_lo), (lo, s_hi))):
                            last = pe.matmul(ps[:, 0:b.shape[2]], a[:, c, :], b[:, c, :],
                                             start=(c == 0 and i == 0), stop=(c == NC - 1 and i == 2))
                last.then_inc(tile_ready, 1)

            def tr_free(key):
                k = TR_NO[key]
                if k:
                    pe.wait_ge(tr_copied, k)

            def tr_values(h, key, src, with_meta):
                tr_free(key)
                if with_meta:
                    pe.transpose(bank[4][0:META, 0:P], src[:, 0:META], ident)
                for t in range(TT):
                    last = pe.transpose(bank[4][:, (t + 1) * P:(t + 2) * P], src[:, META + t * P:META + (t + 1) * P], ident)
                last.then_inc(tr_ready, 1)

            for n in range(FIRST["aq"]):
                if n == 0:
                    pe.wait_ge(u_hi, 1)
                    pe.wait_ge(u_lo, 1)
                tile(n)
                if n == 2:
                    ba_logit_products()
                if n == 3:
                    pe.wait_ge(ba_meta_ready, 1)
                    pe.matmul(bank[3][:, 0:16], spread16[0:META, :], ba_meta[0:META, :], start=True, stop=True).then_inc(ba_spread, 1)
                if n >= FIRST["av"] + 1:
                    h = n - 1 - FIRST["av"]
                    wait_tile_out(pe, n - 1)
                    tr_values(h, ("v", h), vtmp[:, h % 2, :], True)
            for n in range(FIRST["aq"], FIRST["dq"]):
                tile(n)
                if n == FIRST["aq"]:
                    wait_tile_out(pe, n - 1)
                    tr_values(H - 1, ("v", H - 1), vtmp[:, (H - 1) % 2, :], True)
                if n == FIRST["aq"] + 1:
                    pe.wait_ge(g_ready, 1)
                    real, own = slice(0, 2 * H), slice(2 * H, NCOL)
                    pe.matmul(bank[5][:, 0:16], tri, g[:, real], start=True, stop=True)
                    pe.matmul(bank[5][:, 16:17], tri16, g[:, own], start=True, stop=True)
                    pe.matmul(bank[5][:, 17:33], ones, g[:, real], start=True, stop=True)
                    pe.matmul(bank[5][:, 33:34], block16, g[:, own], start=True, stop=True).then_inc(gc_ready, 1)

            def att_scores(i):
                h, t = divmod(i, TT)
                nk = META + (t + 1) * P
                pe.wait_ge(qz_ready, i + 1)
                if i:
                    pe.wait_ge(biased, i)
                for m in range(2):
                    last = pe.matmul(bank[2 + m][:, 0:nk], qz[:, i % NPREP, m, :], akT[:, h, 0:nk], start=True, stop=True)
                last.then_inc(scores_ready, 1)

            def att_turn(i):
                h, t = divmod(i, TT)
                pe.wait_ge(w_ready, i + 1)
                tr_free(("w", i))
                w = prob[:, i % 2, 0, :]
                pe.transpose(bank[4][0:META, 0:P], w[:, 0:META], ident)
                for k in range(t + 1):
                    last = pe.transpose(bank[4][:, (k + 1) * P:(k + 2) * P], w[:, META + k * P:META + (k + 1) * P], ident)
                last.then_inc(tr_ready, 1)

            def att_out(i):
                h, t = divmod(i, TT)
                pe.wait_ge(tr_copied, TR_NO[("w", i)] + 1)
                if i == 0:
                    pe.wait_ge(gc_copied, 1)
                if t == 0 and h >= 2:
                    pe.wait_ge(o_copied, h - 1)
                    pe.wait_ge(osq_ready, h - 1)
                o = bank[5 + h % 2][:, t * P:(t + 1) * P]
                pe.matmul(o, v_meta[:, h, :], wT[:, i % 2, 0, :], start=True, stop=False)
                for k in range(t + 1):
                    last = pe.matmul(o, v_tok[:, k, h, :], wT[:, i % 2, 1 + k, :], start=False, stop=(k == t))
                last.then_inc(o_ready, 1)

            def row_sums(i, src, n):
                return pe.matmul(bank[7][0:NSS, 0:n], one_of[:, NSS - 1 - i:2 * NSS - 1 - i], src,
                                 start=(i == 0), stop=(i == NSS - 1))

            def att_ss(h):
                pe.wait_ge(osq_ready, h + 1)
                row_sums(2 * H + h, osq, SEQ).then_inc(oss_ready, 1)

            def conv_ss(c):
                pe.wait_ge(csq_ready, c + 1)
                row_sums(c, csq[:, c % 2, :], L).then_inc(css_ready, 1)

            def spread(k):
                if k == 0:
                    pe.wait_ge(rs_ready, 1)
                if k < 4:
                    pe.wait_ge(biased, ATT_UNITS)
                    pe.wait_ge(o_copied, H)
                    pe.wait_ge(osq_ready, H)
                else:
                    pe.wait_ge(qk_ready, k - 3)
                pe.matmul(bank[SPREAD_BANKS[k % 4]][:, 0:L], ident[:, SPREAD[k]:SPREAD[k] + 1].broadcast_to([P, P]), rs_rows,
                          start=True, stop=True).then_inc(spread_ready, 1)

            for m in range(SLOTS_A):
                tile(FIRST["dq"] + m)
                if m < ATT_UNITS:
                    att_scores(m)
                if 2 <= m < ATT_UNITS + 2:
                    att_turn(m - 2)
                if m >= 18 and m - 2 < 24:
                    h = m - 18
                    pe.wait_ge(silu_ready, m - 2 + 1)
                    tr_values(h, ("dv", h), acc[:, (m - 2) % NACC, :], False)
                if 3 <= m < ATT_UNITS + 3:
                    att_out(m - 3)
                if 5 <= m < ATT_UNITS + 5 and m % 2 == 1:
                    att_ss((m - 5) // 2)
                if 3 <= m < 16 + 3:
                    conv_ss(m - 3)
                for i in spread_at(m):
                    spread(SPREAD.index(i))

            def dn(t, c, s):
                w = work[c]
                X, Y, Z = (bank[2 + 3 * c + i][:, :].rearrange("p (h i) -> p h i", h=4) for i in range(3))
                n = 1 if t == "meta" else 4
                for engine in ("act", "dve", "pool"):
                    wait_step(pe, engine, (t, c, s), before=True)
                if (t, c, s) == DN[0]:
                    pe.wait_ge(tr_copied, len(TR))
                    pe.wait_ge(qk_ready, NSS)
                    pe.wait_ge(gate_cols, 2)

                def each(o, lhsT, rhs, start=True, stop=True):
                    for h in range(n):
                        last = pe.matmul(o[:, h, :], lhsT(h), rhs(h), start=start, stop=stop)
                    return last

                if t == "meta":
                    kT = lambda h: dkT_meta.rearrange("p h i -> p (h i)")
                    vT = lambda h: dvT_meta.rearrange("p h i -> p (h i)")
                    col = lambda h: g[:, 2 * H:2 * H + 1]
                    lower = tri16
                else:
                    cols = slice(META + t * P, META + (t + 1) * P)
                    kT = lambda h: dkT[:, 4 * c + h, cols]
                    qT = lambda h: dqT[:, 4 * c + h, cols]
                    col = lambda h: g[:, t * H + 4 * c + h:t * H + 4 * c + h + 1]
                    lower = tri
                buf = lambda i: (lambda h: w[i][:, h, :])
                if s == "s0":
                    each(X, lambda h: col(h).broadcast_to([P, P]), lambda h: lower)
                    last = each(Y, kT, kT)
                elif s == "s1":
                    for h in range(n):
                        last = pe.transpose(X[:, h, :], w[1][:, h, :], ident)
                    if t != "meta":
                        last = each(Z, kT, qT)
                elif s == "s2":
                    for h in range(n):
                        last = pe.transpose(Y[:, h, :], w[2][:, h, :], ident)
                elif s == "s3":
                    each(X, buf(4), buf(5))
                    last = each(Z, buf(5), buf(4))
                elif s == "s4":
                    each(Y, buf(0), buf(6))
                    each(X, buf(2), buf(0))
                    last = each(Z, buf(0), buf(2))
                elif s == "s5":
                    each(Y, buf(4), buf(6))
                    last = each(X, buf(5), buf(4))
                elif s == "s6":
                    last = each(Z, buf(2), buf(6))
                elif s == "s7":
                    for h in range(n):
                        pe.transpose(X[:, h, :], w[6][:, h, :], ident)
                    for h in range(n):
                        last = pe.transpose(Y[:, h, :], kT(h), ident)
                    if t == "meta":
                        last = pe.transpose(Z[:, 0, :], vT(0), ident)
                elif s in ("x1", "x2", "x3"):
                    last = each(Z, buf(4), buf(6))
                elif s in ("t1", "t2", "t3"):
                    last = each(X, buf(5), buf(0))
                    if s != "t3":
                        last = each(Z, buf(0), buf(5))
                elif s == "w":
                    if t == "meta":
                        last = pe.matmul(Z[:, 0, :], w[0][:, 0, :], w[3][:, 0, :], start=True, stop=True)
                    else:
                        last = each(X, buf(2), buf(0))
                elif s == "m":
                    for half in range(2):
                        last = pe.matmul(bank[2 + half][:, :], w[7][:, 0, :], um[:, 4 * half:4 * half + 4, :],
                                         start=True, stop=True)
                elif s == "v":
                    for h in range(n):
                        pe.matmul(Z[:, h, :], w[0][:, h, :], w[4][:, h, :], start=True, stop=False)
                        last = pe.matmul(Z[:, h, :], w[6][:, h, :], S[:, 4 * c + h, :], start=False, stop=True)
                elif s == "o":
                    for h in range(n):
                        pe.matmul(Y[:, h, :], S[:, 4 * c + h, :], qT(h), start=True, stop=False)
                        last = pe.matmul(Y[:, h, :], w[5][:, h, :], w[3][:, h, :], start=False, stop=True)
                    if t < TT - 1:
                        last = each(X, buf(7), buf(5))
                elif s == "q":
                    last = pe.matmul(Z, ones, w[6], start=True, stop=True)
                last.then_inc(dn_pe[c], 1)

            for what, arg in MIX_ORDER:
                if what == "tile":
                    tile(arg)
                else:
                    if arg == (0, 1, "s0"):
                        wait_step(pe, "dve", ("meta", 0, "m"))
                        wait_step(pe, "act", ("meta", 0, "m"))
                    dn(*arg)
            for n in range(FIRST["yd"], len(TILES)):
                tile(n)

            for t in range(TT):
                pe.wait_ge(u2_ready, t + 1)
                for c in range(NC):
                    last = pe.transpose(bank[2 + 2 * t + c // 4][:, (c % 4) * P:(c % 4 + 1) * P], u2[:, t, c * P:(c + 1) * P], ident)
                last.then_inc(u2T_ps, 1)
            pe.wait_ge(norms_in, 16 * 6)
            for t in range(TT):
                pe.wait_ge(u2T_ready, t + 1)
                for c in range(NC):
                    last = pe.matmul(bank[6][:, 64 * t:64 * t + 36], u2T[:, c, t * P:(t + 1) * P], r_w[:, c, :],
                                     start=(c == 0), stop=(c == NC - 1))
            last.then_inc(logits_ready, 1)
            wait_tile_out(pe, len(TILES) - 1)
            for t in range(TT):
                for half in range(2):
                    last = pe.matmul(bank[2 * t + half][:, :], ident, h_tok[:, t, half * 512:(half + 1) * 512],
                                     start=True, stop=False, skip_group_check=True)
            last.then_inc(gathered, 1)
            pe.wait_ge(assigned, 1)
            pe.matmul(bank[7][:, 0:32], strict, asg[:, 0, :], start=True, stop=True)
            pe.matmul(bank[7][:, 32:64], ones, asg[:, 0, :], start=True, stop=False)
            pe.matmul(bank[7][:, 32:64], strict, asg[:, 1, :], start=False, stop=True).then_inc(ranked, 1)
            pe.wait_ge(routed, 1)
            pe.matmul(bank[7][:, 64:65], ones, ovcnt[:, 0:1], start=True, stop=True).then_inc(ov_sum, 1)
            pe.wait_ge(ov_flag, 1)

            with pe.Fori(0, N_BATCH) as b:
                pe.wait_ge(picked, b + 1)
                for c in range(NC):
                    for t in range(TT):
                        last = pe.matmul(bank[6 + c // 4][:, (c % 4) * P:(c % 4 + 1) * P], u2[:, t, c * P:(c + 1) * P],
                                         pick[:, t].rearrange("p e s -> p (e s)"), start=(t == 0), stop=(t == TT - 1))
                    if c % 4 == 3:
                        last.then_inc(gathered, 1)
                for t in range(TT):
                    last = pe.transpose(bank[5][:, t * P:(t + 1) * P], pickw[:, t].rearrange("p e s -> p (e s)"), ident)
                last.then_inc(gathered, 1)
                for c in range(NC):
                    pe.wait_ge(xg_a if c < 4 else xg_d, b + 1)
                    pe.wait_ge(slot_in[c], b * 32 + 16 * (N_UNITS // TSLOTS if c < TSLOTS else 0) + 32)
                    for e in range(EPB):
                        last = pe.matmul(bank[4][CAP * e:CAP * (e + 1), :], xg[:, c, CAP * e:CAP * (e + 1)],
                                         ring_gu(c)[:, e].rearrange("p m f -> p (m f)"), start=(c == 0), stop=(c == NC - 1),
                                         tile_position=(0, CAP * e))
                    last.then_inc(slot_used, 1)
                pe.wait_ge(hid_ready, b + 1)
                for fc in range(2):
                    last = pe.transpose(bank[5][:, (2 + fc) * P:(3 + fc) * P], hid[:, fc * P:(fc + 1) * P], ident)
                last.then_inc(hidT_ps, 1)
                pe.wait_ge(hidT_ready, b + 1)
                for half in range(2):
                    for fc in range(2):
                        s = NC + 2 * half + fc
                        pe.wait_ge(slot_in[s], b * 16 + 16)
                        for e in range(EPB):
                            last = pe.matmul(bank[6 + half][CAP * e:CAP * (e + 1), :], hidT[:, fc, CAP * e:CAP * (e + 1)],
                                             ring_down(half, fc)[:, e, :], start=(fc == 0), stop=(fc == 1),
                                             tile_position=(0, CAP * e))
                        last.then_inc(slot_used, 1)
                for half in range(2):
                    pe.wait_ge(down_a if half == 0 else down_d, b + 1)
                    for t in range(TT):
                        last = pe.matmul(bank[2 * t + half][:, :], pickT[:, t, :], dsb[:, half * 512:(half + 1) * 512],
                                         start=False, stop=False, skip_group_check=True)
                last.then_inc(combined, 1)

            beyond = pe.value_load(ovi[0:1, 0:1], min_val=0, max_val=2 * SEQ)
            with pe.If(beyond > 0):
                for s in (f_y, f_hT, f_sum):
                    pe.sem_inc(s, 1)
                with pe.Fori(0, N_EXPERTS) as e:
                    pe.wait_ge(f_in, e * 48 + 48)
                    for fc in range(2):
                        pe.wait_ge(f_hT, e * 2 + fc + 1)
                        for k in range(2):
                            for c in range(NC):
                                last = pe.matmul(bank[4][:, k * SEQ:(k + 1) * SEQ], unit(k)[:, c, fc * P:(fc + 1) * P], u2T[:, c, :],
                                                 start=(c == 0), stop=(c == NC - 1))
                        last.then_inc(f_h, 1)
                    pe.wait_ge(f_hT, e * 2 + 3)
                    for t in range(TT):
                        for half in range(2):
                            k = 2 * t + half
                            for fc in range(2):
                                last = pe.matmul(bank[5][:, :], fhT[:, fc, t * P:(t + 1) * P], f_down[:, fc, half * 512:(half + 1) * 512],
                                                 start=(fc == 0), stop=(fc == 1))
                            last.then_inc(f_y, 1)
                            pe.wait_ge(f_acc, e * 4 + k + 1)
                            last = pe.matmul(bank[k][:, :], ident, dsb[:, 0:512], start=False, stop=False, skip_group_check=True)
                            last.then_inc(f_sum, 1)

        @block.scalar
        def _(act):
            row = lambda v, n: v.rearrange("a n -> (a n)").unsqueeze(0).broadcast_to([P, n])
            act.dma_start(vec_rows[V_NORM1:V_NORM1 + 8, :], norm1_w[0].rearrange("(c p) -> c p", p=P)).then_inc(vec_in, 16)
            act.dma_start(vec_rows[V_SUBLN:V_SUBLN + 1, :], da_subln_w).then_inc(vec_in, 16)
            act.dma_start(vec_rows[V_DNW:V_DNW + 1, :], dn_norm_w).then_inc(vec_in, 16)
            act.dma_start(vec_rows[V_CONV:N_VEC, :], dn_conv_w[0].rearrange("k (c p) -> (k c) p", p=P)).then_inc(vec_in, 16)
            act.dma_start(w_ba, w_in_v[:, :, BA_COL:BA_COL + 16]).then_inc(wba_in, 16)
            for i, v in enumerate((lambda_q1, lambda_k1, lambda_q2, lambda_k2)):
                act.dma_start(lam_in[:, i, :], row(v, 64)).then_inc(small_in, 16)
            for t in range(TT):
                act.dma_start(dtb[:, t * H:(t + 1) * H], row(dn_dt_bias, H)).then_inc(small_in, 16)
                act.dma_start(eA[:, t * H:(t + 1) * H], row(dn_A_log, H)).then_inc(small_in, 16)
            act.preload_act_table_set("natural_log_exp_and_others")
            n_step = [0]

            def link(ins):
                n_step[0] += 1
                ins.then_inc(act_step, 1)
                act.wait_ge(act_step, n_step[0])

            act.wait_ge(x_in, 16 * 3)
            act.wait_ge(const_ready, 1)
            squares = at(zone, 3, D)
            for t in range(3):
                rows = P if t < TT else META
                act.activation(squares[0:rows, t, :], xin[0:rows, t, :], ACT.Square, accum_out=ssq[0:rows, t:t + 1]).then_inc(ssq_ready, 1)
            for t in range(3):
                rows = P if t < TT else META
                act.wait_ge(var_ready, t + 1)
                link(act.activation(rstd[0:rows, t:t + 1], ssq[0:rows, t:t + 1], ACT.Ln))
                act.activation(rstd[0:rows, t:t + 1], rstd[0:rows, t:t + 1], ACT.Exp, scale=-0.5).then_inc(rstd_ready, 1)

            def decay_logs():
                act.wait_ge(ba_logits, 1)
                act.activation(beta, blog, ACT.Exp, scale=-1.0)
                act.activation(eA, eA, ACT.Exp)
                link(act.activation(sp, tmp17, ACT.Exp, scale=-1.0))
                act.activation(sp, sp, ACT.Ln, bias=c_one).then_inc(g_exp, 1)

            def decay_exps():
                act.wait_ge(gc_copied, 2)
                act.activation(egc, gc2[:, 0, :], ACT.Exp)
                act.activation(egt, gc2[:, 1, :], ACT.Exp)
                act.activation(kdec, kdec, ACT.Exp).then_inc(gate_cols, 1)

            def tile_out(n):
                kind, j = TILES[n]
                if kind in BY_DVE:
                    return
                act.wait_ge(tile_ready, n + 1)
                ps = bank[n % 2]
                if kind == "ak":
                    if j == 0:
                        act.wait_ge(uT_ready, 3)
                    last = act.activation(akT[:, j, :], ps[:, 0:L], ACT.Copy)
                elif kind == "av":
                    if j >= 2:
                        act.wait_ge(tr_ready, j - 1)
                    last = act.activation(vtmp[:, j % 2, :], ps[:, 0:L], ACT.Copy)
                elif kind == "aq":
                    last = act.activation(aqT[:, j, :], ps[:, 0:SEQ], ACT.Copy)
                elif kind in ("dq", "dk", "dv"):
                    c = n - FIRST["dq"]
                    if c >= 2:
                        act.wait_ge(conv_ready, c - 1)
                    last = act.activation(cbuf[:, c % 2, CONV - 1:], ps[:, 0:L], ACT.Copy)
                else:
                    k = n - FIRST["gate"] if kind in ("gate", "ga") else n - FIRST["gb"] + 16
                    if k >= 2:
                        act.wait_ge(gate_ready, k - 1)
                    if kind == "gate":
                        act.activation(gx[:, k % 2, :], ps[:, 0:SEQ], ACT.Copy, scale=0.5)
                    last = act.activation(gs[:, k % 2, :], ps[:, 0:SEQ], ACT.Tanh, scale=0.5)
                last.then_inc(tile_copied, 1)

            def tr_out(key):
                act.wait_ge(tr_ready, TR_NO[key] + 1)
                kind, i = key
                ps = bank[4][:, :].rearrange("p (k e) -> p k e", e=P)
                if kind == "v":
                    act.activation(v_meta[0:META, i, :], ps[0:META, 0, :], ACT.Copy)
                    last = act.activation(v_tok[:, :, i, :], ps[:, 1:3, :], ACT.Copy)
                elif kind == "dv":
                    last = act.activation(dv_tok[:, :, i, :], ps[:, 1:3, :], ACT.Copy)
                else:
                    h, t = divmod(i, TT)
                    if i >= 2:
                        act.wait_ge(o_ready, i - 1)
                    act.activation(wT[0:META, i % 2, 0, :], ps[0:META, 0, :], ACT.Copy)
                    last = act.activation(wT[:, i % 2, 1:2 + t, :], ps[:, 1:2 + t, :], ACT.Copy)
                last.then_inc(tr_copied, 1)

            for q in range(AHEAD):
                split_high(q)
            act.wait_ge(uT_ready, 3)
            act.activation(uT_hi, uT, ACT.Copy).then_inc(u_hi, 1)
            for n in range(FIRST["dq"]):
                for q in splits_at(n):
                    split_high(q)
                tile_out(n)
                if FIRST["av"] + 1 <= n <= FIRST["aq"]:
                    tr_out(("v", n - 1 - FIRST["av"]))
                if n == 2:
                    act.wait_ge(lam_dot, 1)
                    act.activation(lam[:, 2:4], lam[:, 0:2], ACT.Exp).then_inc(lam_exp, 1)
                if n == 8:
                    decay_logs()
                if n == FIRST["aq"] + 4:
                    decay_exps()

            def att_exp(i):
                h, t = divmod(i, TT)
                nk = META + (t + 1) * P
                act.wait_ge(nmax_ready, i + 1)
                for m in range(2):
                    last = act.activation(prob[:, i % 2, m, 0:nk], prob[:, i % 2, m, 0:nk], ACT.Exp, scale=SCALE,
                                          bias=nmax[:, i % 2, m:m + 1], accum_out=rsum[:, i % 2, m:m + 1])
                last.then_inc(exp_ready, 1)

            def att_sq(h):
                act.wait_ge(o_ready, 2 * h + 2)
                act.wait_ge(o_copied, h + 1)
                if h:
                    act.wait_ge(oss_ready, h)
                act.activation(osq, bank[5 + h % 2][:, 0:SEQ], ACT.Square).then_inc(osq_ready, 1)

            def conv_sig(c):
                act.wait_ge(conv_ready, c + 1)
                if c >= 2:
                    act.wait_ge(silu_ready, c - 1)
                act.activation(sg[:, c % 2, :], acc[:, c % NACC, :], ACT.Tanh).then_inc(csig, 1)

            def conv_sq(c):
                act.wait_ge(silu_ready, c + 1)
                if c >= 2:
                    act.wait_ge(css_ready, c - 1)
                act.activation(csq[:, c % 2, :], (dqT if c < H else dkT)[:, c % H, :], ACT.Square).then_inc(csq_ready, 1)

            def roots():
                act.wait_ge(css_ready, 16)
                act.wait_ge(oss_ready, H)
                link(act.activation(rs_rows[0:NSS, :], bank[7][0:NSS, 0:L], ACT.Ln, bias=c_mean_eps[0:NSS, :]))
                act.activation(rs_rows[0:NSS, :], rs_rows[0:NSS, :], ACT.Exp, scale=-0.5, bias=c_rs[0:NSS, :]).then_inc(rs_ready, 1)

            for m in range(SLOTS_A):
                tile_out(FIRST["dq"] + m)
                if 1 <= m <= 24:
                    conv_sig(m - 1)
                if 2 <= m < 16 + 2:
                    conv_sq(m - 2)
                if 18 <= m < 26:
                    act.wait_ge(silu_ready, m - 2 + 1)
                    act.activation(dvT_meta[:, m - 18, :], acc[:, (m - 2) % NACC, 0:META], ACT.Copy)
                if 2 <= m < ATT_UNITS + 2:
                    tr_out(("w", m - 2))
                if 18 <= m < 26:
                    tr_out(("dv", m - 18))
                for q in splits_at(FIRST["dq"] + m):
                    split_high(q)
                if m < ATT_UNITS:
                    att_exp(m)
                if 4 <= m < ATT_UNITS + 4 and m % 2 == 0:
                    att_sq((m - 4) // 2)
                if m == 20:
                    roots()

            def dn(t, c, s):
                if not works("act", (t, c, s)):
                    return
                w = work[c]
                X, Y, Z = (bank[2 + 3 * c + i][:, :].rearrange("p (h i) -> p h i", h=4) for i in range(3))
                n = 1 if t == "meta" else 4
                wait_step(act, "pe", (t, c, s))
                if s == "s0":
                    act.wait_ge(dec_masked[c], {"meta": 1, 0: 2 - c, 1: 3 - c}[t])
                    if t != "meta":
                        act.activation(w[7][:, 0:n, :], X[:, 0:n, :], ACT.Exp)
                    for h in range(n):
                        k = 2 * H if t == "meta" else t * H + 4 * c + h
                        last = act.activation(w[0][:, h, :], w[0][:, h, :], ACT.Exp, bias=ngc[:, k:k + 1])
                elif s == "s2":
                    last = act.activation(w[1][:, 0:n, :], Y[:, 0:n, :], ACT.Copy)
                elif s == "s3":
                    last = act.activation(w[0][:, 0:n, :], X[:, 0:n, :], ACT.Copy)
                elif s == "s4":
                    last = act.activation(w[4][:, 0:n, :], X[:, 0:n, :], ACT.Copy)
                elif s == "s5":
                    last = act.activation(w[2][:, 0:n, :], X[:, 0:n, :], ACT.Copy)
                elif s == "s7":
                    last = act.activation(w[0][:, 0:n, :], X[:, 0:n, :], ACT.Copy)
                elif s in ("x1", "x2", "x3"):
                    last = act.activation(w[5][:, 0:n, :], Z[:, 0:n, :], ACT.Copy)
                elif s == "w" and t != "meta":
                    last = act.activation(w[6][:, 0:n, :], X[:, 0:n, :], ACT.Copy, scale=-1.0)
                elif s == "v":
                    last = act.activation(w[5][:, 0:n, :], Z[:, 0:n, :], ACT.Copy)
                elif s == "m":
                    last = act.activation(S[:, 0:4, :], X, ACT.Copy)
                elif s == "o":
                    last = act.activation(w[6][:, 0:n, :], Y[:, 0:n, :], ACT.Square)
                elif s == "q":
                    link(act.activation(w[7][:, 0:n, :], Z[:, 0:n, :], ACT.Ln, scale=1.0 / P, bias=c_eps))
                    last = act.activation(w[7][:, 0:n, :], w[7][:, 0:n, :], ACT.Exp, scale=-0.5)
                last.then_inc(dn_act[c], 1)

            act.wait_ge(qk_ready, NSS)
            for what, arg in BEHIND:
                if what == "split":
                    for q in splits_at(arg):
                        split_high(q)
                elif what == "tile":
                    tile_out(arg)
                elif what == "result":
                    wait_step(act, "pool", (TT - 1, arg, "q"))
                    for part in RESULTS[arg]:
                        last = act.activation(yd_hi[part], gateT[part], ACT.Copy)
                    last.then_inc(yd_hi_ready, 1)
                else:
                    dn(*arg)

            for n in range(FIRST["yd"], len(TILES)):
                for q in splits_at(n):
                    split_high(q)
            act.dma_start(norm2_b, row(norm2_w, D)).then_inc(norms_in, 16)
            act.dma_start(fnorm_b, final_norm_w.unsqueeze(0).broadcast_to([P, D])).then_inc(norms_in, 16)
            act.dma_start(r_w[:, :, 0:4], router_group_w[0].rearrange("(c p) n -> p c n", p=P)).then_inc(norms_in, 16)
            act.dma_start(r_w[:, :, 4:36], router_expert_w[0].rearrange("(c p) n -> p c n", p=P)).then_inc(norms_in, 16)
            act.dma_start(r_b[:, 0:4], row(router_group_b, 4)).then_inc(norms_in, 16)
            act.dma_start(r_b[:, 4:36], row(router_expert_b, 32)).then_inc(norms_in, 16)

            def root(into, ready, src, k):
                link(act.activation(into[:, k:k + 1], src[:, k:k + 1], ACT.Ln))
                act.activation(into[:, k:k + 1], into[:, k:k + 1], ACT.Exp, scale=-0.5).then_inc(ready, 1)

            act.wait_ge(norms_in, 16 * 6)
            for t in range(TT):
                act.wait_ge(mixed, 24)
                if t:
                    act.wait_ge(ssq2_ready, t)
                act.activation(junk, h_tok[:, t, :], ACT.Square, accum_out=ssq[:, t:t + 1]).then_inc(ssq2_ready, 1)
            for t in range(TT):
                act.wait_ge(var2_ready, t + 1)
                root(rstd, rstd2_ready, ssq, t)
            for t in range(TT):
                act.wait_ge(u2T_ps, t + 1)
                for k in range(2):
                    last = act.activation(u2T[:, 4 * k:4 * k + 4, t * P:(t + 1) * P],
                                          bank[2 + 2 * t + k][:, :].rearrange("p (c i) -> p c i", i=P), ACT.Copy)
                last.then_inc(u2T_ready, 1)
            act.wait_ge(r_exp_in, 1)
            act.activation(gd, gd, ACT.Exp).then_inc(r_exp, 1)
            act.wait_ge(r_exp_in, 2)
            act.activation(sc[:, 4, :], sc[:, 4, :], ACT.Exp).then_inc(r_exp, 1)

            with act.Fori(0, N_BATCH) as b:
                act.wait_ge(gathered, b * 3 + 2)
                act.activation(xg[:, 0:4, :], bank[6][:, :].rearrange("p (c i) -> p c i", i=P), ACT.Copy).then_inc(xg_a, 1)
                act.wait_ge(slot_used, b * SLOTS + NC)
                act.activation(sil, bank[4][:, 0:D_EXPERT], ACT.Tanh, scale=0.5).then_inc(g_sig, 1)
                act.wait_ge(slot_used, b * SLOTS + NC + 2)
                act.activation(dsb[:, 0:512], bank[6][:, :], ACT.Copy).then_inc(down_a, 1)

            beyond = act.value_load(ovi[0:1, 0:1], min_val=0, max_val=2 * SEQ)
            with act.If(beyond > 0):
                with act.Fori(0, N_EXPERTS) as e:
                    for fc in range(2):
                        act.wait_ge(f_h, e * 2 + fc + 1)
                        act.activation(ftmp, bank[4][:, 0:SEQ], ACT.Tanh, scale=0.5).then_inc(f_sig, 1)
                act.wait_ge(f_sum, N_EXPERTS * 4 + 1)

            act.wait_ge(combined, N_BATCH)
            for t in range(TT):
                if t:
                    act.wait_ge(ssq3_ready, t)
                for half in range(2):
                    last = act.activation(junk[:, half * 512:(half + 1) * 512], bank[2 * t + half][:, :], ACT.Square,
                                          accum_out=sc[:, 8 + half, t:t + 1])
                last.then_inc(ssq3_ready, 1)
            for t in range(TT):
                act.wait_ge(var3_ready, t + 1)
                root(rstd, rstd3_ready, ssq, t)

        @block.vector
        def _(dve):
            n_step = [0]

            def link(ins):
                n_step[0] += 1
                ins.then_inc(dve_step, 1)
                dve.wait_ge(dve_step, n_step[0])

            tt, ts, stt = dve.tensor_tensor, dve.tensor_scalar, dve.scalar_tensor_tensor

            dve.wait_ge(vec_T, 1)
            dve.tensor_copy(vec[:, 0:V_CONV], bank[0][:, 0:V_CONV])
            ts(vec[:, V_CONV:N_VEC], bank[0][:, V_CONV:N_VEC], 0.5, None, ALU.mult).then_inc(vec_ready, 1)
            for t in range(3):
                rows = P if t < TT else META
                dve.wait_ge(ssq_ready, t + 1)
                ts(ssq[0:rows, t:t + 1], ssq[0:rows, t:t + 1], 1.0 / D, EPS, ALU.mult, ALU.add).then_inc(var_ready, 1)
            for t in range(3):
                rows = P if t < TT else META
                dve.wait_ge(rstd_ready, t + 1)
                ts(xin[0:rows, t, :], xin[0:rows, t, :], rstd[0:rows, t:t + 1], None, ALU.mult).then_inc(xn_ready, 1)
            dve.wait_ge(vec_ready, 1)
            for t in range(3):
                rows, c0 = (P, META + t * P) if t < TT else (META, 0)
                dve.wait_ge(xT_ready, t + 1)
                for k in range(2):
                    ps = bank[2 + 2 * t + k][:, :].rearrange("p (c i) -> p c i", i=P)[:, :, 0:rows]
                    last = tt(uT[:, 4 * k:4 * k + 4, c0:c0 + rows], ps,
                              vec[:, V_NORM1 + 4 * k:V_NORM1 + 4 * k + 4].unsqueeze(2).broadcast_to([P, 4, rows]), ALU.mult)
                last.then_inc(uT_ready, 1)

            dve.wait_ge(uT_ready, 3)
            dve.wait_ge(u_hi, 1)
            tt(uT_lo, uT, uT_hi.bitcast(F32), ALU.subtract).then_inc(u_lo, 1)
            for q in range(AHEAD):
                split_low(dve, q)

            own = slice(2 * H, NCOL)
            minus_lambda = lam[:, 5:6]

            def lambda_dots():
                dve.wait_ge(small_in, 16 * 8)
                dve.wait_ge(const_ready, 1)
                for v in (dtb, eA):
                    link(dve.tensor_tensor_reduce(tmp17[:, 0:H], v[:, 0:H], own_head, 1.0, 0.0, ALU.mult, ALU.add, v[:, own]))
                dve.tensor_tensor_reduce(lam_in[:, 0, :], lam_in[:, 0, :], lam_in[:, 1, :], 1.0, 0.0, ALU.mult, ALU.add, lam[:, 0:1])
                dve.tensor_tensor_reduce(lam_in[:, 2, :], lam_in[:, 2, :], lam_in[:, 3, :], 1.0, 0.0, ALU.mult, ALU.add, lam[:, 1:2]).then_inc(lam_dot, 1)

            def logits_out():
                dve.wait_ge(ba_ready, 1)
                dve.tensor_copy(ba_meta[0:META, :], bank[2][0:META, 32:48]).then_inc(ba_meta_ready, 1)
                ba = bank[2][:, 0:32].rearrange("p (t k) -> p t k", t=TT)
                dve.tensor_copy(blog[:, 0:16].rearrange("p (t h) -> p t h", t=TT), ba[:, :, 0:H])
                dve.tensor_copy(alog[:, 0:16].rearrange("p (t h) -> p t h", t=TT), ba[:, :, H:16])

            def logits_of_meta():
                dve.wait_ge(ba_spread, 1)
                link(dve.tensor_tensor_reduce(tmp17[:, 0:H], bank[3][:, 0:H], own_head, 1.0, 0.0, ALU.mult, ALU.add, blog[:, own]))
                link(dve.tensor_tensor_reduce(tmp17[:, 0:H], bank[3][:, H:16], own_head, 1.0, 0.0, ALU.mult, ALU.add, alog[:, own]))
                link(tt(alog, alog, dtb, ALU.add))
                stt(tmp17, alog, -1.0, alog, ALU.mult, ALU.max).then_inc(ba_logits, 1)
                dve.wait_ge(lam_exp, 1)
                link(stt(lam[:, 4:5], lam[:, 2:3], -1.0, lam[:, 3:4], ALU.mult, ALU.add))
                link(ts(lam[:, 5:6], lam[:, 4:5], -LAMBDA_INIT, None, ALU.add))

            def decays():
                dve.wait_ge(g_exp, 1)
                link(ts(beta, beta, 1.0, None, ALU.add))
                link(dve.reciprocal(beta, beta))
                ts(nbeta, beta, -1.0, None, ALU.mult)
                link(stt(sp, alog, 0.0, sp, ALU.max, ALU.add))
                stt(g, sp, -1.0, eA, ALU.mult, ALU.mult).then_inc(g_ready, 1)

            def decay_sums():
                dve.wait_ge(gc_ready, 1)
                dve.tensor_copy(gc2.rearrange("p a b -> p (a b)"), bank[5][:, 0:2 * NCOL]).then_inc(gc_copied, 1)
                dve.wait_ge(gc_copied, 1)
                ts(ngc, gc2[:, 0, :], -1.0, None, ALU.mult)
                tt(kdec, gc2[:, 1, :], gc2[:, 0, :], ALU.subtract).then_inc(gc_copied, 1)

            def decay_products():
                dve.wait_ge(gate_cols, 1)
                tt(begc, beta, egc, ALU.mult).then_inc(gate_cols, 1)

            def split_lows(n):
                for q in splits_at(n):
                    if not low_by_pool(q):
                        split_low(dve, q)

            for n in range(FIRST["dq"]):
                split_lows(n)
                if n == 1:
                    lambda_dots()
                if n == 2:
                    logits_out()
                if n == 4:
                    logits_of_meta()
                if n == 9:
                    decays()
                if n == FIRST["aq"] + 2:
                    decay_sums()
                if n == FIRST["aq"] + 6:
                    decay_products()

            def conv(c):
                wait_tile_out(dve, FIRST["dq"] + c)
                if c >= NACC + 16:
                    dve.wait_ge(tr_copied, TR_NO[("dv", c - NACC - 16)] + 1)
                elif c >= NACC:
                    dve.wait_ge(silu_ready, c - NACC + 1)
                a, x_ = acc[:, c % NACC, :], cbuf[:, c % 2, :]
                tap = lambda k: vec[:, V_CONV + k * 3 * H + c:V_CONV + k * 3 * H + c + 1]
                link(ts(a, x_[:, 0:L], tap(0), None, ALU.mult))
                for k in range(1, CONV):
                    last = stt(a, x_[:, k:k + L], tap(k), a, ALU.mult, ALU.add)
                    if k < CONV - 1:
                        link(last)
                last.then_inc(conv_ready, 1)

            def silu(c):
                dve.wait_ge(csig, c + 1)
                s_ = sg[:, c % 2, :]
                a = acc[:, c % NACC, :]
                if c == 0:
                    dve.wait_ge(xT_ready, 3)
                dst = dqT[:, c, :] if c < H else dkT[:, c - H, :] if c < 2 * H else a
                stt(dst, s_, 1.0, a, ALU.add, ALU.mult).then_inc(silu_ready, 1)

            def scale_by(i):
                k = SPREAD.index(i)
                dve.wait_ge(spread_ready, k + 1)
                ps = bank[SPREAD_BANKS[k % 4]]
                h = i % H
                if i >= 2 * H:
                    last = stt(yaT[:, h, :], yaT[:, h, :], vec[:, V_SUBLN:V_SUBLN + 1], ps[:, 0:SEQ], ALU.mult, ALU.mult)
                else:
                    dst = (dqT if i < H else dkT)[:, h, :]
                    if i >= H:
                        tt(dkT_meta[:, h, :], dst[:, 0:META], ps[:, 0:META], ALU.mult)
                    last = tt(dst[:, META:L], dst[:, META:L], ps[:, META:L], ALU.mult)
                last.then_inc(qk_ready, 1)

            def att_bias(i):
                h, t = divmod(i, TT)
                nk = META + (t + 1) * P
                dve.wait_ge(scores_ready, i + 1)
                dve.wait_ge(qz_ready, i + 1)
                if i >= 2:
                    dve.wait_ge(tr_ready, TR_NO[("w", i - 2)] + 1)
                for m in range(2):
                    last = dve.tensor_tensor_reduce(prob[:, i % 2, m, 0:nk], bank[2 + m][:, 0:nk], bias[:, i % NPREP, 0:nk], 1.0, -3e38,
                                                    ALU.add, ALU.max, mx[:, i % 2, m:m + 1])
                last.then_inc(biased, 1)
                dve.wait_ge(biased, i + 1)
                ts(nmax[:, i % 2, :], mx[:, i % 2, :], -SCALE, None, ALU.mult).then_inc(nmax_ready, 1)

            def att_w(i):
                h, t = divmod(i, TT)
                nk = META + (t + 1) * P
                dve.wait_ge(exp_ready, i + 1)
                r = rinv[:, i % 2, :]
                link(dve.reciprocal(r, rsum[:, i % 2, :]))
                link(ts(r[:, 1:2], r[:, 1:2], minus_lambda, None, ALU.mult))
                a, b = prob[:, i % 2, 0, 0:nk], prob[:, i % 2, 1, 0:nk]
                link(ts(b, b, r[:, 1:2], None, ALU.mult))
                stt(a, a, r[:, 0:1], b, ALU.mult, ALU.add).then_inc(w_ready, 1)

            def tile_out(n):
                kind, j = TILES[n]
                ps = bank[n % 2][:, 0:SEQ]
                if kind in ("gate", "ga", "gb"):
                    k = n - FIRST["gate"] if kind in ("gate", "ga") else n - FIRST["gb"] + 16
                    wait_tile_out(dve, n)
                    s_ = gs[:, k % 2, :]
                    if kind == "gate":
                        last = stt(gateT[:, j, :], s_, 1.0, gx[:, k % 2, :], ALU.add, ALU.mult)
                    else:
                        last = ts({"ga": gaT, "gb": gbT}[kind][:, j, :], s_, 1.0, 0.5, ALU.add, ALU.mult)
                    last.then_inc(gate_ready, 1)
                    return
                dve.wait_ge(tile_ready, n + 1)
                if kind == "ya":
                    last = tt(gaT[:, j, :], ps, gaT[:, j, :], ALU.mult)
                elif kind == "yd":
                    link(tt(gbT[:, j, :], ps, gbT[:, j, :], ALU.mult))
                    last = tt(mixT[:, j, :], gaT[:, j, :], gbT[:, j, :], ALU.add)
                else:
                    if j == 0:
                        dve.wait_ge(h_in, 16 * TT)
                    piece = h_tok[:, j % 2, (j // 2) * 256:(j // 2 + 1) * 256]
                    last = tt(piece, ps, piece, ALU.add)
                last.then_inc(mixed, 1)

            def att_keep(h):
                dve.wait_ge(o_ready, 2 * h + 2)
                dve.tensor_copy(yaT[:, h, :], bank[5 + h % 2][:, 0:SEQ]).then_inc(o_copied, 1)

            for m in range(SLOTS_A):
                if 1 <= m < ATT_UNITS + 1:
                    att_w(m - 1)
                if m < ATT_UNITS:
                    att_bias(m)
                if m < 24:
                    conv(m)
                if 1 <= m <= 24:
                    silu(m - 1)
                split_lows(FIRST["dq"] + m)
                if 4 <= m < ATT_UNITS + 4 and m % 2 == 0:
                    att_keep((m - 4) // 2)
                for i in spread_at(m):
                    scale_by(i)
                if m >= 24:
                    tile_out(FIRST["dq"] + m)

            def dn(t, c, s):
                if not works("dve", (t, c, s)):
                    return
                w = work[c]
                X, Y, Z = (bank[2 + 3 * c + i][:, :].rearrange("p (h i) -> p h i", h=4)[:, 0:1 if t == "meta" else 4, :] for i in range(3))
                n = 1 if t == "meta" else 4
                k0 = 2 * H if t == "meta" else t * H + 4 * c
                hs = slice(4 * c, 4 * c + 4)
                per_head = lambda v: v[:, k0:k0 + n].unsqueeze(2).broadcast_to([P, n, P])
                wait_step(dve, "pe", (t, c, s))
                b = lambda i: w[i][:, 0:n, :]
                if s == "s0":
                    mask = causal_add16 if t == "meta" else causal_add
                    tt(b(0), X, mask.unsqueeze(1).broadcast_to([P, n, P]), ALU.add).then_inc(dec_masked[c], 1)
                    wait_step(dve, "act", (t, c, s))
                    last = tt(b(1), Y, b(0), ALU.mult)
                elif s == "s1":
                    last = tt(b(2), X, per_head(nbeta), ALU.mult)
                    if t != "meta":
                        last = tt(b(3), Z, b(0), ALU.mult)
                elif s == "s3":
                    last = dve.tensor_copy(b(2), Z)
                elif s == "s4":
                    dve.tensor_copy(b(5), Z)
                    last = tt(b(6), Y, b(6), ALU.add)
                elif s == "s5":
                    last = tt(b(6), Y, b(6), ALU.add)
                elif s == "s6":
                    last = tt(b(6), Z, b(6), ALU.add)
                elif s == "s7":
                    last = tt(b(7), Y, per_head(kdec), ALU.mult)
                    if t == "meta":
                        last = tt(b(3), Z, per_head(beta), ALU.mult)
                    else:
                        last = tt(b(2), Y, per_head(begc), ALU.mult)
                elif s in ("t1", "t2", "t3"):
                    last = tt(b(0), X, b(0), ALU.add)
                    if s != "t3":
                        last = tt(b(6), Z, b(6), ALU.add)
                    else:
                        last = tt(b(4), dv_tok[:, t, hs, :], per_head(beta), ALU.mult)
                elif s == "w":
                    last = tt(um, Z[:, 0, :].unsqueeze(1).broadcast_to([P, H, P]),
                              own_head.unsqueeze(2).broadcast_to([P, H, P]), ALU.mult)
                elif s == "m":
                    last = dve.tensor_copy(S[:, 4:8, :], bank[3][:, :].rearrange("p (h i) -> p h i", h=4))
                elif s == "o":
                    for h in range(n):
                        last = stt(S[:, 4 * c + h, :], S[:, 4 * c + h, :], egt[:, k0 + h:k0 + h + 1], X[:, h, :], ALU.mult, ALU.add)
                elif s == "q":
                    wait_step(dve, "act", (t, c, s))
                    flat = lambda a: a.rearrange("p h i -> p (h i)")
                    last = stt(flat(b(7)), flat(Y), vec[:, V_DNW:V_DNW + 1], flat(b(7)), ALU.mult, ALU.mult)
                last.then_inc(dn_dve[c], 1)

            dve.wait_ge(tr_copied, len(TR))
            for what, arg in BEHIND:
                if what == "split":
                    split_lows(arg)
                elif what == "tile":
                    tile_out(arg)
                elif what == "result":
                    wait_step(dve, "pool", (TT - 1, arg, "q"))
                    dve.wait_ge(yd_hi_ready, arg + 1)
                    for part in RESULTS[arg]:
                        last = tt(yd_lo[part], gateT[part], yd_hi[part].bitcast(F32), ALU.subtract)
                    last.then_inc(yd_lo_ready, 1)
                else:
                    dn(*arg)
            for n in range(FIRST["yd"], len(TILES)):
                split_lows(n)
                tile_out(n)

            for t in range(TT):
                dve.wait_ge(ssq2_ready, t + 1)
                ts(ssq[:, t:t + 1], ssq[:, t:t + 1], 1.0 / D, EPS, ALU.mult, ALU.add).then_inc(var2_ready, 1)
            dve.wait_ge(norms_in, 16 * 6)
            for t in range(TT):
                dve.wait_ge(rstd2_ready, t + 1)
                stt(u2[:, t, :], h_tok[:, t, :], rstd[:, t:t + 1], norm2_b, ALU.mult, ALU.mult).then_inc(u2_ready, 1)
            dve.wait_ge(logits_ready, 1)
            wide = lambda v, n: v.unsqueeze(2).broadcast_to([P, TT, n])
            sc_ = lambda i: sc[:, i, :]
            link(tt(lg, bank[6][:, 0:128].rearrange("p (t k) -> p t k", t=TT)[:, :, 0:36],
                    r_b.unsqueeze(1).broadcast_to([P, TT, 36]), ALU.add))
            link(dve.tensor_reduce(sc_(0), lg[:, :, 0:4], AX, ALU.max))
            link(tt(gd, lg[:, :, 0:4], wide(sc_(0), 4), ALU.subtract))

            def first(into, equal, n):
                for t in range(TT):
                    link(dve.tensor_tensor_scan(cum[:, t, 0:n], ones[:, 0:n], equal[:, t, :], 0.0, ALU.mult, ALU.add))
                link(stt(into, cum[:, :, 0:n], 1.0, equal, ALU.is_equal, ALU.mult))

            link(ts(pen, gd, 0.0, None, ALU.is_ge))
            first(gsel, pen, 4)
            link(ts(pen, gsel, -1.0, -NEG, ALU.add, ALU.mult))
            for t in range(TT):
                last = tt(me[:, t, :].rearrange("p (g e) -> p g e", g=4), lg[:, t, 4:36].rearrange("p (g e) -> p g e", g=4),
                          pen[:, t, :].unsqueeze(2).broadcast_to([P, 4, PER_GROUP]), ALU.add)
            last.then_inc(r_exp_in, 1)
            dve.wait_ge(r_exp_in, 1)
            link(dve.tensor_reduce(sc_(1), me, AX, ALU.max))
            link(tt(eq, me, wide(sc_(1), 32), ALU.is_equal))
            first(e1, eq, 32)
            link(stt(me2, e1, 2 * NEG, me, ALU.mult, ALU.add))
            link(dve.tensor_reduce(sc_(2), me2, AX, ALU.max))
            link(tt(eq, me2, wide(sc_(2), 32), ALU.is_equal))
            first(e2, eq, 32)
            tt(asg, e1, e2, ALU.add).then_inc(assigned, 1)
            tt(sc_(4), sc_(2), sc_(1), ALU.subtract).then_inc(r_exp_in, 1)
            dve.wait_ge(r_exp, 1)
            link(dve.tensor_reduce(sc_(5), gd, AX, ALU.add))
            link(dve.reciprocal(sc_(5), sc_(5)))
            dve.wait_ge(r_exp, 2)
            link(ts(sc_(6), sc_(4), 1.0, None, ALU.add))
            link(dve.reciprocal(sc_(6), sc_(6)))
            link(tt(sc_(6), sc_(6), sc_(5), ALU.mult))
            link(tt(sc_(7), sc_(6), sc_(4), ALU.mult))
            link(tt(e1, e1, wide(sc_(6), 32), ALU.mult))
            link(tt(e2, e2, wide(sc_(7), 32), ALU.mult))
            link(tt(comb, e1, e2, ALU.add))
            dve.wait_ge(ranked, 1)
            link(ts(rank, bank[7][:, 0:64].rearrange("p (t k) -> p t k", t=TT), 1.0, None, ALU.add))
            link(tt(rank, rank, asg, ALU.mult))
            link(ts(rank, rank, -1.0, None, ALU.add))
            link(ts(eq, rank, float(CAP), None, ALU.is_ge))
            tt(ovf, eq, comb, ALU.mult)
            link(dve.tensor_reduce(sc_(9), eq, AX, ALU.add))
            tt(ovcnt[:, 0:1], sc[:, 9, 0:1], sc[:, 9, 1:2], ALU.add).then_inc(routed, 1)
            dve.wait_ge(ov_sum, 1)
            dve.tensor_copy(ovi, bank[7][:, 64:65]).then_inc(ov_flag, 1)

            with dve.Fori(0, N_BATCH) as b:
                dve.wait_ge(gathered, b * 3 + 1)
                for t in range(TT):
                    last = tt(pick[:, t], slot_no.unsqueeze(1).broadcast_to([P, EPB, CAP]),
                              rank[:, t, bass.ds(b * EPB, EPB)].unsqueeze(2).broadcast_to([P, EPB, CAP]), ALU.is_equal)
                last.then_inc(pick_made, 1)
                dve.wait_ge(pick_made, b + 1)
                for t in range(TT):
                    last = tt(pickw[:, t], pick[:, t],
                              comb[:, t, bass.ds(b * EPB, EPB)].unsqueeze(2).broadcast_to([P, EPB, CAP]), ALU.mult)
                last.then_inc(picked, 1)
                dve.wait_ge(gathered, b * 3 + 3)
                dve.tensor_copy(xg[:, 4:8, :], bank[7][:, :].rearrange("p (c i) -> p c i", i=P)).then_inc(xg_d, 1)
                dve.wait_ge(gathered, b * 3 + 4)
                dve.tensor_copy(pickT, bank[5][:, 0:2 * P].rearrange("p (t i) -> p t i", t=TT))
                dve.wait_ge(g_sig, b + 1)
                stt(sil, sil, 1.0, bank[4][:, 0:D_EXPERT], ALU.add, ALU.mult).then_inc(hid_step, 1)
                dve.wait_ge(hid_step, b + 1)
                stt(hid, sil, 0.5, bank[4][:, D_EXPERT:2 * D_EXPERT], ALU.mult, ALU.mult).then_inc(hid_ready, 1)
                dve.wait_ge(hidT_ps, b + 1)
                dve.tensor_copy(hidT, bank[5][:, 2 * P:4 * P].rearrange("p (t i) -> p t i", t=2)).then_inc(hidT_ready, 1)
                dve.wait_ge(slot_used, b * SLOTS + SLOTS)
                dve.tensor_copy(dsb[:, 512:D], bank[7][:, :]).then_inc(down_d, 1)

            beyond = dve.value_load(ovi[0:1, 0:1], min_val=0, max_val=2 * SEQ)
            with dve.If(beyond > 0):
                with dve.Fori(0, N_EXPERTS) as e:
                    for fc in range(2):
                        dve.wait_ge(f_sig, e * 2 + fc + 1)
                        stt(ftmp, ftmp, 1.0, bank[4][:, 0:SEQ], ALU.add, ALU.mult).then_inc(f_step, 1)
                        dve.wait_ge(f_step, e * 2 + fc + 1)
                        stt(fhT[:, fc, :], ftmp, 0.5, bank[4][:, SEQ:2 * SEQ], ALU.mult, ALU.mult).then_inc(f_hT, 1)
                    for t in range(TT):
                        for half in range(2):
                            k = 2 * t + half
                            dve.wait_ge(f_y, e * 4 + k + 2)
                            dve.wait_ge(f_sum, e * 4 + k + 1)
                            dve.tensor_scalar(dsb[:, 0:512], bank[5][:, :], ovf[:, t, bass.ds(e, 1)], None, ALU.mult).then_inc(f_acc, 1)
                dve.wait_ge(f_sum, N_EXPERTS * 4 + 1)

            for t in range(TT):
                dve.wait_ge(ssq3_ready, t + 1)
                link(tt(ssq[:, t:t + 1], sc[:, 8, t:t + 1], sc[:, 9, t:t + 1], ALU.add))
                ts(ssq[:, t:t + 1], ssq[:, t:t + 1], 1.0 / D, EPS, ALU.mult, ALU.add).then_inc(var3_ready, 1)
            for t in range(TT):
                dve.wait_ge(rstd3_ready, t + 1)
                for half in range(2):
                    cols = slice(half * 512, (half + 1) * 512)
                    last = stt(result[:, t, cols], bank[2 * t + half][:, :], rstd[:, t:t + 1], fnorm_b[:, cols], ALU.mult, ALU.mult)
                last.then_inc(out_ready, 1)


_INS = ['x', 'meta_tokens', 'norm1_w', 'w_in', 'lambda_q1', 'lambda_k1', 'lambda_q2', 'lambda_k2', 'da_subln_w',
        'dn_conv_w', 'dn_A_log', 'dn_dt_bias', 'dn_norm_w', 'w_branch_attn', 'w_branch_dn', 'w_out', 'norm2_w',
        'router_group_w', 'router_group_b', 'router_expert_w', 'router_expert_b', 'expert_w_gate', 'expert_w_up',
        'expert_w_down', 'final_norm_w']
_OUTS = [((1, SEQ, D), 'float32')]


def kernel(**inputs):
    import numpy as _np
    import concourse.bacc as _bacc
    from concourse import mybir as _mybir
    from concourse.bass_utils import run_bass_kernel_spmd as _run

    nc = _bacc.Bacc("TRN2", target_bir_lowering=False, num_devices=1)
    arrays, args = {}, []
    for name in _INS:
        a = _np.ascontiguousarray(inputs[name])
        arrays[f"in_{name}_dram"] = a
        args.append(nc.dram_tensor(f"in_{name}_dram", a.shape, _mybir.dt.from_np(a.dtype), kind="ExternalInput").ap())
    for i, (shape, dtype) in enumerate(_OUTS):
        dt = _mybir.dt.from_np(_np.dtype(dtype))
        args.append(nc.dram_tensor(f"out_{i}_dram", shape, dt, kind="ExternalOutput").ap())
    hybrid_block(nc, *args)
    r = _run(nc, [arrays], core_ids=[0])
    got = tuple(r.results[0][f"out_{i}_dram"] for i in range(len(_OUTS)))
    return got[0]
```

```python
from contextlib import ExitStack
import math

import concourse.bass as bass
from concourse import mybir

P = 128
D = 1024
NC = D // P
META = 16
SEQ = 256
L = META + SEQ
TT = SEQ // P
H = 8
SCALE = 64 ** -0.5
LAMBDA_INIT = 0.8 - 0.6 * math.exp(-0.3 * 0)
EPS = 1e-6
NEG = -1e30
CONV = 4
PER_GROUP, N_EXPERTS, D_EXPERT = 8, 32, 256
EPB = 4
N_BATCH = N_EXPERTS // EPB
CAP = P // EPB
UNIT = 2048
SLOTS = 12
NEXTRA = 4
NSS = 3 * H

F32 = mybir.dt.float32
F32R = mybir.dt.float32r
I32 = mybir.dt.int32
ALU = mybir.AluOpType
ACT = mybir.ActivationFunctionType
AX = mybir.AxisListType.X

W_COL = dict(aq=0, ak=1024, av=2048, dq=3072, dk=4096, dv=5120, gate=6144, ga=7184, gb=8208)
BA_COL = 7168
KINDS = ["ak", "av", "aq", "dq", "dk", "dv", "gate", "ga", "ya", "gb", "yd", "out"]
TILES = [(kind, j) for kind in KINDS for j in range(8)]
FIRST = {kind: 8 * i for i, kind in enumerate(KINDS)}
SPLIT = [n for n, (kind, _) in enumerate(TILES) if kind not in ("ya", "out")]
AHEAD = 3
NSPLIT = AHEAD + 2
TSLOTS = 6
N_UNITS = len(TILES) // 2
V_NORM1, V_SUBLN, V_DNW, V_NORM2, V_CONV = 0, 8, 9, 10, 18
N_VEC = V_CONV + CONV * 3 * H


def hybrid_block(nc, x, meta_tokens, norm1_w, w_in, lambda_q1, lambda_k1, lambda_q2, lambda_k2, da_subln_w,
                 dn_conv_w, dn_A_log, dn_dt_bias, dn_norm_w, w_branch_attn, w_branch_dn, w_out, norm2_w,
                 router_group_w, router_group_b, router_expert_w, router_expert_b, expert_w_gate,
                 expert_w_up, expert_w_down, final_norm_w, out):
    with ExitStack() as ctx:
        def sem(name):
            return ctx.enter_context(nc.semaphore(name))

        FLOATS = 53100
        base = -(-nc.sbuf_base // 64) * 64
        arena = nc.alloc_sbuf_tensor_at("arena", [P, FLOATS], F32, offset=base)
        bank = [ctx.enter_context(nc.psum_tensor(f"bank{i}", [P, 512], F32)) for i in range(8)]
        top = [0]

        def at(start, *shape):
            n = math.prod(shape)
            ap = arena[:, start:start + n]
            if len(shape) == 2:
                return ap.rearrange("p (a b) -> p a b", b=shape[1])
            if len(shape) == 3:
                return ap.rearrange("p (a b c) -> p a b c", b=shape[1], c=shape[2])
            return ap

        def rounded(name, start, a, b, kind=F32R):
            t = nc.alloc_sbuf_tensor_at(name, [P, a * b], kind, offset=base + 4 * start)
            return t[:, :].rearrange("p (a b) -> p a b", b=b)

        def new(*shape):
            start = top[0]
            top[0] += math.prod(shape)
            assert top[0] <= FLOATS, top[0]
            return at(start, *shape)

        ring = new(SLOTS, UNIT)
        w_hi = [rounded(f"w_hi{i}", (TSLOTS + i) * UNIT, NC, P) for i in range(NSPLIT)]
        w_lo = [rounded(f"w_lo{i}", (TSLOTS + i) * UNIT + D, NC, P) for i in range(NSPLIT)]
        spare = (TSLOTS + NSPLIT) * UNIT
        gx, gs = at(spare, 2, SEQ), at(spare + 2 * SEQ, 2, SEQ)
        S = at(spare + 4 * SEQ, H, P)
        ident, ones, tri, strict, causal_add = (new(P) for _ in range(5))
        block16, off32, off64, off128 = (new(P) for _ in range(4))
        tri16, causal_add16, spread16 = (new(P) for _ in range(3))
        own_head = new(H)
        one_of = new(2 * NSS - 1)
        c_rs, c_mean_eps = new(1), new(1)
        slot_no = new(CAP)
        keep4, keep32 = new(TT, 4), new(TT, 32)
        const = new(4)
        c_eps, c_one = (const[:, i:i + 1] for i in range(2))
        vec = new(P)
        lam_in, lam = new(4, 64), new(8)
        ssq, rstd = new(4), new(4)
        NCOL = 2 * H + 1
        blog, alog, dtb, eA, beta, g, sp, tmp17 = (new(NCOL) for _ in range(8))
        gc2 = new(2, NCOL)
        egc, begc, kdec, egt, ngc, nbeta = (new(NCOL) for _ in range(6))
        ba_meta = new(16)
        mx, rsum, rinv, nmax = (new(2, 2) for _ in range(4))
        top[0] = -(-top[0] // 8) * 8
        uT_start = top[0]
        new(2 * NC, L)
        uT_hi, uT_lo = rounded("uT_hi", uT_start, NC, L), rounded("uT_lo", uT_start + NC * L, NC, L)
        dqk_start = top[0]
        dqT, dkT = new(H, L), new(H, L)
        dv_start = top[0]
        dv_tok, dvT_meta, dkT_meta = new(TT, H, P), new(H, META), new(H, META)
        yaT_start = top[0]
        yaT = new(H, SEQ)
        top[0] = -(-top[0] // 8) * 8
        zone = top[0]

        aqT, akT, v_tok = new(H, SEQ), new(H, L), new(TT, H, P)
        v_meta = at(spare, H, P)
        NPREP = 3
        qz = new(NPREP * 2, P).rearrange("p (a b) i -> p a b i", b=2)
        dist, bias = new(TT, L), new(NPREP, L)
        prob = at(dv_start, 2, 2, L)
        wT = new(2, 3, P)
        vtmp = new(2, L)
        osq = at(dv_start + H * P + 6 * P, SEQ)
        rs_rows = at(FLOATS - FLOATS % 8 - L, L)
        cbuf = new(2, L + CONV - 1)
        NACC = 3
        acc = new(NACC, L)
        sg = new(2, L)
        csq = vtmp
        first_use_end = top[0]
        xin = at(dqk_start, 3, D)
        vec_rows = at(dqk_start + 3 * D, P)
        w_ba = at(dqk_start + 3 * D + P, NC, 16)
        uT = rounded("uT", dv_start, NC, L, F32)

        top[0] = zone
        NB = 8
        work = [[new(4, P) for _ in range(NB)] for _ in range(2)]
        yd_hi, yd_lo = rounded("yd_hi", zone, H, SEQ), rounded("yd_lo", zone + 2048, H, SEQ)
        gateT = rounded("gateT", top[0], H, SEQ, F32)
        new(H * SEQ)
        gaT = new(H, SEQ)
        gbT = at(yaT_start, H, SEQ)
        mixT = gaT
        um = at(zone + 8 * 512, H, P)

        h_tok = at(uT_start, TT, D)
        u2, u2T = at(dqk_start, TT, D), at(dqk_start + TT * D, NC, SEQ)
        norm2_b, fnorm_b = at(dv_start, D), at(dv_start + D, D)
        top[0] = zone
        r_w, r_b = at(uT_start + TT * D, NC, 36), at(uT_start + TT * D + NC * 36, 36)
        junk = new(D)
        lgT = new(SEQ)
        ssq_part = new(TT, 4)
        lg, me, me2, eq, e1, e2 = new(TT, 36), new(TT, 32), new(TT, 32), new(TT, 32), new(TT, 32), new(TT, 32)
        cum, comb, asg, rank, ovf = new(TT, 32), new(TT, 32), new(TT, 32), new(TT, 32), new(TT, 32)
        gsel, gd, pen, pen_cum = new(TT, 4), new(TT, 4), new(TT, 4), new(TT, 4)
        sc = new(12, TT)
        pick, pickw = new(TT, EPB, CAP), new(TT, EPB, CAP)
        pickT = new(TT, P)
        xg = new(NC, P)
        sil, hid, hidT = new(D_EXPERT), new(D_EXPERT), new(2, P)
        dsb = new(D)
        ovcnt = new(1)
        ovi = new(1).bitcast(I32)
        ftmp = new(SEQ)
        fhT = new(2, SEQ)
        result = u2
        after_experts = -(-top[0] // 8) * 8
        extra = [at(yaT_start, UNIT)] + [at(after_experts + i * UNIT, UNIT) for i in range(NEXTRA - 1)]
        assert after_experts >= zone + 4096 and after_experts + 3 * UNIT <= FLOATS

        x_in, vec_in, wba_in, small_in = sem("x_in"), sem("vec_in"), sem("wba_in"), sem("small_in")
        h_in, norms_in, stored = sem("h_in"), sem("norms_in"), sem("stored")
        slot_in = [sem(f"slot_in{i}") for i in range(SLOTS)]
        extra_in = [sem(f"extra_in{i}") for i in range(NEXTRA)]
        ident_ready, const_ready = sem("ident_ready"), sem("const_ready")
        vec_T, vec_ready = sem("vec_T"), sem("vec_ready")
        ssq_ready, var_ready, rstd_ready, xn_ready = sem("ssq_ready"), sem("var_ready"), sem("rstd_ready"), sem("xn_ready")
        xT_ready, uT_ready = sem("xT_ready"), sem("uT_ready")
        ba_ready, ba_meta_ready, ba_spread, ba_logits = sem("ba_ready"), sem("ba_meta_ready"), sem("ba_spread"), sem("ba_logits")
        g_exp, g_ready, gc_ready, gc_copied, gate_cols = sem("g_exp"), sem("g_ready"), sem("gc_ready"), sem("gc_copied"), sem("gate_cols")
        lam_dot, lam_exp = sem("lam_dot"), sem("lam_exp")
        tile_ready, tile_copied, mixed = sem("tile_ready"), sem("tile_copied"), sem("mixed")
        tr_ready, tr_copied = sem("tr_ready"), sem("tr_copied")
        qz_ready, scores_ready, biased, nmax_ready, exp_ready, w_ready = (sem("qz_ready"), sem("scores_ready"), sem("biased"), sem("nmax_ready"), sem("exp_ready"), sem("w_ready"))
        o_ready, osq_ready, oss_ready = sem("o_ready"), sem("osq_ready"), sem("oss_ready")
        conv_ready, csig, silu_ready, csq_ready, css_ready, rs_ready, qk_ready, spread_ready, o_copied = (sem("conv_ready"), sem("csig"), sem("silu_ready"), sem("csq_ready"), sem("css_ready"), sem("rs_ready"), sem("qk_ready"), sem("spread_ready"), sem("o_copied"))
        gate_ready = sem("gate_ready")
        w_hi_ready, w_lo_dve, w_lo_pool, u_hi, u_lo = sem("w_hi_ready"), sem("w_lo_dve"), sem("w_lo_pool"), sem("u_hi"), sem("u_lo")
        yd_hi_ready, yd_lo_ready = sem("yd_hi_ready"), sem("yd_lo_ready")
        dn_pe = [sem("dn_pe_a"), sem("dn_pe_b")]
        dn_dve = [sem("dn_dve_a"), sem("dn_dve_b")]
        dn_act = [sem("dn_act_a"), sem("dn_act_b")]
        dn_pool = [sem("dn_pool_a"), sem("dn_pool_b")]
        dec_masked = [sem("dec_masked_a"), sem("dec_masked_b")]
        dve_step, act_step, pool_step = sem("dve_step"), sem("act_step"), sem("pool_step")
        ssq2_ready, var2_ready, rstd2_ready, u2_scaled, u2_ready, hT_ps, hT_ready = (
            sem(n) for n in ("ssq2_ready", "var2_ready", "rstd2_ready", "u2_scaled", "u2_ready", "hT_ps", "hT_ready"))
        lgT_ps, lgT_ready, f_u2T_ps, f_u2T = sem("lgT_ps"), sem("lgT_ready"), sem("f_u2T_ps"), sem("f_u2T")
        logits_ready, r_exp_in, r_exp, assigned, ranked, routed = (sem("logits_ready"), sem("r_exp_in"), sem("r_exp"), sem("assigned"), sem("ranked"), sem("routed"))
        rank_ready, ovf_ready, ov_sum, ov_flag = sem("rank_ready"), sem("ovf_ready"), sem("ov_sum"), sem("ov_flag")
        picked, gathered, xg_a, xg_d, g_sig, hid_ready, hidT_ps, hidT_ready, down_a, down_d, combined = (
            sem(n) for n in ("picked", "gathered", "xg_a", "xg_d", "g_sig", "hid_ready", "hidT_ps", "hidT_ready",
                             "down_a", "down_d", "combined"))
        slot_used, pick_made, hid_step, f_step = sem("slot_used"), sem("pick_made"), sem("hid_step"), sem("f_step")
        f_in, f_h, f_sig, f_hT, f_y, f_acc, f_sum = (sem(n) for n in ("f_in", "f_h", "f_sig", "f_hT", "f_y", "f_acc", "f_sum"))
        ssq3_ready, var3_ready, rstd3_ready, out_ready = sem("ssq3_ready"), sem("var3_ready"), sem("rstd3_ready"), sem("out_ready")

        w_in_v = w_in[0].rearrange("(c p) n -> p c n", p=P)
        branch_v = {k: w[0].rearrange("(c p) n -> p c n", p=P)
                    for k, w in (("ya", w_branch_attn), ("yd", w_branch_dn), ("out", w_out))}
        w_gate_v = expert_w_gate[0].rearrange("e (c p) f -> c p e f", p=P)
        w_up_v = expert_w_up[0].rearrange("e (c p) f -> c p e f", p=P)
        w_down_v = expert_w_down[0].rearrange("e (c p) n -> c p e n", p=P)

        w_gate_e = expert_w_gate[0].rearrange("e (c p) f -> p e c f", p=P)
        w_up_e = expert_w_up[0].rearrange("e (c p) f -> p e c f", p=P)
        w_down_e = expert_w_down[0].rearrange("e (c p) n -> p e c n", p=P)
        f_down = ring[:, 2, :].rearrange("p (c n) -> p c n", c=2)

        def unit(u):
            return ring[:, u % TSLOTS, :].rearrange("p (c n) -> p c n", c=NC)

        def low_by_pool(q):
            return FIRST["dq"] <= q < FIRST["gate"] and q % 3 != 0

        def wait_split(eng, q):
            eng.wait_ge(w_hi_ready, q + 1)
            mine = [i for i in range(q + 1) if low_by_pool(i) == low_by_pool(q)]
            eng.wait_ge(w_lo_pool if low_by_pool(q) else w_lo_dve, len(mine))

        def split_source(eng, q):
            n = SPLIT[q]
            u, half = divmod(n, 2)
            eng.wait_ge(slot_in[u % TSLOTS], 16 * (u // TSLOTS + 1))
            if q >= NSPLIT:
                eng.wait_ge(tile_ready, SPLIT[q - NSPLIT] + 1)
            return unit(u)[:, :, half * P:(half + 1) * P]

        def split_high(q):
            nc.scalar.activation(w_hi[q % NSPLIT], split_source(nc.scalar, q), ACT.Copy).then_inc(w_hi_ready, 1)

        def split_low(eng, q):
            src = split_source(eng, q)
            eng.wait_ge(w_hi_ready, q + 1)
            eng.tensor_tensor(w_lo[q % NSPLIT], src, w_hi[q % NSPLIT].bitcast(F32), ALU.subtract).then_inc(
                w_lo_pool if low_by_pool(q) else w_lo_dve, 1)

        def splits_at(n):
            if n not in SPLIT:
                return []
            q = SPLIT.index(n)
            return [q + AHEAD] if q + AHEAD < len(SPLIT) else []

        def row(v, n):
            return v.rearrange("a n -> (a n)").unsqueeze(0).broadcast_to([P, n])

        def ring_gu(c, odd):
            return (extra[c] if odd and c < NEXTRA else ring[:, c, :]).rearrange("p (e m f) -> p e m f", e=EPB, m=2)

        def ring_down(half, fc):
            return ring[:, NC + 2 * half + fc, :].rearrange("p (e n) -> p e n", e=EPB)

        TOKENS = [slice(META + t * P, META + (t + 1) * P) for t in range(TT)] + [slice(0, META)]

        BY_DVE = ("ya", "yd", "out")

        def wait_tile_out(eng, n):
            kind = TILES[n][0]
            same = [i for i in range(n + 1) if (TILES[i][0] in BY_DVE) == (kind in BY_DVE)]
            eng.wait_ge(mixed if kind in BY_DVE else tile_copied, len(same))

        ATT_UNITS = H * TT
        SLOTS_A = 24 + 2
        SPREAD = [H + h for h in range(H)] + list(range(H)) + [2 * H + h for h in range(H)]

        N_DN = 2 * H

        def spread_bank(k):
            return bank[(2, 3, 5, 6)[k % 4] if k < N_DN else (5, 6)[k % 2]]

        def spread_at(m):
            return SPREAD[4 * (m - 22):min(4 * (m - 21), N_DN)] if m >= 22 else []

        TR = []
        for h in range(H):
            TR.append(("v", h))
        for m in range(SLOTS_A):
            if 2 <= m < ATT_UNITS + 2:
                TR.append(("w", m - 2))
            if m >= 16 + 2 and m - 2 < 24:
                TR.append(("dv", m - 2 - 16))
        TR_NO = {k: i for i, k in enumerate(TR)}

        STEPS = ["s0", "s1", "s2", "s3", "s4", "s5", "s6", "s7", "x1", "t1", "x2", "t2", "x3", "t3", "w", "v", "o", "q"]
        META_STEPS = ["s0", "s1", "s2", "s3", "s4", "s5", "s6", "s7", "w", "m"]
        DN = [("meta", 0, s) for s in META_STEPS]
        for t in range(TT):
            for s in STEPS:
                DN += [(t, 0, s), (t, 1, s)]
        WORKS = {
            "pe": set(STEPS + META_STEPS),
            "dve": {"s0", "s1", "s2", "s3", "s4", "s5", "s6", "s7", "t1", "t2", "t3", "q", "m"},
            "act": {"s0", "s2", "s3", "s4", "s5", "s7", "x1", "x2", "x3", "w", "v", "o", "q", "m"},
            "pool": {"s1", "s2", "s7", "t1", "t2", "q"},
        }

        def works(engine, key):
            t, _, s = key
            if t == "meta":
                if engine == "pool":
                    return s == "s2"
                if engine in ("dve", "act") and s == "w":
                    return engine == "dve"
            if engine == "dve" and s == "o":
                return t == 0
            return s in WORKS[engine]

        def done(engine, key, before=False):
            chain = [k for k in DN if k[1] == key[1]]
            upto = chain.index(key) + (0 if before else 1)
            return sum(works(engine, k) for k in chain[:upto])

        def wait_step(eng, engine, key, before=False):
            sems = {"pe": dn_pe, "dve": dn_dve, "act": dn_act, "pool": dn_pool}[engine]
            n = done(engine, key, before)
            if n:
                eng.wait_ge(sems[key[1]], n)

        every, first_half, rest = slice(None), slice(0, H // 2), slice(H // 2, H)
        RESULTS = [[(every, every, slice(0, SEQ - P)), (every, first_half, slice(SEQ - P, SEQ))],
                   [(every, rest, slice(SEQ - P, SEQ))]]

        AFTER = 4
        filler = list(range(FIRST["dq"] + SLOTS_A, FIRST["yd"] - AFTER))
        after = list(range(FIRST["yd"] - AFTER, FIRST["yd"]))
        MIX_ORDER = []
        groups = [[k] for k in DN if k[0] == "meta"]
        pairs = [k for k in DN if k[0] != "meta"]
        groups += [pairs[i:i + 2] for i in range(0, len(pairs), 2)]
        given = 0
        for i, group in enumerate(groups):
            while given < len(filler) and given * (len(groups) - 4) < i * len(filler):
                MIX_ORDER.append(("tile", filler[given]))
                given += 1
            MIX_ORDER += [("dn", k) for k in group]
            if i < H:
                MIX_ORDER.append(("spread", N_DN + i))
        MIX_ORDER += [("tile", n) for n in filler[given:]]

        BEHIND = []
        held = []
        for what in MIX_ORDER:
            if what[0] == "tile":
                BEHIND.append(("split", what[1]))
                held.append(what)
            elif what[0] == "spread":
                BEHIND.append(what)
            else:
                BEHIND.append(what)
                BEHIND += held
                held = []
        BEHIND += held
        for i, n in enumerate(after):
            MIX_ORDER.append(("tile", n))
            BEHIND += [("split", n)] + ([("result", i)] if i < 2 else []) + [("tile", n)]

        block = ctx.enter_context(nc.Block())

        @block.sync
        def _(sp):
            for t in range(TT):
                sp.dma_start(xin[:, t, :], x[0, t * P:(t + 1) * P, :]).then_inc(x_in, 16)
            sp.dma_start(xin[0:META, 2, :], meta_tokens).then_inc(x_in, 16)
            for u in range(N_UNITS):
                kind, j = TILES[2 * u]
                if u >= TSLOTS:
                    n = 2 * (u - TSLOTS)
                    if n in SPLIT:
                        wait_split(sp, SPLIT.index(n))
                        wait_split(sp, SPLIT.index(n + 1))
                    else:
                        sp.wait_ge(tile_ready, n + 2)
                src = branch_v[kind] if kind in branch_v else w_in_v
                c0 = (0 if kind in branch_v else W_COL[kind]) + j * P
                sp.dma_start(unit(u), src[:, :, c0:c0 + 2 * P]).then_inc(slot_in[u % TSLOTS], 16)
                if u == TSLOTS - 1:
                    for i, v in enumerate((lambda_q1, lambda_k1, lambda_q2, lambda_k2)):
                        sp.dma_start(lam_in[:, i, :], row(v, 64)).then_inc(small_in, 16)
                    for t in range(TT):
                        sp.dma_start(dtb[:, t * H:(t + 1) * H], row(dn_dt_bias, H)).then_inc(small_in, 16)
                        sp.dma_start(eA[:, t * H:(t + 1) * H], row(dn_A_log, H)).then_inc(small_in, 16)
                if u == N_UNITS - 2:
                    sp.wait_ge(tile_ready, FIRST["gb"] + 8)
                    for t in range(TT):
                        sp.dma_start(h_tok[:, t, :], x[0, t * P:(t + 1) * P, :]).then_inc(h_in, 16)

            def load_chunk(first_expert, odd, s):
                signal = (extra_in if odd and s < NEXTRA else slot_in)[s]
                if s < NC:
                    sp.dma_start(ring_gu(s, odd)[:, :, 0, :], w_gate_v[s, :, bass.ds(first_expert, EPB), :]).then_inc(signal, 16)
                    sp.dma_start(ring_gu(s, odd)[:, :, 1, :], w_up_v[s, :, bass.ds(first_expert, EPB), :]).then_inc(signal, 16)
                else:
                    half, fc = divmod(s - NC, 2)
                    sp.dma_start(ring_down(half, fc), w_down_v[fc, :, bass.ds(first_expert, EPB), half * 512:(half + 1) * 512]).then_inc(signal, 16)

            def wait_tiles(s):
                n = 2 * (N_UNITS - TSLOTS + s)
                if s >= TSLOTS:
                    sp.wait_ge(tile_ready, FIRST["out"])
                elif n in SPLIT:
                    wait_split(sp, SPLIT.index(n))
                    wait_split(sp, SPLIT.index(n + 1))
                else:
                    sp.wait_ge(tile_ready, n + 2)

            out_slots = [u % TSLOTS for u in range(FIRST["out"] // 2, N_UNITS)]
            for s in range(SLOTS):
                if s not in out_slots:
                    wait_tiles(s)
                    load_chunk(0, False, s)
            sp.wait_ge(mixed, 2 * NC)
            for s in range(2):
                load_chunk(EPB, True, s)
            for s in out_slots:
                wait_tiles(s)
                load_chunk(0, False, s)
            sp.wait_ge(tile_ready, len(TILES))
            for s in range(2, NEXTRA):
                load_chunk(EPB, True, s)

            def load_first(first_expert, odd, used):
                for s in range(NEXTRA):
                    sp.wait_ge(slot_used, used * SLOTS + s + 1)
                    load_chunk(first_expert, odd, s)

            def load_rest(first_expert, odd, used):
                for s in range(NEXTRA, NC):
                    sp.wait_ge(slot_used, used * SLOTS + s + 1)
                    load_chunk(first_expert, odd, s)
                for half in range(2):
                    sp.wait_ge(slot_used, used * SLOTS + NC + 2 * half + 2)
                    for fc in (1, 0):
                        load_chunk(first_expert, odd, NC + 2 * half + fc)

            with sp.Fori(0, N_BATCH // 2 - 1) as pair:
                load_first((2 * pair + 2) * EPB, False, 2 * pair)
                load_rest((2 * pair + 1) * EPB, True, 2 * pair)
                load_first((2 * pair + 3) * EPB, True, 2 * pair + 1)
                load_rest((2 * pair + 2) * EPB, False, 2 * pair + 1)
            for s in range(NEXTRA, SLOTS):
                sp.wait_ge(slot_used, (N_BATCH - 2) * SLOTS + s + 1)
                load_chunk((N_BATCH - 1) * EPB, True, s)

            sp.wait_ge(ov_flag, 1)
            beyond = sp.value_load(ovi[0:1, 0:1], min_val=0, max_val=2 * SEQ)
            with sp.If(beyond > 0):
                with sp.Fori(0, N_EXPERTS) as e:
                    sp.wait_ge(combined, N_BATCH)
                    sp.wait_ge(f_y, e * 4 + 1)
                    sp.dma_start(unit(0), w_gate_e[:, bass.ds(e, 1), :, :].rearrange("p a c f -> p (a c) f")).then_inc(f_in, 16)
                    sp.dma_start(unit(1), w_up_e[:, bass.ds(e, 1), :, :].rearrange("p a c f -> p (a c) f")).then_inc(f_in, 16)
                    sp.dma_start(f_down, w_down_e[:, bass.ds(e, 1), :, :].rearrange("p a c f -> p (a c) f")).then_inc(f_in, 16)

            for t in range(TT):
                sp.wait_ge(out_ready, t + 1)
                sp.dma_start(out[0, t * P:(t + 1) * P, :], result[:, t, :]).then_inc(stored, 16)
            sp.wait_ge(stored, 16 * TT)

        @block.gpsimd
        def _(pool):
            n_step = [0]

            def link(ins):
                n_step[0] += 1
                ins.then_inc(pool_step, 1)
                pool.wait_ge(pool_step, n_step[0])

            def select(o, i, pattern, op, fill, base, mult):
                return pool.affine_select(out=o, in_=i, pattern=pattern, compare_op=op, fill=fill,
                                          base=base, channel_multiplier=mult)

            link(pool.memset(ones, 1.0))
            select(ident, ones, [[-1, P]], ALU.is_equal, 0.0, 0, 1).then_inc(ident_ready, 1)
            pool.memset(c_eps, EPS)
            pool.memset(one_of, 0.0)
            for keep in (keep4, keep32):
                link(pool.memset(keep, 1.0))
                pool.memset(keep[:, :, 0:1], 0.0)
            pool.memset(c_rs, 0.0)
            pool.memset(c_one, 1.0)
            link(pool.memset(causal_add, 0.0))
            select(tri, ones, [[1, P]], ALU.is_ge, 0.0, 0, -1)
            select(strict, ones, [[1, P]], ALU.is_gt, 0.0, 0, -1)
            link(select(causal_add, causal_add, [[1, P]], ALU.is_ge, NEG, 0, -1))

            def blocks(dst, src, size, fill=0.0):
                v = dst.rearrange("p (b s) -> p b s", s=size)
                w = src.rearrange("p (b s) -> p b s", s=size)
                link(select(v, w, [[-size, P // size], [0, size]], ALU.is_ge, fill, 0, 1))
                link(select(v, v, [[size, P // size], [0, size]], ALU.is_ge, fill, size - 1, -1))

            blocks(block16, ones, META)
            blocks(tri16, tri, META)
            blocks(causal_add16, causal_add, META, NEG)
            blocks(off32, ones, 32)
            blocks(off64, ones, 64)
            link(pool.tensor_tensor(off128, ones, off64, ALU.subtract))
            link(pool.tensor_tensor(off64, off64, off32, ALU.subtract))
            link(pool.tensor_tensor(off32, off32, block16, ALU.subtract))
            link(pool.tensor_copy(own_head, block16.rearrange("p (b s) -> p b s", s=META)[:, :, 0]))
            pool.tensor_copy(spread16[0:META, :].rearrange("p (b s) -> p b s", s=META),
                             ident[0:META, 0:META].unsqueeze(1).broadcast_to([META, H, META]))
            pool.iota(slot_no.bitcast(I32), [[1, CAP]], base=0, channel_multiplier=0)
            for t in range(TT):
                pool.iota(dist[:, t, :].bitcast(I32), [[1, L]], base=-(META + t * P), channel_multiplier=-1)
            pool.memset(qz, 0.0)
            pool.memset(v_meta, 0.0)
            pool.memset(rs_rows, 0.0)
            for i in range(2):
                pool.memset(wT[:, i, 0, :], 0.0)
            for i in range(2):
                pool.memset(cbuf[:, i, 0:CONV - 1], 0.0)
            pool.memset(one_of[:, NSS - 1:NSS], 1.0)
            link(select(c_rs, c_rs, [[0, 1]], ALU.is_ge, -0.5 * math.log(P), -H, 1))
            link(select(c_mean_eps, c_eps, [[0, 1]], ALU.is_ge, EPS * P, 2 * H - 1, -1))
            link(select(c_rs, c_rs, [[0, 1]], ALU.is_ge, 0.5 * math.log(P) + math.log(1.0 - LAMBDA_INIT), 2 * H - 1, -1))
            link(pool.memset(rsum, 0.0))
            pool.tensor_copy(slot_no, slot_no.bitcast(I32))
            link(pool.tensor_copy(dist, dist.bitcast(I32)))
            for t in range(TT):
                last = select(dist[:, t, :], dist[:, t, :], [[-1, L]], ALU.is_ge, NEG, META + t * P, 1)
            last.then_inc(const_ready, 1)

            def att_prep(i):
                h, t = divmod(i, TT)
                b = i % NPREP
                if i == 0:
                    pool.wait_ge(const_ready, 1)
                wait_tile_out(pool, FIRST["aq"] + h)
                if i >= NPREP:
                    pool.wait_ge(scores_ready, i - NPREP + 1)
                    pool.wait_ge(biased, i - NPREP + 1)
                link(pool.tensor_copy(qz[0:64, b, 0, :], aqT[0:64, h, t * P:(t + 1) * P]))
                link(pool.tensor_copy(qz[64:P, b, 1, :], aqT[64:P, h, t * P:(t + 1) * P]))
                nk = META + (t + 1) * P
                pool.tensor_scalar(bias[:, b, 0:nk], dist[:, t, 0:nk], 2.0 ** (-(h + 1)) / SCALE, 0.0,
                                   ALU.mult, ALU.add).then_inc(qz_ready, 1)

            for n in range(FIRST["dq"]):
                for q in splits_at(n):
                    if low_by_pool(q):
                        split_low(pool, q)
            for i in range(NPREP - 1):
                att_prep(i)
            for n in range(FIRST["dq"], FIRST["dq"] + SLOTS_A):
                i = n - FIRST["dq"] + NPREP - 1
                if i < ATT_UNITS:
                    att_prep(i)
                for q in splits_at(n):
                    if low_by_pool(q):
                        split_low(pool, q)

            def dn(t, c, s):
                if not works("pool", (t, c, s)):
                    return
                w = work[c]
                n = 1 if t == "meta" else 4
                hs = slice(4 * c, 4 * c + 4)
                every = lambda m: m.unsqueeze(1).broadcast_to([P, n, P])
                for engine in ("pe", "act", "dve"):
                    wait_step(pool, engine, (t, c, s))
                if s == "s1":
                    q = dqT[:, hs, META + t * P:META + (t + 1) * P]
                    last = pool.tensor_tensor(q, q, w[7][:, 0:n, :], ALU.mult)
                elif s == "s2":
                    last = pool.tensor_tensor(w[5][:, 0:n, :], w[1][:, 0:n, :], every(block16), ALU.mult)
                elif s in ("s7", "t1", "t2"):
                    off = {"s7": off32, "t1": off64, "t2": off128}[s]
                    last = pool.tensor_tensor(w[4][:, 0:n, :], w[1][:, 0:n, :], every(off), ALU.mult)
                elif s == "q":
                    y = gateT[:, hs, t * P:(t + 1) * P]
                    last = pool.tensor_tensor(y, y, w[7][:, 0:n, :], ALU.mult)
                last.then_inc(dn_pool[c], 1)

            for what, arg in BEHIND:
                if what == "dn":
                    dn(*arg)

            pool.wait_ge(norms_in, 16 * 6)
            for t in range(TT):
                pool.wait_ge(u2_scaled, t + 1)
                pool.tensor_tensor(u2[:, t, :], u2[:, t, :], norm2_b, ALU.mult).then_inc(u2_ready, 1)
            pool.wait_ge(rank_ready, 1)
            pool.tensor_scalar(eq, rank, float(CAP), None, ALU.is_ge).then_inc(routed, 1)
            pool.wait_ge(routed, 1)
            pool.tensor_tensor(ovf, eq, comb, ALU.mult).then_inc(ovf_ready, 1)

        @block.tensor
        def _(pe):
            pe.wait_ge(ident_ready, 1)
            for t in range(3):
                rows = P if t < TT else META
                pe.wait_ge(xn_ready, t + 1)
                for c in range(NC):
                    last = pe.transpose(bank[2 + 2 * t + c // 4][:, (c % 4) * P:(c % 4) * P + rows],
                                        xin[0:rows, t, c * P:(c + 1) * P], ident[0:rows, 0:rows])
                last.then_inc(xT_ready, 1)
                if t == 0:
                    pe.wait_ge(vec_in, 16 * 5)
                    pe.transpose(bank[0][:, 0:N_VEC], vec_rows[0:N_VEC, :], ident[0:N_VEC, 0:N_VEC]).then_inc(vec_T, 1)

            def ba_logit_products():
                pe.wait_ge(wba_in, 16)
                for t in range(3):
                    rows, c0 = (P, META + t * P) if t < TT else (META, 0)
                    for c in range(NC):
                        last = pe.matmul(bank[2][0:rows, 16 * t:16 * t + 16], uT[:, c, c0:c0 + rows], w_ba[:, c, :],
                                         start=(c == 0), stop=(c == NC - 1))
                last.then_inc(ba_ready, 1)

            def tile(n):
                kind, j = TILES[n]
                u, half = divmod(n, 2)
                if n in SPLIT:
                    q = SPLIT.index(n)
                    wait_split(pe, q)
                    hi, lo = w_hi[q % NSPLIT], w_lo[q % NSPLIT]
                else:
                    pe.wait_ge(slot_in[u % TSLOTS], 16 * (u // TSLOTS + 1))
                if n >= 2:
                    wait_tile_out(pe, n - 2)
                ps = bank[n % 2]
                if kind == "ya":
                    if j == 0:
                        pe.wait_ge(qk_ready, NSS)
                    for c in range(NC):
                        last = pe.matmul(ps[:, 0:SEQ], unit(u)[:, c, half * P:(half + 1) * P], yaT[:, c, :],
                                         start=(c == 0), stop=(c == NC - 1))
                elif kind == "out":
                    t = j % 2
                    pe.wait_ge(mixed, 2 * NC)
                    for c in range(NC):
                        last = pe.matmul(ps[:, 0:SEQ], mixT[:, c, t * P:(t + 1) * P], unit(u)[:, c, :],
                                         start=(c == 0), stop=(c == NC - 1))
                else:
                    if kind == "yd":
                        pe.wait_ge(yd_hi_ready, 2)
                        pe.wait_ge(yd_lo_ready, 2)
                        s_hi, s_lo = yd_hi, yd_lo
                    else:
                        s_hi, s_lo = (uT_hi, uT_lo) if kind in ("ak", "av", "dq", "dk", "dv") else (uT_hi[:, :, META:], uT_lo[:, :, META:])
                    for c in range(NC):
                        for i, (a, b) in enumerate(((hi, s_hi), (hi, s_lo), (lo, s_hi))):
                            last = pe.matmul(ps[:, 0:b.shape[2]], a[:, c, :], b[:, c, :],
                                             start=(c == 0 and i == 0), stop=(c == NC - 1 and i == 2))
                last.then_inc(tile_ready, 1)

            def tr_free(key):
                k = TR_NO[key]
                if k:
                    pe.wait_ge(tr_copied, k)

            def tr_values(h, key, src, with_meta):
                tr_free(key)
                if with_meta:
                    pe.transpose(bank[4][0:META, 0:P], src[:, 0:META], ident)
                for t in range(TT):
                    last = pe.transpose(bank[4][:, (t + 1) * P:(t + 2) * P], src[:, META + t * P:META + (t + 1) * P], ident)
                last.then_inc(tr_ready, 1)

            for n in range(FIRST["aq"]):
                if n == 0:
                    pe.wait_ge(u_hi, 3)
                    pe.wait_ge(u_lo, 3)
                tile(n)
                if n == 2:
                    ba_logit_products()
                if n == 3:
                    pe.wait_ge(const_ready, 1)
                    pe.wait_ge(ba_meta_ready, 1)
                    pe.matmul(bank[3][:, 0:16], spread16[0:META, :], ba_meta[0:META, :], start=True, stop=True).then_inc(ba_spread, 1)
                if n >= FIRST["av"] + 1:
                    h = n - 1 - FIRST["av"]
                    wait_tile_out(pe, n - 1)
                    tr_values(h, ("v", h), vtmp[:, h % 2, :], True)
            for n in range(FIRST["aq"], FIRST["dq"]):
                tile(n)
                if n == FIRST["aq"]:
                    wait_tile_out(pe, n - 1)
                    tr_values(H - 1, ("v", H - 1), vtmp[:, (H - 1) % 2, :], True)
                if n == FIRST["aq"] + 1:
                    pe.wait_ge(g_ready, 1)
                    real, own = slice(0, 2 * H), slice(2 * H, NCOL)
                    pe.matmul(bank[5][:, 0:16], tri, g[:, real], start=True, stop=True)
                    pe.matmul(bank[5][:, 16:17], tri16, g[:, own], start=True, stop=True)
                    pe.matmul(bank[5][:, 17:33], ones, g[:, real], start=True, stop=True)
                    pe.matmul(bank[5][:, 33:34], block16, g[:, own], start=True, stop=True).then_inc(gc_ready, 1)

            def att_scores(i):
                h, t = divmod(i, TT)
                nk = META + (t + 1) * P
                pe.wait_ge(qz_ready, i + 1)
                if i:
                    pe.wait_ge(biased, i)
                for m in range(2):
                    last = pe.matmul(bank[2 + m][:, 0:nk], qz[:, i % NPREP, m, :], akT[:, h, 0:nk], start=True, stop=True)
                last.then_inc(scores_ready, 1)

            def att_turn(i):
                h, t = divmod(i, TT)
                pe.wait_ge(w_ready, i + 1)
                tr_free(("w", i))
                w = prob[:, i % 2, 0, :]
                pe.transpose(bank[4][0:META, 0:P], w[:, 0:META], ident)
                for k in range(t + 1):
                    last = pe.transpose(bank[4][:, (k + 1) * P:(k + 2) * P], w[:, META + k * P:META + (k + 1) * P], ident)
                last.then_inc(tr_ready, 1)

            def att_out(i):
                h, t = divmod(i, TT)
                pe.wait_ge(tr_copied, TR_NO[("w", i)] + 1)
                if i == 0:
                    pe.wait_ge(gc_copied, 1)
                if t == 0 and h >= 2:
                    pe.wait_ge(o_copied, h - 1)
                    pe.wait_ge(osq_ready, h - 1)
                o = bank[5 + h % 2][:, t * P:(t + 1) * P]
                pe.matmul(o, v_meta[:, h, :], wT[:, i % 2, 0, :], start=True, stop=False)
                for k in range(t + 1):
                    last = pe.matmul(o, v_tok[:, k, h, :], wT[:, i % 2, 1 + k, :], start=False, stop=(k == t))
                last.then_inc(o_ready, 1)

            def row_sums(i, src, n):
                return pe.matmul(bank[7][0:NSS, 0:n], one_of[:, NSS - 1 - i:2 * NSS - 1 - i], src,
                                 start=(i == 0), stop=(i == NSS - 1))

            def att_ss(h):
                pe.wait_ge(osq_ready, h + 1)
                row_sums(2 * H + h, osq, SEQ).then_inc(oss_ready, 1)

            def conv_ss(c):
                pe.wait_ge(csq_ready, c + 1)
                row_sums(c, csq[:, c % 2, :], L).then_inc(css_ready, 1)

            def spread(k):
                if k == 0:
                    pe.wait_ge(rs_ready, 1)
                if k < 4:
                    pe.wait_ge(biased, ATT_UNITS)
                    pe.wait_ge(o_copied, H)
                    pe.wait_ge(osq_ready, H)
                else:
                    pe.wait_ge(qk_ready, k - 3 if k < N_DN else k - 1)
                pe.matmul(spread_bank(k)[:, 0:L], ident[:, SPREAD[k]:SPREAD[k] + 1].broadcast_to([P, P]), rs_rows,
                          start=True, stop=True).then_inc(spread_ready, 1)

            for m in range(SLOTS_A):
                tile(FIRST["dq"] + m)
                if m < ATT_UNITS:
                    att_scores(m)
                if 2 <= m < ATT_UNITS + 2:
                    att_turn(m - 2)
                if m >= 18 and m - 2 < 24:
                    h = m - 18
                    pe.wait_ge(silu_ready, m - 2 + 1)
                    tr_values(h, ("dv", h), acc[:, (m - 2) % NACC, :], False)
                if 3 <= m < ATT_UNITS + 3:
                    att_out(m - 3)
                if 5 <= m < ATT_UNITS + 5 and m % 2 == 1:
                    att_ss((m - 5) // 2)
                if 3 <= m < 16 + 3:
                    conv_ss(m - 3)
                for i in spread_at(m):
                    spread(SPREAD.index(i))

            def dn(t, c, s):
                w = work[c]
                X, Y, Z = (bank[2 + 3 * c + i][:, :].rearrange("p (h i) -> p h i", h=4) for i in range(3))
                n = 1 if t == "meta" else 4
                for engine in ("act", "dve", "pool"):
                    wait_step(pe, engine, (t, c, s), before=True)
                if (t, c, s) == DN[0]:
                    pe.wait_ge(tr_copied, len(TR))
                    pe.wait_ge(qk_ready, N_DN)
                    pe.wait_ge(gate_cols, 2)

                def each(o, lhsT, rhs, start=True, stop=True):
                    for h in range(n):
                        last = pe.matmul(o[:, h, :], lhsT(h), rhs(h), start=start, stop=stop)
                    return last

                if t == "meta":
                    kT = lambda h: dkT_meta.rearrange("p h i -> p (h i)")
                    vT = lambda h: dvT_meta.rearrange("p h i -> p (h i)")
                    col = lambda h: g[:, 2 * H:2 * H + 1]
                    lower = tri16
                else:
                    cols = slice(META + t * P, META + (t + 1) * P)
                    kT = lambda h: dkT[:, 4 * c + h, cols]
                    qT = lambda h: dqT[:, 4 * c + h, cols]
                    col = lambda h: g[:, t * H + 4 * c + h:t * H + 4 * c + h + 1]
                    lower = tri
                buf = lambda i: (lambda h: w[i][:, h, :])
                if s == "s0":
                    each(X, lambda h: col(h).broadcast_to([P, P]), lambda h: lower)
                    last = each(Y, kT, kT)
                elif s == "s1":
                    for h in range(n):
                        last = pe.transpose(X[:, h, :], w[1][:, h, :], ident)
                    if t != "meta":
                        last = each(Z, kT, qT)
                elif s == "s2":
                    for h in range(n):
                        last = pe.transpose(Y[:, h, :], w[2][:, h, :], ident)
                elif s == "s3":
                    each(X, buf(4), buf(5))
                    last = each(Z, buf(5), buf(4))
                elif s == "s4":
                    each(Y, buf(0), buf(6))
                    each(X, buf(2), buf(0))
                    last = each(Z, buf(0), buf(2))
                elif s == "s5":
                    each(Y, buf(4), buf(6))
                    last = each(X, buf(5), buf(4))
                elif s == "s6":
                    last = each(Z, buf(2), buf(6))
                elif s == "s7":
                    for h in range(n):
                        pe.transpose(X[:, h, :], w[6][:, h, :], ident)
                    for h in range(n):
                        last = pe.transpose(Y[:, h, :], kT(h), ident)
                    if t == "meta":
                        last = pe.transpose(Z[:, 0, :], vT(0), ident)
                elif s in ("x1", "x2", "x3"):
                    last = each(Z, buf(4), buf(6))
                elif s in ("t1", "t2", "t3"):
                    last = each(X, buf(5), buf(0))
                    if s != "t3":
                        last = each(Z, buf(0), buf(5))
                elif s == "w":
                    if t == "meta":
                        last = pe.matmul(Z[:, 0, :], w[0][:, 0, :], w[3][:, 0, :], start=True, stop=True)
                    else:
                        last = each(X, buf(2), buf(0))
                elif s == "m":
                    for half in range(2):
                        last = pe.matmul(bank[2 + half][:, :], w[7][:, 0, :], um[:, 4 * half:4 * half + 4, :],
                                         start=True, stop=True)
                elif s == "v":
                    for h in range(n):
                        pe.matmul(Z[:, h, :], w[0][:, h, :], w[4][:, h, :], start=True, stop=False)
                        last = pe.matmul(Z[:, h, :], w[6][:, h, :], S[:, 4 * c + h, :], start=False, stop=True)
                elif s == "o":
                    for h in range(n):
                        pe.matmul(Y[:, h, :], S[:, 4 * c + h, :], qT(h), start=True, stop=False)
                        last = pe.matmul(Y[:, h, :], w[5][:, h, :], w[3][:, h, :], start=False, stop=True)
                    if t < TT - 1:
                        last = each(X, buf(7), buf(5))
                elif s == "q":
                    last = pe.matmul(Z, ones, w[6], start=True, stop=True)
                last.then_inc(dn_pe[c], 1)

            for what, arg in MIX_ORDER:
                if what == "tile":
                    tile(arg)
                elif what == "spread":
                    spread(arg)
                else:
                    if arg == (0, 1, "s0"):
                        pe.wait_ge(qk_ready, NSS)
                        wait_step(pe, "dve", ("meta", 0, "m"))
                        wait_step(pe, "act", ("meta", 0, "m"))
                    dn(*arg)
            for n in range(FIRST["yd"], FIRST["out"]):
                tile(n)

            def piece_turn(i):
                pe.wait_ge(mixed, 16 + 2 * (i + 1))
                if i >= 2:
                    pe.wait_ge(hT_ready, i - 1)
                for k in range(2):
                    for t in range(TT):
                        last = pe.transpose(bank[4 + i % 2][:, (2 * k + t) * P:(2 * k + t + 1) * P],
                                            h_tok[:, t, (2 * i + k) * P:(2 * i + k + 1) * P], ident)
                last.then_inc(hT_ps, 1)

            def piece_logits(i):
                pe.wait_ge(norms_in, 16 * 6)
                pe.wait_ge(hT_ready, i + 1)
                for c in (2 * i, 2 * i + 1):
                    last = pe.matmul(bank[6][0:36, 0:SEQ], r_w[:, c, :], u2T[:, c, :], start=(c == 0), stop=(c == NC - 1))
                if i == 3:
                    last.then_inc(lgT_ps, 1)

            def piece_seed(t, i):
                return pe.matmul(bank[2 * t + i // 2][:, (i % 2) * 256:(i % 2 + 1) * 256], ident,
                                 h_tok[:, t, i * 256:(i + 1) * 256], start=(i % 2 == 0), stop=False, skip_group_check=True)

            for n in range(FIRST["out"], len(TILES)):
                tile(n)
                j = n - FIRST["out"]
                if j >= 2 and j % 2 == 0:
                    piece_turn(j // 2 - 1)
                if j >= 3 and j % 2 == 1:
                    piece_logits(j // 2 - 1)
                    piece_seed(1, j // 2 - 1)
            piece_turn(3)
            piece_seed(1, 3)
            piece_seed(0, 0)
            piece_logits(3)
            pe.wait_ge(lgT_ready, 1)
            for t in range(TT):
                last = pe.transpose(bank[6][:, 256 + 64 * t:256 + 64 * t + 36], lgT[0:36, t * P:(t + 1) * P], ident[0:36, 0:36])
            last.then_inc(logits_ready, 1)
            for i in range(1, 4):
                last = piece_seed(0, i)
            last.then_inc(gathered, 1)
            pe.wait_ge(assigned, 1)
            pe.matmul(bank[7][:, 0:32], strict, asg[:, 0, :], start=True, stop=True)
            pe.matmul(bank[7][:, 32:64], ones, asg[:, 0, :], start=True, stop=False)
            pe.matmul(bank[7][:, 32:64], strict, asg[:, 1, :], start=False, stop=True).then_inc(ranked, 1)
            pe.wait_ge(routed, 1)
            pe.matmul(bank[5][:, 0:TT * 32], ones, eq.rearrange("p t k -> p (t k)"), start=True, stop=True).then_inc(ov_sum, 1)

            pe.wait_ge(u2_ready, TT)
            def batch(pair, odd):
                b = 2 * pair + odd
                pe.wait_ge(pick_made, b + 1)
                for group in range(2):
                    for c in range(4 * group, 4 * group + 4):
                        for t in range(TT):
                            last = pe.matmul(bank[6 + group][:, (c % 4) * P:(c % 4 + 1) * P], u2[:, t, c * P:(c + 1) * P],
                                             pick[:, t].rearrange("p e s -> p (e s)"), start=(t == 0), stop=(t == TT - 1))
                    last.then_inc(gathered, 1)
                    pe.wait_ge(xg_d if group else xg_a, b + 1)
                    for c in range(4 * group, 4 * group + 4):
                        if c < NEXTRA and odd:
                            pe.wait_ge(extra_in[c], pair * 32 + 32)
                        else:
                            pe.wait_ge(slot_in[c], (pair if c < NEXTRA else b) * 32 + 16 * (N_UNITS // TSLOTS if c < TSLOTS else 0) + 32)
                        for e in range(EPB):
                            last = pe.matmul(bank[4][CAP * e:CAP * (e + 1), :], xg[:, c, CAP * e:CAP * (e + 1)],
                                             ring_gu(c, odd)[:, e].rearrange("p m f -> p (m f)"), start=(c == 0), stop=(c == NC - 1),
                                             tile_position=(0, CAP * e))
                        last.then_inc(slot_used, 1)
                pe.wait_ge(picked, b + 1)
                pe.wait_ge(ov_flag, 1)
                for t in range(TT):
                    last = pe.transpose(bank[5][:, t * P:(t + 1) * P], pickw[:, t].rearrange("p e s -> p (e s)"), ident)
                last.then_inc(gathered, 1)
                pe.wait_ge(hid_ready, b + 1)
                for fc in range(2):
                    last = pe.transpose(bank[5][:, (2 + fc) * P:(3 + fc) * P], hid[:, fc * P:(fc + 1) * P], ident)
                last.then_inc(hidT_ps, 1)
                pe.wait_ge(hidT_ready, b + 1)
                for half in range(2):
                    for fc in range(2):
                        s = NC + 2 * half + fc
                        pe.wait_ge(slot_in[s], b * 16 + 16)
                        for e in range(EPB):
                            last = pe.matmul(bank[6 + half][CAP * e:CAP * (e + 1), :], hidT[:, fc, CAP * e:CAP * (e + 1)],
                                             ring_down(half, fc)[:, e, :], start=(fc == 0), stop=(fc == 1),
                                             tile_position=(0, CAP * e))
                        last.then_inc(slot_used, 1)
                for half in range(2):
                    pe.wait_ge(down_a if half == 0 else down_d, b + 1)
                    for t in range(TT):
                        last = pe.matmul(bank[2 * t + half][:, :], pickT[:, t, :], dsb[:, half * 512:(half + 1) * 512],
                                         start=False, stop=False, skip_group_check=True)
                last.then_inc(combined, 1)

            with pe.Fori(0, N_BATCH // 2) as pair:
                for odd in range(2):
                    batch(pair, odd)

            beyond = pe.value_load(ovi[0:1, 0:1], min_val=0, max_val=2 * SEQ)
            with pe.If(beyond > 0):
                for s in (f_y, f_hT, f_sum):
                    pe.sem_inc(s, 1)
                for t in range(TT):
                    for c in range(NC):
                        last = pe.transpose(bank[4 + 2 * t + c // 4][:, (c % 4) * P:(c % 4 + 1) * P],
                                            u2[:, t, c * P:(c + 1) * P], ident)
                last.then_inc(f_u2T_ps, 1)
                pe.wait_ge(f_u2T, 1)
                with pe.Fori(0, N_EXPERTS) as e:
                    pe.wait_ge(f_in, e * 48 + 48)
                    for fc in range(2):
                        pe.wait_ge(f_hT, e * 2 + fc + 1)
                        for k in range(2):
                            for c in range(NC):
                                last = pe.matmul(bank[4][:, k * SEQ:(k + 1) * SEQ], unit(k)[:, c, fc * P:(fc + 1) * P], u2T[:, c, :],
                                                 start=(c == 0), stop=(c == NC - 1))
                        last.then_inc(f_h, 1)
                    pe.wait_ge(f_hT, e * 2 + 3)
                    for t in range(TT):
                        for half in range(2):
                            k = 2 * t + half
                            for fc in range(2):
                                last = pe.matmul(bank[5][:, :], fhT[:, fc, t * P:(t + 1) * P], f_down[:, fc, half * 512:(half + 1) * 512],
                                                 start=(fc == 0), stop=(fc == 1))
                            last.then_inc(f_y, 1)
                            pe.wait_ge(f_acc, e * 4 + k + 1)
                            last = pe.matmul(bank[k][:, :], ident, dsb[:, 0:512], start=False, stop=False, skip_group_check=True)
                            last.then_inc(f_sum, 1)

        @block.scalar
        def _(act):
            act.dma_start(vec_rows[V_NORM1:V_NORM1 + 8, :], norm1_w[0].rearrange("(c p) -> c p", p=P)).then_inc(vec_in, 16)
            act.dma_start(vec_rows[V_SUBLN:V_SUBLN + 1, :], da_subln_w).then_inc(vec_in, 16)
            act.dma_start(vec_rows[V_DNW:V_DNW + 1, :], dn_norm_w).then_inc(vec_in, 16)
            act.dma_start(vec_rows[V_NORM2:V_NORM2 + 8, :], norm2_w[0].rearrange("(c p) -> c p", p=P)).then_inc(vec_in, 16)
            act.dma_start(vec_rows[V_CONV:N_VEC, :], dn_conv_w[0].rearrange("k (c p) -> (k c) p", p=P)).then_inc(vec_in, 16)
            act.preload_act_table_set("natural_log_exp_and_others")
            n_step = [0]

            def link(ins):
                n_step[0] += 1
                ins.then_inc(act_step, 1)
                act.wait_ge(act_step, n_step[0])

            act.wait_ge(x_in, 16 * 3)
            squares = at(zone, 3, D)
            for t in range(4):
                if t < 3:
                    rows = P if t < TT else META
                    act.activation(squares[0:rows, t, :], xin[0:rows, t, :], ACT.Square, accum_out=ssq[0:rows, t:t + 1]).then_inc(ssq_ready, 1)
                if t:
                    rows = P if t - 1 < TT else META
                    act.wait_ge(var_ready, t)
                    link(act.activation(rstd[0:rows, t - 1:t], ssq[0:rows, t - 1:t], ACT.Ln))
                    act.activation(rstd[0:rows, t - 1:t], rstd[0:rows, t - 1:t], ACT.Exp, scale=-0.5).then_inc(rstd_ready, 1)

            def decay_logs():
                act.wait_ge(ba_logits, 1)
                act.wait_ge(const_ready, 1)
                act.activation(beta, blog, ACT.Exp, scale=-1.0)
                act.activation(eA, eA, ACT.Exp)
                link(act.activation(sp, tmp17, ACT.Exp, scale=-1.0))
                act.activation(sp, sp, ACT.Ln, bias=c_one).then_inc(g_exp, 1)

            def decay_exps():
                act.wait_ge(gc_copied, 2)
                act.activation(egc, gc2[:, 0, :], ACT.Exp)
                act.activation(egt, gc2[:, 1, :], ACT.Exp)
                act.activation(kdec, kdec, ACT.Exp).then_inc(gate_cols, 1)

            def tile_out(n):
                kind, j = TILES[n]
                if kind in BY_DVE:
                    return
                act.wait_ge(tile_ready, n + 1)
                ps = bank[n % 2]
                if kind == "ak":
                    if j == 0:
                        act.wait_ge(uT_ready, 3)
                    last = act.activation(akT[:, j, :], ps[:, 0:L], ACT.Copy)
                elif kind == "av":
                    if j >= 2:
                        act.wait_ge(tr_ready, j - 1)
                    last = act.activation(vtmp[:, j % 2, :], ps[:, 0:L], ACT.Copy)
                elif kind == "aq":
                    last = act.activation(aqT[:, j, :], ps[:, 0:SEQ], ACT.Copy)
                elif kind in ("dq", "dk", "dv"):
                    c = n - FIRST["dq"]
                    if c >= 2:
                        act.wait_ge(conv_ready, c - 1)
                    last = act.activation(cbuf[:, c % 2, CONV - 1:], ps[:, 0:L], ACT.Copy)
                else:
                    k = n - FIRST["gate"] if kind in ("gate", "ga") else n - FIRST["gb"] + 16
                    if k >= 2:
                        act.wait_ge(gate_ready, k - 1)
                    if kind == "gate":
                        act.activation(gx[:, k % 2, :], ps[:, 0:SEQ], ACT.Copy, scale=0.5)
                    last = act.activation(gs[:, k % 2, :], ps[:, 0:SEQ], ACT.Tanh, scale=0.5)
                last.then_inc(tile_copied, 1)

            def tr_out(key):
                act.wait_ge(tr_ready, TR_NO[key] + 1)
                kind, i = key
                ps = bank[4][:, :].rearrange("p (k e) -> p k e", e=P)
                if kind == "v":
                    act.activation(v_meta[0:META, i, :], ps[0:META, 0, :], ACT.Copy)
                    last = act.activation(v_tok[:, :, i, :], ps[:, 1:3, :], ACT.Copy)
                elif kind == "dv":
                    last = act.activation(dv_tok[:, :, i, :], ps[:, 1:3, :], ACT.Copy)
                else:
                    h, t = divmod(i, TT)
                    if i >= 2:
                        act.wait_ge(o_ready, i - 1)
                    act.activation(wT[0:META, i % 2, 0, :], ps[0:META, 0, :], ACT.Copy)
                    last = act.activation(wT[:, i % 2, 1:2 + t, :], ps[:, 1:2 + t, :], ACT.Copy)
                last.then_inc(tr_copied, 1)

            act.dma_start(w_ba, w_in_v[:, :, BA_COL:BA_COL + 16]).then_inc(wba_in, 16)
            for q in range(AHEAD):
                split_high(q)
            for t in range(3):
                act.wait_ge(uT_ready, t + 1)
                act.activation(uT_hi[:, :, TOKENS[t]], uT[:, :, TOKENS[t]], ACT.Copy).then_inc(u_hi, 1)
            for n in range(FIRST["dq"]):
                for q in splits_at(n):
                    split_high(q)
                tile_out(n)
                if FIRST["av"] + 1 <= n <= FIRST["aq"]:
                    tr_out(("v", n - 1 - FIRST["av"]))
                if n == 2:
                    act.wait_ge(lam_dot, 1)
                    act.activation(lam[:, 2:4], lam[:, 0:2], ACT.Exp).then_inc(lam_exp, 1)
                if n == 8:
                    decay_logs()
                if n == FIRST["aq"] + 4:
                    decay_exps()

            def att_exp(i):
                h, t = divmod(i, TT)
                nk = META + (t + 1) * P
                act.wait_ge(nmax_ready, i + 1)
                for m in range(2):
                    last = act.activation(prob[:, i % 2, m, 0:nk], prob[:, i % 2, m, 0:nk], ACT.Exp, scale=SCALE,
                                          bias=nmax[:, i % 2, m:m + 1], accum_out=rsum[:, i % 2, m:m + 1])
                last.then_inc(exp_ready, 1)

            def att_sq(h):
                act.wait_ge(o_ready, 2 * h + 2)
                act.wait_ge(o_copied, h + 1)
                if h:
                    act.wait_ge(oss_ready, h)
                act.activation(osq, bank[5 + h % 2][:, 0:SEQ], ACT.Square).then_inc(osq_ready, 1)

            def conv_sig(c):
                act.wait_ge(conv_ready, c + 1)
                if c >= 2:
                    act.wait_ge(silu_ready, c - 1)
                act.activation(sg[:, c % 2, :], acc[:, c % NACC, :], ACT.Tanh).then_inc(csig, 1)

            def conv_sq(c):
                act.wait_ge(silu_ready, c + 1)
                if c >= 2:
                    act.wait_ge(css_ready, c - 1)
                act.activation(csq[:, c % 2, :], (dqT if c < H else dkT)[:, c % H, :], ACT.Square).then_inc(csq_ready, 1)

            def roots():
                act.preload_act_table_set("natural_log_exp_and_others")
                act.wait_ge(css_ready, 16)
                act.wait_ge(oss_ready, H)
                link(act.activation(rs_rows[0:NSS, :], bank[7][0:NSS, 0:L], ACT.Ln, bias=c_mean_eps[0:NSS, :]))
                act.activation(rs_rows[0:NSS, :], rs_rows[0:NSS, :], ACT.Exp, scale=-0.5, bias=c_rs[0:NSS, :]).then_inc(rs_ready, 1)

            for m in range(SLOTS_A):
                tile_out(FIRST["dq"] + m)
                if 1 <= m <= 24:
                    conv_sig(m - 1)
                if 2 <= m < 16 + 2:
                    conv_sq(m - 2)
                if 18 <= m < 26:
                    act.wait_ge(silu_ready, m - 2 + 1)
                    act.activation(dvT_meta[:, m - 18, :], acc[:, (m - 2) % NACC, 0:META], ACT.Copy)
                if 2 <= m < ATT_UNITS + 2:
                    tr_out(("w", m - 2))
                if 18 <= m < 26:
                    tr_out(("dv", m - 18))
                for q in splits_at(FIRST["dq"] + m):
                    split_high(q)
                if m < ATT_UNITS:
                    att_exp(m)
                if 4 <= m < ATT_UNITS + 4 and m % 2 == 0:
                    att_sq((m - 4) // 2)
                if m == 20:
                    roots()

            def dn(t, c, s):
                if not works("act", (t, c, s)):
                    return
                w = work[c]
                X, Y, Z = (bank[2 + 3 * c + i][:, :].rearrange("p (h i) -> p h i", h=4) for i in range(3))
                n = 1 if t == "meta" else 4
                if s == "q" and c == 0:
                    act.preload_act_table_set("natural_log_exp_and_others")
                wait_step(act, "pe", (t, c, s))
                if s == "s0":
                    act.wait_ge(dec_masked[c], {"meta": 1, 0: 2 - c, 1: 3 - c}[t])
                    if t != "meta":
                        act.activation(w[7][:, 0:n, :], X[:, 0:n, :], ACT.Exp)
                    for h in range(n):
                        k = 2 * H if t == "meta" else t * H + 4 * c + h
                        last = act.activation(w[0][:, h, :], w[0][:, h, :], ACT.Exp, bias=ngc[:, k:k + 1])
                elif s == "s2":
                    last = act.activation(w[1][:, 0:n, :], Y[:, 0:n, :], ACT.Copy)
                elif s == "s3":
                    last = act.activation(w[0][:, 0:n, :], X[:, 0:n, :], ACT.Copy)
                elif s == "s4":
                    last = act.activation(w[4][:, 0:n, :], X[:, 0:n, :], ACT.Copy)
                elif s == "s5":
                    last = act.activation(w[2][:, 0:n, :], X[:, 0:n, :], ACT.Copy)
                elif s == "s7":
                    last = act.activation(w[0][:, 0:n, :], X[:, 0:n, :], ACT.Copy)
                elif s in ("x1", "x2", "x3"):
                    last = act.activation(w[5][:, 0:n, :], Z[:, 0:n, :], ACT.Copy)
                elif s == "w" and t != "meta":
                    last = act.activation(w[6][:, 0:n, :], X[:, 0:n, :], ACT.Copy, scale=-1.0)
                elif s == "v":
                    last = act.activation(w[5][:, 0:n, :], Z[:, 0:n, :], ACT.Copy)
                elif s == "m":
                    last = act.activation(S[:, 0:4, :], X, ACT.Copy)
                elif s == "o":
                    last = act.activation(w[6][:, 0:n, :], Y[:, 0:n, :], ACT.Square)
                elif s == "q":
                    link(act.activation(w[7][:, 0:n, :], Z[:, 0:n, :], ACT.Ln, scale=1.0 / P, bias=c_eps))
                    last = act.activation(w[7][:, 0:n, :], w[7][:, 0:n, :], ACT.Exp, scale=-0.5)
                last.then_inc(dn_act[c], 1)

            act.wait_ge(qk_ready, N_DN)
            for what, arg in BEHIND:
                if what == "split":
                    for q in splits_at(arg):
                        split_high(q)
                elif what == "tile":
                    tile_out(arg)
                elif what == "spread":
                    pass
                elif what == "result":
                    wait_step(act, "pool", (TT - 1, arg, "q"))
                    for part in RESULTS[arg]:
                        last = act.activation(yd_hi[part], gateT[part], ACT.Copy)
                    last.then_inc(yd_hi_ready, 1)
                else:
                    dn(*arg)

            for n in range(FIRST["yd"], len(TILES)):
                for q in splits_at(n):
                    split_high(q)
            act.dma_start(norm2_b, row(norm2_w, D)).then_inc(norms_in, 16)
            act.dma_start(fnorm_b, final_norm_w.unsqueeze(0).broadcast_to([P, D])).then_inc(norms_in, 16)
            act.dma_start(r_w[:, :, 0:4], router_group_w[0].rearrange("(c p) n -> p c n", p=P)).then_inc(norms_in, 16)
            act.dma_start(r_w[:, :, 4:36], router_expert_w[0].rearrange("(c p) n -> p c n", p=P)).then_inc(norms_in, 16)
            act.dma_start(r_b[:, 0:4], row(router_group_b, 4)).then_inc(norms_in, 16)
            act.dma_start(r_b[:, 4:36], row(router_expert_b, 32)).then_inc(norms_in, 16)

            def root(into, ready, src, k):
                link(act.activation(into[:, k:k + 1], src[:, k:k + 1], ACT.Ln))
                act.activation(into[:, k:k + 1], into[:, k:k + 1], ACT.Exp, scale=-0.5).then_inc(ready, 1)

            act.preload_act_table_set("natural_log_exp_and_others")
            for i in range(4):
                act.wait_ge(mixed, 16 + 2 * (i + 1))
                for t in range(TT):
                    last = act.activation(junk[:, t * 256:(t + 1) * 256] if i % 2 else junk[:, 512 + t * 256:768 + t * 256],
                                          h_tok[:, t, i * 256:(i + 1) * 256], ACT.Square, accum_out=ssq_part[:, t, i:i + 1])
                if i < 3:
                    link(last)
            last.then_inc(ssq2_ready, 1)
            act.wait_ge(var2_ready, 1)
            link(act.activation(rstd[:, 0:TT], ssq[:, 0:TT], ACT.Ln))
            act.activation(rstd[:, 0:TT], rstd[:, 0:TT], ACT.Exp, scale=-0.5).then_inc(rstd2_ready, 1)
            act.wait_ge(rstd2_ready, 1)
            for t in range(TT):
                act.activation(u2[:, t, :], h_tok[:, t, :], ACT.Copy, scale=rstd[:, t:t + 1]).then_inc(u2_scaled, 1)
            act.wait_ge(r_exp_in, 1)
            act.activation(gd, gd, ACT.Exp).then_inc(r_exp, 1)
            act.wait_ge(r_exp_in, 2)
            act.activation(sc[:, 4, :], sc[:, 4, :], ACT.Exp).then_inc(r_exp, 1)

            act.wait_ge(ov_sum, 1)
            link(act.activation(junk[:, 0:TT * 32], bank[5][:, 0:TT * 32], ACT.Copy, accum_out=ovcnt))
            act.activation(ovi, ovcnt, ACT.Copy).then_inc(ov_flag, 1)
            with act.Fori(0, N_BATCH) as b:
                act.wait_ge(gathered, b * 3 + 2)
                act.activation(xg[:, 0:4, :], bank[6][:, :].rearrange("p (c i) -> p c i", i=P), ACT.Copy).then_inc(xg_a, 1)
                act.wait_ge(slot_used, b * SLOTS + NC)
                act.activation(sil, bank[4][:, 0:D_EXPERT], ACT.Tanh, scale=0.5).then_inc(g_sig, 1)
                act.wait_ge(slot_used, b * SLOTS + NC + 2)
                act.activation(dsb[:, 0:512], bank[6][:, :], ACT.Copy).then_inc(down_a, 1)

            beyond = act.value_load(ovi[0:1, 0:1], min_val=0, max_val=2 * SEQ)
            with act.If(beyond > 0):
                with act.Fori(0, N_EXPERTS) as e:
                    for fc in range(2):
                        act.wait_ge(f_h, e * 2 + fc + 1)
                        act.activation(ftmp, bank[4][:, 0:SEQ], ACT.Tanh, scale=0.5).then_inc(f_sig, 1)
                act.wait_ge(f_sum, N_EXPERTS * 4 + 1)

            act.preload_act_table_set("natural_log_exp_and_others")
            act.wait_ge(combined, N_BATCH)
            for t in range(TT):
                if t:
                    act.wait_ge(ssq3_ready, t)
                for half in range(2):
                    last = act.activation(junk[:, half * 512:(half + 1) * 512], bank[2 * t + half][:, :], ACT.Square,
                                          accum_out=sc[:, 8 + half, t:t + 1])
                last.then_inc(ssq3_ready, 1)
            for t in range(TT):
                act.wait_ge(var3_ready, t + 1)
                root(rstd, rstd3_ready, ssq, t)

        @block.vector
        def _(dve):
            n_step = [0]

            def link(ins):
                n_step[0] += 1
                ins.then_inc(dve_step, 1)
                dve.wait_ge(dve_step, n_step[0])

            def mark(ins):
                n_step[0] += 1
                ins.then_inc(dve_step, 1)

            def follow():
                dve.wait_ge(dve_step, n_step[0])

            tt, ts, stt = dve.tensor_tensor, dve.tensor_scalar, dve.scalar_tensor_tensor

            for t in range(4):
                if t < 3:
                    rows = P if t < TT else META
                    dve.wait_ge(ssq_ready, t + 1)
                    ts(ssq[0:rows, t:t + 1], ssq[0:rows, t:t + 1], 1.0 / D, EPS, ALU.mult, ALU.add).then_inc(var_ready, 1)
                if t:
                    rows = P if t - 1 < TT else META
                    dve.wait_ge(rstd_ready, t)
                    ts(xin[0:rows, t - 1, :], xin[0:rows, t - 1, :], rstd[0:rows, t - 1:t], None, ALU.mult).then_inc(xn_ready, 1)
            dve.wait_ge(vec_T, 1)
            dve.tensor_copy(vec[:, 0:V_CONV], bank[0][:, 0:V_CONV])
            ts(vec[:, V_CONV:N_VEC], bank[0][:, V_CONV:N_VEC], 0.5, None, ALU.mult).then_inc(vec_ready, 1)
            split_low(dve, 0)
            dve.wait_ge(vec_ready, 1)

            def low_of_tokens(t):
                dve.wait_ge(uT_ready, t + 1)
                dve.wait_ge(u_hi, t + 1)
                tt(uT_lo[:, :, TOKENS[t]], uT[:, :, TOKENS[t]], uT_hi[:, :, TOKENS[t]].bitcast(F32), ALU.subtract).then_inc(u_lo, 1)

            for t in range(3):
                dve.wait_ge(xT_ready, t + 1)
                rows = P if t < TT else META
                for k in range(2):
                    ps = bank[2 + 2 * t + k][:, :].rearrange("p (c i) -> p c i", i=P)[:, :, 0:rows]
                    last = tt(uT[:, 4 * k:4 * k + 4, TOKENS[t]], ps,
                              vec[:, V_NORM1 + 4 * k:V_NORM1 + 4 * k + 4].unsqueeze(2).broadcast_to([P, 4, rows]), ALU.mult)
                last.then_inc(uT_ready, 1)
                if t:
                    low_of_tokens(t - 1)
            low_of_tokens(2)
            for q in range(1, AHEAD):
                split_low(dve, q)

            own = slice(2 * H, NCOL)
            minus_lambda = lam[:, 5:6]

            def lambda_dots():
                dve.wait_ge(small_in, 16 * 8)
                dve.wait_ge(const_ready, 1)
                for v in (dtb, eA):
                    link(dve.tensor_tensor_reduce(tmp17[:, 0:H], v[:, 0:H], own_head, 1.0, 0.0, ALU.mult, ALU.add, v[:, own]))
                dve.tensor_tensor_reduce(lam_in[:, 0, :], lam_in[:, 0, :], lam_in[:, 1, :], 1.0, 0.0, ALU.mult, ALU.add, lam[:, 0:1])
                dve.tensor_tensor_reduce(lam_in[:, 2, :], lam_in[:, 2, :], lam_in[:, 3, :], 1.0, 0.0, ALU.mult, ALU.add, lam[:, 1:2]).then_inc(lam_dot, 1)

            def logits_out():
                dve.wait_ge(ba_ready, 1)
                dve.tensor_copy(ba_meta[0:META, :], bank[2][0:META, 32:48]).then_inc(ba_meta_ready, 1)
                ba = bank[2][:, 0:32].rearrange("p (t k) -> p t k", t=TT)
                dve.tensor_copy(blog[:, 0:16].rearrange("p (t h) -> p t h", t=TT), ba[:, :, 0:H])
                dve.tensor_copy(alog[:, 0:16].rearrange("p (t h) -> p t h", t=TT), ba[:, :, H:16])

            def logits_of_meta():
                dve.wait_ge(ba_spread, 1)
                link(dve.tensor_tensor_reduce(tmp17[:, 0:H], bank[3][:, 0:H], own_head, 1.0, 0.0, ALU.mult, ALU.add, blog[:, own]))
                link(dve.tensor_tensor_reduce(tmp17[:, 0:H], bank[3][:, H:16], own_head, 1.0, 0.0, ALU.mult, ALU.add, alog[:, own]))
                link(tt(alog, alog, dtb, ALU.add))
                stt(tmp17, alog, -1.0, alog, ALU.mult, ALU.max).then_inc(ba_logits, 1)
                dve.wait_ge(lam_exp, 1)
                link(stt(lam[:, 4:5], lam[:, 2:3], -1.0, lam[:, 3:4], ALU.mult, ALU.add))
                link(ts(lam[:, 5:6], lam[:, 4:5], -LAMBDA_INIT, None, ALU.add))

            def decays():
                dve.wait_ge(g_exp, 1)
                link(ts(beta, beta, 1.0, None, ALU.add))
                link(dve.reciprocal(beta, beta))
                ts(nbeta, beta, -1.0, None, ALU.mult)
                link(stt(sp, alog, 0.0, sp, ALU.max, ALU.add))
                stt(g, sp, -1.0, eA, ALU.mult, ALU.mult).then_inc(g_ready, 1)

            def decay_sums():
                dve.wait_ge(gc_ready, 1)
                dve.tensor_copy(gc2.rearrange("p a b -> p (a b)"), bank[5][:, 0:2 * NCOL]).then_inc(gc_copied, 1)
                dve.wait_ge(gc_copied, 1)
                ts(ngc, gc2[:, 0, :], -1.0, None, ALU.mult)
                tt(kdec, gc2[:, 1, :], gc2[:, 0, :], ALU.subtract).then_inc(gc_copied, 1)

            def decay_products():
                dve.wait_ge(gate_cols, 1)
                tt(begc, beta, egc, ALU.mult).then_inc(gate_cols, 1)

            def split_lows(n):
                for q in splits_at(n):
                    if not low_by_pool(q):
                        split_low(dve, q)

            for n in range(FIRST["dq"]):
                split_lows(n)
                if n == 1:
                    lambda_dots()
                if n == 2:
                    logits_out()
                if n == 4:
                    logits_of_meta()
                if n == 9:
                    decays()
                if n == FIRST["aq"] + 2:
                    decay_sums()
                if n == FIRST["aq"] + 6:
                    decay_products()

            def conv(c):
                wait_tile_out(dve, FIRST["dq"] + c)
                if c >= NACC + 16:
                    dve.wait_ge(tr_copied, TR_NO[("dv", c - NACC - 16)] + 1)
                elif c >= NACC:
                    dve.wait_ge(silu_ready, c - NACC + 1)
                a, x_ = acc[:, c % NACC, :], cbuf[:, c % 2, :]
                tap = lambda k: vec[:, V_CONV + k * 3 * H + c:V_CONV + k * 3 * H + c + 1]
                link(ts(a, x_[:, 0:L], tap(0), None, ALU.mult))
                for k in range(1, CONV):
                    last = stt(a, x_[:, k:k + L], tap(k), a, ALU.mult, ALU.add)
                    if k < CONV - 1:
                        link(last)
                last.then_inc(conv_ready, 1)

            def silu(c):
                dve.wait_ge(csig, c + 1)
                s_ = sg[:, c % 2, :]
                a = acc[:, c % NACC, :]
                if c == 0:
                    dve.wait_ge(xT_ready, 3)
                dst = dqT[:, c, :] if c < H else dkT[:, c - H, :] if c < 2 * H else a
                stt(dst, s_, 1.0, a, ALU.add, ALU.mult).then_inc(silu_ready, 1)

            def scale_by(i):
                k = SPREAD.index(i)
                dve.wait_ge(spread_ready, k + 1)
                ps = spread_bank(k)
                h = i % H
                if i >= 2 * H:
                    last = stt(yaT[:, h, :], yaT[:, h, :], vec[:, V_SUBLN:V_SUBLN + 1], ps[:, 0:SEQ], ALU.mult, ALU.mult)
                else:
                    dst = (dqT if i < H else dkT)[:, h, :]
                    if i >= H:
                        tt(dkT_meta[:, h, :], dst[:, 0:META], ps[:, 0:META], ALU.mult)
                    last = tt(dst[:, META:L], dst[:, META:L], ps[:, META:L], ALU.mult)
                last.then_inc(qk_ready, 1)

            def att_bias(i):
                h, t = divmod(i, TT)
                nk = META + (t + 1) * P
                dve.wait_ge(scores_ready, i + 1)
                dve.wait_ge(qz_ready, i + 1)
                if i >= 2:
                    dve.wait_ge(tr_ready, TR_NO[("w", i - 2)] + 1)
                for m in range(2):
                    last = dve.tensor_tensor_reduce(prob[:, i % 2, m, 0:nk], bank[2 + m][:, 0:nk], bias[:, i % NPREP, 0:nk], 1.0, -3e38,
                                                    ALU.add, ALU.max, mx[:, i % 2, m:m + 1])
                last.then_inc(biased, 1)
                dve.wait_ge(biased, i + 1)
                ts(nmax[:, i % 2, :], mx[:, i % 2, :], -SCALE, None, ALU.mult).then_inc(nmax_ready, 1)

            def att_w(i):
                h, t = divmod(i, TT)
                nk = META + (t + 1) * P
                dve.wait_ge(exp_ready, i + 1)
                r = rinv[:, i % 2, :]
                link(dve.reciprocal(r, rsum[:, i % 2, :]))
                link(ts(r[:, 1:2], r[:, 1:2], minus_lambda, None, ALU.mult))
                a, b = prob[:, i % 2, 0, 0:nk], prob[:, i % 2, 1, 0:nk]
                link(ts(b, b, r[:, 1:2], None, ALU.mult))
                stt(a, a, r[:, 0:1], b, ALU.mult, ALU.add).then_inc(w_ready, 1)

            def tile_out(n):
                kind, j = TILES[n]
                ps = bank[n % 2][:, 0:SEQ]
                if kind in ("gate", "ga", "gb"):
                    k = n - FIRST["gate"] if kind in ("gate", "ga") else n - FIRST["gb"] + 16
                    wait_tile_out(dve, n)
                    s_ = gs[:, k % 2, :]
                    if kind == "gate":
                        last = stt(gateT[:, j, :], s_, 1.0, gx[:, k % 2, :], ALU.add, ALU.mult)
                    else:
                        last = ts({"ga": gaT, "gb": gbT}[kind][:, j, :], s_, 1.0, 0.5, ALU.add, ALU.mult)
                    last.then_inc(gate_ready, 1)
                    return
                dve.wait_ge(tile_ready, n + 1)
                if kind == "ya":
                    last = tt(gaT[:, j, :], ps, gaT[:, j, :], ALU.mult)
                elif kind == "yd":
                    link(tt(gbT[:, j, :], ps, gbT[:, j, :], ALU.mult))
                    last = tt(mixT[:, j, :], gaT[:, j, :], gbT[:, j, :], ALU.add)
                else:
                    if j == 0:
                        dve.wait_ge(h_in, 16 * TT)
                    piece = h_tok[:, j % 2, (j // 2) * 256:(j // 2 + 1) * 256]
                    last = tt(piece, ps, piece, ALU.add)
                last.then_inc(mixed, 1)

            def att_keep(h):
                dve.wait_ge(o_ready, 2 * h + 2)
                dve.tensor_copy(yaT[:, h, :], bank[5 + h % 2][:, 0:SEQ]).then_inc(o_copied, 1)

            for m in range(SLOTS_A):
                if 1 <= m < ATT_UNITS + 1:
                    att_w(m - 1)
                if m < ATT_UNITS:
                    att_bias(m)
                if m < 24:
                    conv(m)
                if 1 <= m <= 24:
                    silu(m - 1)
                if m < 22:
                    split_lows(FIRST["dq"] + m)
                if 4 <= m < ATT_UNITS + 4 and m % 2 == 0:
                    att_keep((m - 4) // 2)
                for i in spread_at(m):
                    scale_by(i)
                if m >= 24:
                    tile_out(FIRST["dq"] + m)
                if m >= 22:
                    split_lows(FIRST["dq"] + m)

            def dn(t, c, s):
                if not works("dve", (t, c, s)):
                    return
                w = work[c]
                X, Y, Z = (bank[2 + 3 * c + i][:, :].rearrange("p (h i) -> p h i", h=4)[:, 0:1 if t == "meta" else 4, :] for i in range(3))
                n = 1 if t == "meta" else 4
                k0 = 2 * H if t == "meta" else t * H + 4 * c
                hs = slice(4 * c, 4 * c + 4)
                per_head = lambda v: v[:, k0:k0 + n].unsqueeze(2).broadcast_to([P, n, P])
                if s == "s2":
                    wait_step(dve, "dve", (t, c, "s1"))
                else:
                    wait_step(dve, "pe", (t, c, s))
                b = lambda i: w[i][:, 0:n, :]
                each_head = lambda m: m.unsqueeze(1).broadcast_to([P, n, P])
                if s == "s0":
                    mask = causal_add16 if t == "meta" else causal_add
                    tt(b(0), X, mask.unsqueeze(1).broadcast_to([P, n, P]), ALU.add).then_inc(dec_masked[c], 1)
                    wait_step(dve, "act", (t, c, s))
                    link(tt(b(1), Y, b(0), ALU.mult))
                    last = tt(b(1), b(1), each_head(strict), ALU.mult)
                elif s == "s1":
                    last = tt(b(2), X, per_head(nbeta), ALU.mult)
                    if t != "meta":
                        last = tt(b(3), Z, b(0), ALU.mult)
                elif s == "s2":
                    link(tt(b(4), b(2), each_head(block16), ALU.mult))
                    last = tt(b(6), b(4), each_head(ident), ALU.add)
                elif s == "s3":
                    last = dve.tensor_copy(b(2), Z)
                elif s == "s4":
                    dve.tensor_copy(b(5), Z)
                    last = tt(b(6), Y, b(6), ALU.add)
                elif s == "s5":
                    last = tt(b(6), Y, b(6), ALU.add)
                elif s == "s6":
                    last = tt(b(6), Z, b(6), ALU.add)
                elif s == "s7":
                    last = tt(b(7), Y, per_head(kdec), ALU.mult)
                    if t == "meta":
                        last = tt(b(3), Z, per_head(beta), ALU.mult)
                    else:
                        last = tt(b(2), Y, per_head(begc), ALU.mult)
                elif s in ("t1", "t2", "t3"):
                    last = tt(b(0), X, b(0), ALU.add)
                    if s != "t3":
                        last = tt(b(6), Z, b(6), ALU.add)
                    else:
                        last = tt(b(4), dv_tok[:, t, hs, :], per_head(beta), ALU.mult)
                elif s == "w":
                    last = tt(um, Z[:, 0, :].unsqueeze(1).broadcast_to([P, H, P]),
                              own_head.unsqueeze(2).broadcast_to([P, H, P]), ALU.mult)
                elif s == "m":
                    last = dve.tensor_copy(S[:, 4:8, :], bank[3][:, :].rearrange("p (h i) -> p h i", h=4))
                elif s == "o":
                    for h in range(n):
                        last = stt(S[:, 4 * c + h, :], S[:, 4 * c + h, :], egt[:, k0 + h:k0 + h + 1], X[:, h, :], ALU.mult, ALU.add)
                elif s == "q":
                    wait_step(dve, "act", (t, c, s))
                    flat = lambda a: a.rearrange("p h i -> p (h i)")
                    last = stt(flat(b(7)), flat(Y), vec[:, V_DNW:V_DNW + 1], flat(b(7)), ALU.mult, ALU.mult)
                last.then_inc(dn_dve[c], 1)

            dve.wait_ge(tr_copied, len(TR))
            for what, arg in BEHIND:
                if what == "split":
                    split_lows(arg)
                elif what == "tile":
                    tile_out(arg)
                elif what == "spread":
                    scale_by(SPREAD[arg])
                elif what == "result":
                    wait_step(dve, "pool", (TT - 1, arg, "q"))
                    dve.wait_ge(yd_hi_ready, arg + 1)
                    for part in RESULTS[arg]:
                        last = tt(yd_lo[part], gateT[part], yd_hi[part].bitcast(F32), ALU.subtract)
                    last.then_inc(yd_lo_ready, 1)
                else:
                    dn(*arg)
            def piece_out(i):
                dve.wait_ge(hT_ps, i + 1)
                tt(u2T[:, 2 * i:2 * i + 2, :], bank[4 + i % 2][:, :].rearrange("p (c i) -> p c i", c=2),
                   vec[:, V_NORM2 + 2 * i:V_NORM2 + 2 * i + 2].unsqueeze(2).broadcast_to([P, 2, SEQ]), ALU.mult).then_inc(hT_ready, 1)

            for n in range(FIRST["yd"], len(TILES)):
                split_lows(n)
                tile_out(n)
                j = n - FIRST["out"]
                if j >= 2 and j % 2 == 0:
                    piece_out(j // 2 - 1)
            piece_out(3)

            dve.wait_ge(ssq2_ready, 1)
            link(dve.tensor_reduce(ssq[:, 0:TT], ssq_part, AX, ALU.add))
            ts(ssq[:, 0:TT], ssq[:, 0:TT], 1.0 / D, EPS, ALU.mult, ALU.add).then_inc(var2_ready, 1)
            dve.wait_ge(lgT_ps, 1)
            dve.tensor_copy(lgT[0:36, :], bank[6][0:36, 0:SEQ]).then_inc(lgT_ready, 1)
            dve.wait_ge(rstd2_ready, 1)
            dve.wait_ge(norms_in, 16 * 6)
            dve.wait_ge(logits_ready, 1)
            wide = lambda v, n: v.unsqueeze(2).broadcast_to([P, TT, n])
            sc_ = lambda i: sc[:, i, :]
            for t in range(TT):
                mark(stt(lg[:, t, :], bank[6][:, 256 + 64 * t:256 + 64 * t + 36], rstd[:, t:t + 1], r_b, ALU.mult, ALU.add))
            follow()
            link(dve.tensor_reduce(sc_(0), lg[:, :, 0:4], AX, ALU.max))
            mark(tt(gd, lg[:, :, 0:4], wide(sc_(0), 4), ALU.subtract))

            def first(into, equal, n):
                keep, count = (keep4, pen_cum) if n == 4 else (keep32, cum)
                flat = lambda a: a.rearrange("p t k -> p (t k)")
                link(dve.tensor_tensor_scan(flat(count), flat(keep), flat(equal), 0.0, ALU.mult, ALU.add))
                link(stt(into, count, 1.0, equal, ALU.is_equal, ALU.mult))

            link(tt(pen, lg[:, :, 0:4], wide(sc_(0), 4), ALU.is_equal))
            first(gsel, pen, 4)
            link(ts(pen, gsel, -1.0, -NEG, ALU.add, ALU.mult))
            for t in range(TT):
                last = tt(me[:, t, :].rearrange("p (g e) -> p g e", g=4), lg[:, t, 4:36].rearrange("p (g e) -> p g e", g=4),
                          pen[:, t, :].unsqueeze(2).broadcast_to([P, 4, PER_GROUP]), ALU.add)
            last.then_inc(r_exp_in, 1)
            dve.wait_ge(r_exp_in, 1)
            link(dve.tensor_reduce(sc_(1), me, AX, ALU.max))
            link(tt(eq, me, wide(sc_(1), 32), ALU.is_equal))
            first(e1, eq, 32)
            link(stt(me2, e1, 2 * NEG, me, ALU.mult, ALU.add))
            link(dve.tensor_reduce(sc_(2), me2, AX, ALU.max))
            link(tt(eq, me2, wide(sc_(2), 32), ALU.is_equal))
            first(e2, eq, 32)
            tt(asg, e1, e2, ALU.add).then_inc(assigned, 1)
            tt(sc_(4), sc_(2), sc_(1), ALU.subtract).then_inc(r_exp_in, 1)
            dve.wait_ge(r_exp, 1)
            link(dve.tensor_reduce(sc_(5), gd, AX, ALU.add))
            link(dve.reciprocal(sc_(5), sc_(5)))
            dve.wait_ge(r_exp, 2)
            link(ts(sc_(6), sc_(4), 1.0, None, ALU.add))
            link(dve.reciprocal(sc_(6), sc_(6)))
            link(tt(sc_(6), sc_(6), sc_(5), ALU.mult))
            link(tt(sc_(7), sc_(6), sc_(4), ALU.mult))
            link(tt(e1, e1, wide(sc_(6), 32), ALU.mult))
            link(tt(e2, e2, wide(sc_(7), 32), ALU.mult))
            link(tt(comb, e1, e2, ALU.add))
            dve.wait_ge(ranked, 1)
            link(ts(rank, bank[7][:, 0:64].rearrange("p (t k) -> p t k", t=TT), 1.0, None, ALU.add))
            link(tt(rank, rank, asg, ALU.mult))
            ts(rank, rank, -1.0, None, ALU.add).then_inc(rank_ready, 1)
            dve.wait_ge(rank_ready, 1)

            with dve.Fori(0, N_BATCH) as b:
                dve.wait_ge(gathered, b * 3 + 1)
                for t in range(TT):
                    last = tt(pick[:, t], slot_no.unsqueeze(1).broadcast_to([P, EPB, CAP]),
                              rank[:, t, bass.ds(b * EPB, EPB)].unsqueeze(2).broadcast_to([P, EPB, CAP]), ALU.is_equal)
                last.then_inc(pick_made, 1)
                dve.wait_ge(pick_made, b + 1)
                for t in range(TT):
                    last = tt(pickw[:, t], pick[:, t],
                              comb[:, t, bass.ds(b * EPB, EPB)].unsqueeze(2).broadcast_to([P, EPB, CAP]), ALU.mult)
                last.then_inc(picked, 1)
                dve.wait_ge(gathered, b * 3 + 3)
                dve.tensor_copy(xg[:, 4:8, :], bank[7][:, :].rearrange("p (c i) -> p c i", i=P)).then_inc(xg_d, 1)
                dve.wait_ge(gathered, b * 3 + 4)
                dve.tensor_copy(pickT, bank[5][:, 0:2 * P].rearrange("p (t i) -> p t i", t=TT))
                dve.wait_ge(g_sig, b + 1)
                stt(sil, sil, 1.0, bank[4][:, 0:D_EXPERT], ALU.add, ALU.mult).then_inc(hid_step, 1)
                dve.wait_ge(hid_step, b + 1)
                stt(hid, sil, 0.5, bank[4][:, D_EXPERT:2 * D_EXPERT], ALU.mult, ALU.mult).then_inc(hid_ready, 1)
                dve.wait_ge(hidT_ps, b + 1)
                dve.tensor_copy(hidT, bank[5][:, 2 * P:4 * P].rearrange("p (t i) -> p t i", t=2)).then_inc(hidT_ready, 1)
                dve.wait_ge(slot_used, b * SLOTS + SLOTS)
                dve.tensor_copy(dsb[:, 512:D], bank[7][:, :]).then_inc(down_d, 1)

            beyond = dve.value_load(ovi[0:1, 0:1], min_val=0, max_val=2 * SEQ)
            with dve.If(beyond > 0):
                dve.wait_ge(ovf_ready, 1)
                dve.wait_ge(f_u2T_ps, 1)
                for t in range(TT):
                    for k in range(2):
                        last = dve.tensor_copy(u2T[:, 4 * k:4 * k + 4, t * P:(t + 1) * P],
                                               bank[4 + 2 * t + k][:, :].rearrange("p (c i) -> p c i", i=P))
                last.then_inc(f_u2T, 1)
                with dve.Fori(0, N_EXPERTS) as e:
                    for fc in range(2):
                        dve.wait_ge(f_sig, e * 2 + fc + 1)
                        stt(ftmp, ftmp, 1.0, bank[4][:, 0:SEQ], ALU.add, ALU.mult).then_inc(f_step, 1)
                        dve.wait_ge(f_step, e * 2 + fc + 1)
                        stt(fhT[:, fc, :], ftmp, 0.5, bank[4][:, SEQ:2 * SEQ], ALU.mult, ALU.mult).then_inc(f_hT, 1)
                    for t in range(TT):
                        for half in range(2):
                            k = 2 * t + half
                            dve.wait_ge(f_y, e * 4 + k + 2)
                            dve.wait_ge(f_sum, e * 4 + k + 1)
                            dve.tensor_scalar(dsb[:, 0:512], bank[5][:, :], ovf[:, t, bass.ds(e, 1)], None, ALU.mult).then_inc(f_acc, 1)
                dve.wait_ge(f_sum, N_EXPERTS * 4 + 1)

            for t in range(TT):
                dve.wait_ge(ssq3_ready, t + 1)
                link(tt(ssq[:, t:t + 1], sc[:, 8, t:t + 1], sc[:, 9, t:t + 1], ALU.add))
                ts(ssq[:, t:t + 1], ssq[:, t:t + 1], 1.0 / D, EPS, ALU.mult, ALU.add).then_inc(var3_ready, 1)
            for t in range(TT):
                dve.wait_ge(rstd3_ready, t + 1)
                for half in range(2):
                    cols = slice(half * 512, (half + 1) * 512)
                    last = stt(result[:, t, cols], bank[2 * t + half][:, :], rstd[:, t:t + 1], fnorm_b[:, cols], ALU.mult, ALU.mult)
                last.then_inc(out_ready, 1)


_INS = ['x', 'meta_tokens', 'norm1_w', 'w_in', 'lambda_q1', 'lambda_k1', 'lambda_q2', 'lambda_k2', 'da_subln_w',
        'dn_conv_w', 'dn_A_log', 'dn_dt_bias', 'dn_norm_w', 'w_branch_attn', 'w_branch_dn', 'w_out', 'norm2_w',
        'router_group_w', 'router_group_b', 'router_expert_w', 'router_expert_b', 'expert_w_gate', 'expert_w_up',
        'expert_w_down', 'final_norm_w']
_OUTS = [((1, SEQ, D), 'float32')]


def kernel(**inputs):
    import numpy as _np
    import concourse.bacc as _bacc
    from concourse import mybir as _mybir
    from concourse.bass_utils import run_bass_kernel_spmd as _run

    nc = _bacc.Bacc("TRN2", target_bir_lowering=False, num_devices=1)
    arrays, args = {}, []
    for name in _INS:
        a = _np.ascontiguousarray(inputs[name])
        arrays[f"in_{name}_dram"] = a
        args.append(nc.dram_tensor(f"in_{name}_dram", a.shape, _mybir.dt.from_np(a.dtype), kind="ExternalInput").ap())
    for i, (shape, dtype) in enumerate(_OUTS):
        dt = _mybir.dt.from_np(_np.dtype(dtype))
        args.append(nc.dram_tensor(f"out_{i}_dram", shape, dt, kind="ExternalOutput").ap())
    hybrid_block(nc, *args)
    r = _run(nc, [arrays], core_ids=[0])
    got = tuple(r.results[0][f"out_{i}_dram"] for i in range(len(_OUTS)))
    return got[0]
```
